# Optimizing a Trainium2 kernel written in Bass

```python
import jax, jax.numpy as jnp
from jax import lax
import numpy as np

D_MODEL = 1024
BATCH = 1
SEQ = 256
DEPTH = 1

GRID_W = 64
CTX_LEN = 256
MLA_HEADS = 8
MLA_NOPE = 64
MLA_ROPE = 32
MLA_QK = MLA_NOPE + MLA_ROPE
MLA_V = 64
Q_LORA = 384
KV_LORA = 256
NA_HEADS = 8
NA_DIM = 64
NA_WIN_H = 8
NA_WIN_W = 16
MIX_WIDTH = MLA_HEADS * MLA_V + NA_HEADS * NA_DIM
Q_COLS = Q_LORA + NA_HEADS * NA_DIM
KV_COLS = KV_LORA + MLA_ROPE + 2 * NA_HEADS * NA_DIM
N_GROUPS = 4
EXPERTS_PER_GROUP = 4
N_EXPERTS = N_GROUPS * EXPERTS_PER_GROUP
TOP_K_IN_GROUP = 2
D_EXPERT = 512
Q_BLOCK = 128
ROPE_THETA = 10000.0
NORM_EPS = 1e-6
MASK_VALUE = -1e30


def rmsnorm(x, g):
    xf = x.astype(jnp.float32)
    y = xf * lax.rsqrt(jnp.mean(xf * xf, axis=-1, keepdims=True) + NORM_EPS)
    return (y * g.astype(jnp.float32)).astype(x.dtype)

def adaln(cond, w_mod, b_mod):
    return jnp.split(jax.nn.silu(cond) @ w_mod + b_mod, 6, axis=-1)

def modulate(h, shift, scale):
    return h * (1 + scale) + shift

def axial_rope_tables(row, col, dtype):
    half = MLA_ROPE // 2
    inv_freq = ROPE_THETA ** (-jnp.arange(0, half, 2, dtype=jnp.float32) / half)
    ang = jnp.concatenate([row.astype(jnp.float32)[:, None] * inv_freq,
                           col.astype(jnp.float32)[:, None] * inv_freq], axis=-1)
    return jnp.cos(ang).astype(dtype), jnp.sin(ang).astype(dtype)

def apply_rope(x, cos, sin):
    x1, x2 = jnp.split(x, 2, axis=-1)
    c, s = cos[:, None, :], sin[:, None, :]
    return jnp.concatenate([x1 * c - x2 * s, x1 * s + x2 * c], axis=-1)

def mixer_queries(pq, q_a_g, w_uq):
    B, L, _ = pq.shape
    q_lat, na_q = jnp.split(pq, [Q_LORA], axis=-1)
    q_mla = (rmsnorm(q_lat, q_a_g) @ w_uq).reshape(B, L, MLA_HEADS, MLA_QK)
    return q_mla, na_q.reshape(B, L, NA_HEADS, NA_DIM)

def mixer_keys_values(pkv, kv_a_g, w_ukv):
    B, L, _ = pkv.shape
    kv_lat, k_rope, na_k, na_v = jnp.split(
        pkv, [KV_LORA, KV_LORA + MLA_ROPE, KV_LORA + MLA_ROPE + NA_HEADS * NA_DIM], axis=-1)
    kv = (rmsnorm(kv_lat, kv_a_g) @ w_ukv).reshape(B, L, MLA_HEADS, MLA_NOPE + MLA_V)
    k_nope, v_mla = jnp.split(kv, [MLA_NOPE], axis=-1)
    return (k_nope, k_rope, v_mla,
            na_k.reshape(B, L, NA_HEADS, NA_DIM), na_v.reshape(B, L, NA_HEADS, NA_DIM))

def mla_keys(k_nope, k_rope_b):
    return jnp.concatenate([k_nope, jnp.broadcast_to(k_rope_b, k_nope.shape[:3] + (MLA_ROPE,))], axis=-1)

def dense_attention(q, k, v):
    s = jnp.einsum('bqhd,bkhd->bhqk', q, k).astype(jnp.float32) * (q.shape[-1] ** -0.5)
    p = jax.nn.softmax(s, axis=-1).astype(v.dtype)
    return jnp.einsum('bhqk,bkhd->bqhd', p, v)

def mla_latent_attention(q, k, v, k_ctx, v_ctx):
    B, N, H, Dq = q.shape
    k_all = jnp.concatenate([k_ctx, k], axis=1)
    v_all = jnp.concatenate([v_ctx, v], axis=1)
    q_blocks = jnp.moveaxis(q.reshape(B, N // Q_BLOCK, Q_BLOCK, H, Dq), 1, 0)
    out = lax.map(lambda qb: dense_attention(qb, k_all, v_all), q_blocks)
    return jnp.moveaxis(out, 0, 1).reshape(B, N, H, v.shape[-1])

def neighbourhood_attention(q, k, v, k_ctx, v_ctx, rel_bias):
    B, N, H, Dh = q.shape
    rows = N // GRID_W
    kh = min(NA_WIN_H, rows)
    kw = NA_WIN_W
    scale = Dh ** -0.5
    qg = jnp.moveaxis(q.reshape(B, rows, GRID_W, H, Dh), 1, 0)
    kg = k.reshape(B, rows, GRID_W, H, Dh)
    vg = v.reshape(B, rows, GRID_W, H, Dh)
    col = jnp.arange(GRID_W)
    col_start = jnp.clip(col - kw // 2, 0, GRID_W - kw)
    col_in = (col[None, :] >= col_start[:, None]) & (col[None, :] < col_start[:, None] + kw)
    bias_cols = rel_bias[:, :, col[None, :] - col[:, None] + (NA_WIN_W - 1)]

    def one_row(args):
        r, qr = args
        start = jnp.clip(r - kh // 2, 0, rows - kh)
        kr = lax.dynamic_slice_in_dim(kg, start, kh, axis=1)
        vr = lax.dynamic_slice_in_dim(vg, start, kh, axis=1)
        bias = bias_cols[:, start + jnp.arange(kh) - r + (NA_WIN_H - 1)]
        s = jnp.einsum('bqhd,bjkhd->bhqjk', qr, kr).astype(jnp.float32) * scale
        s = s + jnp.transpose(bias, (0, 2, 1, 3)).astype(jnp.float32)[None]
        s = jnp.where(col_in[None, None, :, None, :], s, MASK_VALUE).reshape(B, H, GRID_W, kh * GRID_W)
        s_ctx = jnp.einsum('bqhd,bchd->bhqc', qr, k_ctx).astype(jnp.float32) * scale
        p = jax.nn.softmax(jnp.concatenate([s, s_ctx], axis=-1), axis=-1).astype(v.dtype)
        p_win = p[..., :kh * GRID_W].reshape(B, H, GRID_W, kh, GRID_W)
        p_ctx = p[..., kh * GRID_W:]
        return (jnp.einsum('bhqjk,bjkhd->bqhd', p_win, vr)
                + jnp.einsum('bhqc,bchd->bqhd', p_ctx, v_ctx))

    out = lax.map(one_row, (jnp.arange(rows), qg))
    return jnp.moveaxis(out, 0, 1).reshape(B, N, H, Dh)

def hierarchical_moe(h, w_rg, b_rg, w_re, b_re, w_gate, w_up, w_down):
    B, L, D = h.shape
    t = h.reshape(B * L, D)
    T = t.shape[0]
    g_logits = (t @ w_rg + b_rg).astype(jnp.float32)
    g_prob = jax.nn.softmax(g_logits, axis=-1)
    g_sel = jnp.argmax(g_logits, axis=-1)
    g_w = jnp.take_along_axis(g_prob, g_sel[:, None], axis=-1)
    e_logits = (t @ w_re + b_re).astype(jnp.float32).reshape(T, N_GROUPS, EXPERTS_PER_GROUP)
    e_logits = jnp.take_along_axis(e_logits, g_sel[:, None, None], axis=1)[:, 0]
    top_p, top_i = lax.top_k(jax.nn.softmax(e_logits, axis=-1), TOP_K_IN_GROUP)
    top_p = top_p / jnp.sum(top_p, axis=-1, keepdims=True)
    within = jnp.sum(jax.nn.one_hot(top_i, EXPERTS_PER_GROUP, dtype=jnp.float32) * top_p[..., None], axis=1)
    combine = (jax.nn.one_hot(g_sel, N_GROUPS, dtype=jnp.float32)[:, :, None]
               * (g_w * within)[:, None, :]).astype(h.dtype)
    wg = w_gate.reshape(N_GROUPS, EXPERTS_PER_GROUP, D, D_EXPERT)
    wu = w_up.reshape(N_GROUPS, EXPERTS_PER_GROUP, D, D_EXPERT)
    wd = w_down.reshape(N_GROUPS, EXPERTS_PER_GROUP, D_EXPERT, D)

    def one_group(args):
        wg_g, wu_g, wd_g, comb_g = args
        hid = jax.nn.silu(jnp.einsum('td,edf->tef', t, wg_g)) * jnp.einsum('td,edf->tef', t, wu_g)
        return jnp.einsum('tef,efd->td', hid * comb_g[:, :, None], wd_g)

    y = jnp.sum(lax.map(one_group, (wg, wu, wd, jnp.moveaxis(combine, 1, 0))), axis=0)
    return y.reshape(B, L, D)

def first_inputs(seed: int = 0) -> dict:
    key = jax.random.key(seed)
    ks = jax.random.split(key, 24)
    D = D_MODEL

    def nrm(k, shape, scale):
        return jax.random.normal(k, shape, jnp.float32) * scale

    return {
        'x': nrm(ks[0], (BATCH, SEQ, D), 1.0),
        'c': nrm(ks[1], (BATCH, D), 1.0),
        'ctx': nrm(ks[2], (BATCH, CTX_LEN, D), 1.0),
        'c_ctx': nrm(ks[3], (D,), 1.0),
        'w_mod': nrm(ks[4], (DEPTH, D, 6 * D), 0.5 * D ** -0.5),
        'b_mod': nrm(ks[5], (DEPTH, 6 * D), 0.02),
        'norm_attn_g': 1.0 + nrm(ks[6], (DEPTH, D), 0.02),
        'norm_ffn_g': 1.0 + nrm(ks[7], (DEPTH, D), 0.02),
        'w_in': nrm(ks[8], (DEPTH, D, Q_COLS + KV_COLS), D ** -0.5),
        'q_a_norm_g': 1.0 + nrm(ks[9], (DEPTH, Q_LORA), 0.02),
        'kv_a_norm_g': 1.0 + nrm(ks[10], (DEPTH, KV_LORA), 0.02),
        'w_uq': nrm(ks[11], (DEPTH, Q_LORA, MLA_HEADS * MLA_QK), Q_LORA ** -0.5),
        'w_ukv': nrm(ks[12], (DEPTH, KV_LORA, MLA_HEADS * (MLA_NOPE + MLA_V)), KV_LORA ** -0.5),
        'na_rel_bias': nrm(ks[13], (DEPTH, NA_HEADS, 2 * NA_WIN_H - 1, 2 * NA_WIN_W - 1), 0.5),
        'w_out': nrm(ks[14], (DEPTH, MIX_WIDTH, D), MIX_WIDTH ** -0.5),
        'w_router_group': nrm(ks[15], (DEPTH, D, N_GROUPS), D ** -0.5),
        'b_router_group': nrm(ks[16], (DEPTH, N_GROUPS), 0.01),
        'w_router_expert': nrm(ks[17], (DEPTH, D, N_EXPERTS), D ** -0.5),
        'b_router_expert': nrm(ks[18], (DEPTH, N_EXPERTS), 0.01),
        'w_gate': nrm(ks[19], (DEPTH, N_EXPERTS, D, D_EXPERT), D ** -0.5),
        'w_up': nrm(ks[20], (DEPTH, N_EXPERTS, D, D_EXPERT), D ** -0.5),
        'w_down': nrm(ks[21], (DEPTH, N_EXPERTS, D_EXPERT, D), D_EXPERT ** -0.5),
        'final_norm_g': 1.0 + nrm(ks[22], (D,), 0.02),
    }

def first_block(x, c, ctx, c_ctx, w_mod, b_mod, norm_attn_g, norm_ffn_g, w_in, q_a_norm_g, kv_a_norm_g,
              w_uq, w_ukv, na_rel_bias, w_out, w_router_group, b_router_group, w_router_expert,
              b_router_expert, w_gate, w_up, w_down, final_norm_g):
    B, N, D = x.shape
    pos = jnp.arange(N)
    cos, sin = axial_rope_tables(pos // GRID_W, pos % GRID_W, x.dtype)
    for l in range(DEPTH):
        sh1, sc1, g1, sh2, sc2, g2 = [m[:, None, :] for m in adaln(c, w_mod[l], b_mod[l])]
        csh1, csc1, cg1, csh2, csc2, cg2 = adaln(c_ctx, w_mod[l], b_mod[l])
        hx = modulate(rmsnorm(x, norm_attn_g[l]), sh1, sc1)
        hc = modulate(rmsnorm(ctx, norm_attn_g[l]), csh1, csc1)

        kn_c, kr_c, v_c, nk_c, nv_c = mixer_keys_values(hc @ w_in[l][:, Q_COLS:], kv_a_norm_g[l], w_ukv[l])
        k_c = mla_keys(kn_c, kr_c[:, :, None, :])

        proj = hx @ w_in[l]
        q_m, nq = mixer_queries(proj[..., :Q_COLS], q_a_norm_g[l], w_uq[l])
        kn, kr, v_m, nk, nv = mixer_keys_values(proj[..., Q_COLS:], kv_a_norm_g[l], w_ukv[l])
        q_m = jnp.concatenate([q_m[..., :MLA_NOPE], apply_rope(q_m[..., MLA_NOPE:], cos, sin)], axis=-1)
        k_m = mla_keys(kn, apply_rope(kr[:, :, None, :], cos, sin))
        o_mla = mla_latent_attention(q_m, k_m, v_m, k_c, v_c)
        o_na = neighbourhood_attention(nq, nk, nv, nk_c, nv_c, na_rel_bias[l])
        mixed = jnp.concatenate([o_mla.reshape(B, N, -1), o_na.reshape(B, N, -1)], axis=-1) @ w_out[l]

        if l < DEPTH - 1:
            Bc, C = ctx.shape[:2]
            q_c, nq_c = mixer_queries(hc @ w_in[l][:, :Q_COLS], q_a_norm_g[l], w_uq[l])
            mixed_c = jnp.concatenate([dense_attention(q_c, k_c, v_c).reshape(Bc, C, -1),
                                       dense_attention(nq_c, nk_c, nv_c).reshape(Bc, C, -1)], axis=-1) @ w_out[l]
            ctx = ctx + cg1 * mixed_c
            hc2 = modulate(rmsnorm(ctx, norm_ffn_g[l]), csh2, csc2)
            ctx = ctx + cg2 * hierarchical_moe(hc2, w_router_group[l], b_router_group[l], w_router_expert[l],
                                               b_router_expert[l], w_gate[l], w_up[l], w_down[l])

        x = x + g1 * mixed
        hx2 = modulate(rmsnorm(x, norm_ffn_g[l]), sh2, sc2)
        x = x + g2 * hierarchical_moe(hx2, w_router_group[l], b_router_group[l], w_router_expert[l],
                                      b_router_expert[l], w_gate[l], w_up[l], w_down[l])
    return rmsnorm(x, final_norm_g)


CHUNK = 64
D_MIX = D_MODEL
HEAD_DIM = 64
N_HEADS_A = 8
N_HEADS_B = 8
D_A = N_HEADS_A * HEAD_DIM
D_B = N_HEADS_B * HEAD_DIM
SG_BLOCK = 128
D_FF = 2816
CONV_W = 3
EPS = 1e-6
D_IN = 2 * D_A + 3 * D_B + N_HEADS_B


def rms_norm(x, g):
    xf = x.astype(jnp.float32)
    y = xf * lax.rsqrt(jnp.mean(xf * xf, axis=-1, keepdims=True) + EPS)
    return (y * g.astype(jnp.float32)).astype(x.dtype)

def spatial_gating(u, v, ln_g, w_s, b_s):
    B, S, _ = u.shape
    n = S // SG_BLOCK
    v = v.reshape(B, n, SG_BLOCK, N_HEADS_A, HEAD_DIM)
    vf = v.astype(jnp.float32)
    mu = jnp.mean(vf, axis=-1, keepdims=True)
    var = jnp.mean(jnp.square(vf - mu), axis=-1, keepdims=True)
    vn = ((vf - mu) * lax.rsqrt(var + EPS) * ln_g.astype(jnp.float32)).astype(u.dtype)
    pos_chunk = jnp.arange(SG_BLOCK) // CHUNK
    mask = pos_chunk[:, None] >= pos_chunk[None, :]
    w = jnp.where(mask[None], w_s, 0).astype(u.dtype)
    mixed = jnp.einsum('hts,bnshd->bnthd', w, vn) + b_s.T.astype(u.dtype)[None, None, :, :, None]
    out = u.reshape(B, n, SG_BLOCK, N_HEADS_A, HEAD_DIM) * mixed
    return out.reshape(B, S, D_A)

def forgetting_attention(q, k, v, f_logit):
    B, S, H, Dh = q.shape
    n = S // Q_BLOCK
    scale = Dh ** -0.5
    c = jnp.cumsum(jax.nn.log_sigmoid(f_logit.astype(jnp.float32)), axis=1)
    c = c.transpose(0, 2, 1)
    qb = q.reshape(B, n, Q_BLOCK, H, Dh).transpose(1, 0, 3, 2, 4)
    cb = c.reshape(B, H, n, Q_BLOCK).transpose(2, 0, 1, 3)
    kpos = jnp.arange(S)

    def block(args):
        i, qi, ci = args
        s = jnp.einsum('bhtd,bshd->bhts', qi, k, preferred_element_type=jnp.float32) * scale
        s = s + ci[..., :, None] - c[:, :, None, :]
        qpos = i * Q_BLOCK + jnp.arange(Q_BLOCK)
        s = jnp.where(kpos[None, :] <= qpos[:, None], s, -jnp.inf)
        p = jax.nn.softmax(s, axis=-1)
        return jnp.einsum('bhts,bshd->bthd', p.astype(v.dtype), v)

    out = lax.map(block, (jnp.arange(n), qb, cb))
    return out.transpose(1, 0, 2, 3, 4).reshape(B, S, H * Dh)

def conv_ffn(h, w_up, w_conv, b_conv, w_down):
    a = h @ w_up
    C = a.shape[-1]
    a = lax.conv_general_dilated(
        a, w_conv[:, None, :].astype(a.dtype), window_strides=(1,),
        padding=[(CONV_W - 1, 0)], dimension_numbers=('NWC', 'WIO', 'NWC'),
        feature_group_count=C) + b_conv.astype(a.dtype)
    g, val = jnp.split(a, 2, axis=-1)
    return (jax.nn.silu(g) * val) @ w_down

def second_inputs(seed: int = 0) -> dict:
    key = jax.random.key(seed)
    ks = jax.random.split(key, 14)
    L = DEPTH
    nrm = jax.random.normal
    return {
        "x": nrm(ks[0], (BATCH, SEQ, D_MODEL), jnp.float32),
        "norm_mix_g": 1.0 + 0.02 * nrm(ks[1], (L, D_MODEL), jnp.float32),
        "w_in": nrm(ks[2], (L, D_MODEL, D_IN), jnp.float32) * D_MODEL ** -0.5,
        "f_bias": 3.0 + 0.5 * nrm(ks[3], (L, N_HEADS_B), jnp.float32),
        "sg_ln_g": 1.0 + 0.02 * nrm(ks[4], (L, N_HEADS_A, HEAD_DIM), jnp.float32),
        "sg_w": nrm(ks[5], (L, N_HEADS_A, SG_BLOCK, SG_BLOCK), jnp.float32) * SG_BLOCK ** -0.5,
        "sg_b": 1.0 + 0.1 * nrm(ks[6], (L, N_HEADS_A, SG_BLOCK), jnp.float32),
        "w_out": nrm(ks[7], (L, D_MIX, D_MODEL), jnp.float32) * D_MIX ** -0.5,
        "norm_ffn_g": 1.0 + 0.02 * nrm(ks[8], (L, D_MODEL), jnp.float32),
        "w_up": nrm(ks[9], (L, D_MODEL, 2 * D_FF), jnp.float32) * D_MODEL ** -0.5,
        "w_conv": nrm(ks[10], (L, CONV_W, 2 * D_FF), jnp.float32) * CONV_W ** -0.5,
        "b_conv": 0.02 * nrm(ks[11], (L, 2 * D_FF), jnp.float32),
        "w_down": nrm(ks[12], (L, D_FF, D_MODEL), jnp.float32) * D_FF ** -0.5,
        "norm_final_g": 1.0 + 0.02 * nrm(ks[13], (D_MODEL,), jnp.float32),
    }

def second_block(x, norm_mix_g, w_in, f_bias, sg_ln_g, sg_w, sg_b, w_out,
              norm_ffn_g, w_up, w_conv, b_conv, w_down, norm_final_g):
    B, S, _ = x.shape
    for l in range(DEPTH):
        h = rms_norm(x, norm_mix_g[l])
        z = h @ w_in[l]
        o = 0
        u_a = jax.nn.gelu(z[..., o:o + D_A], approximate=False); o += D_A
        v_a = jax.nn.gelu(z[..., o:o + D_A], approximate=False); o += D_A
        q_b = z[..., o:o + D_B].reshape(B, S, N_HEADS_B, HEAD_DIM); o += D_B
        k_b = z[..., o:o + D_B].reshape(B, S, N_HEADS_B, HEAD_DIM); o += D_B
        v_b = z[..., o:o + D_B].reshape(B, S, N_HEADS_B, HEAD_DIM); o += D_B
        f_logit = z[..., o:o + N_HEADS_B] + f_bias[l].astype(z.dtype)
        out_a = spatial_gating(u_a, v_a, sg_ln_g[l], sg_w[l], sg_b[l])
        out_b = forgetting_attention(q_b, k_b, v_b, f_logit)
        x = x + jnp.concatenate([out_a, out_b], axis=-1) @ w_out[l]
        x = x + conv_ffn(rms_norm(x, norm_ffn_g[l]), w_up[l], w_conv[l], b_conv[l], w_down[l])
    return rms_norm(x, norm_final_g)


def setup_inputs(seed=0):
    out = dict(first_inputs(seed))
    for name, value in second_inputs(seed + 1).items():
        if name != "x":
            out[name + "_2"] = value
    return out


def reference(
    x, c, ctx, c_ctx, w_mod, b_mod, norm_attn_g, norm_ffn_g, w_in, q_a_norm_g, kv_a_norm_g,
    w_uq, w_ukv, na_rel_bias, w_out, w_router_group, b_router_group, w_router_expert,
    b_router_expert, w_gate, w_up, w_down, final_norm_g, norm_mix_g_2, w_in_2, f_bias_2,
    sg_ln_g_2, sg_w_2, sg_b_2, w_out_2, norm_ffn_g_2, w_up_2, w_conv_2, b_conv_2, w_down_2,
    norm_final_g_2,
):
    x = first_block(
        x, c, ctx, c_ctx, w_mod, b_mod, norm_attn_g, norm_ffn_g, w_in, q_a_norm_g, kv_a_norm_g,
        w_uq, w_ukv, na_rel_bias, w_out, w_router_group, b_router_group, w_router_expert,
        b_router_expert, w_gate, w_up, w_down, final_norm_g,
    )
    return second_block(
        x, norm_mix_g_2, w_in_2, f_bias_2, sg_ln_g_2, sg_w_2, sg_b_2, w_out_2, norm_ffn_g_2,
        w_up_2, w_conv_2, b_conv_2, w_down_2, norm_final_g_2,
    )


_drawn_inputs = setup_inputs


def setup_inputs(seed=0):
    import zlib

    import numpy as np

    out = dict(_drawn_inputs(seed))
    spreads = {}
    factors = {'b_mod': 2.728,
     'norm_attn_g': 8.0,
     'norm_ffn_g': 4.956,
     'q_a_norm_g': 8.0,
     'kv_a_norm_g': 8.0,
     'na_rel_bias': 4.467,
     'b_router_group': 8.0,
     'b_router_expert': 8.0,
     'norm_mix_g_2': 3.508,
     'sg_ln_g_2': 7.938,
     'norm_ffn_g_2': 11.191,
     'b_conv_2': 22.955,
     'norm_final_g_2': 21.554,
     'sg_b_2': 3.254}
    for name, (base, spread) in spreads.items():
        noise = np.random.default_rng([zlib.crc32(name.encode()), seed]).standard_normal(out[name].shape)
        drawn = base * np.exp(spread * noise) if base else spread * noise
        out[name] = __import__('jax').numpy.asarray(drawn.astype(out[name].dtype))
    for name, factor in factors.items():
        out[name] = (out[name] * factor).astype(out[name].dtype)
    return out
```

```python
from contextlib import ExitStack

import concourse.bass as bass
from concourse import mybir

P = 128
T = 256
D = 1024
KD = D // P
NT = T // P
H = 8
HD = 64
QK = 96
NOPE, ROPE = 64, 32
QL, KVL = 384, 256
GRID_W = 64
NE, NG, EG = 16, 4, 4
FE = 512
FF = 2816
NP = FF // P
EPS = 1e-6
BIG = 1e30

ALU = mybir.AluOpType
ACT = mybir.ActivationFunctionType
F32 = mybir.dt.float32
AX = mybir.AxisListType.X

SLOTS = 6
SLOT = 4096
N_MOD = 12
L_QL, L_KVL, L_NAQ, L_NAK, L_NAV, L_UQ, L_UKV = range(4, 11)
L_MOD2 = 11
L_OUT = 19
L_MOE = 21
L_IN2 = L_MOE + 3 * NE
L_OUT2 = L_IN2 + 5
L_UP = L_OUT2 + 2
N_UP = NP // 2
L_DOWN = L_UP + N_UP
N_DOWN = (NP + 3) // 4
N_LOADS = L_DOWN + N_DOWN


def slot_of(n):
    if L_UP <= n < L_UP + N_UP - 1:
        return 4 + (n - L_UP) % 2
    if n == L_UP + N_UP - 1:
        return 0
    if n >= L_DOWN:
        return (n - L_DOWN + 1) % SLOTS
    return n % SLOTS


def last_in_slot(n):
    before = [m for m in range(n) if slot_of(m) == slot_of(n)]
    return before[-1] if before else None


def dmas_of(n):
    return 2 if L_UP <= n < L_DOWN else 1


def landed_count(n):
    return 16 * sum(dmas_of(m) for m in range(n + 1) if slot_of(m) == slot_of(n))


def columns(widths):
    at, out = 0, {}
    for name, w in widths:
        out[name] = at
        at += w
    return out, at


VEC, NVEC = columns([("c", 16), ("b_mod", 48), ("g_attn", 8), ("g_ffn", 8), ("g_qa", 3), ("g_kva", 2),
                     ("g_final", 8), ("g_mix2", 8), ("g_ffn2", 8), ("b_conv", 44), ("w_conv", 132),
                     ("g_final2", 8), ("sg_b", 8)])
ROW, NROW = columns([("b_router", 20), ("f_bias", 8), ("sg_ln", 512)])
CON, NCON = columns([("ident", 128), ("tri", 128), ("upper", 128), ("ones", 128), ("namask", 64),
                     ("rot", 32), ("cos", 512), ("sin", 512), ("desc", 4)])

PROD = ([("ql", i, "AD"[i % 2]) for i in range(3)] + [("kvl", 0, "D"), ("kvl", 1, "A"), ("kr", 0, "D")]
        + [("naq", i, "AD"[i % 2]) for i in range(4)]
        + [("nak", i, "AD"[i % 2]) for i in range(4)] + [("nav", i, "AD"[i % 2]) for i in range(4)]
        + [("uq", i, "AD"[i % 2]) for i in range(8)] + [("kn", i, "A") for i in range(2)]
        + [("rotk", 0, "D")] + [("rotq", i, "D") for i in range(4)]
        + [("kn", i, "A") for i in range(2, 8)] + [("vm", i, "AD"[i % 2]) for i in range(4)])
N_BEFORE_LAT = 10
PROD2 = ([("f", 0, "D")] + [("u", i, "A") for i in range(2)] + [("va", i, "A") for i in range(2)]
         + [("q", i, "D") for i in range(4)] + [("cq", 0, "D")] + [("nck", i, "A") for i in range(4)]
         + [("k", i, "D") for i in range(4)] + [("v", i, "A") for i in range(2)])


def copied(prod, n):
    e = prod[n][2]
    return e, sum(1 for p in prod[:n + 1] if p[2] == e)


def total(prod, e):
    return sum(1 for p in prod if p[2] == e)


UNITS = [(a, h, q, 4) for a in range(2) for h in range(H) for q in range(NT)]
UNITS2 = [(2, h, q, q + 1) for h in range(H) for q in range(NT)]


def block_pair_kernel(nc, xT_d, ctxT_d, vec_d, row_d, con_d, w_mod, w_in, w_uq, w_ukv, bias_d, w_out,
                      wr_d, w_gate, w_up, w_down, w_in2, wf_d, sgw_d, w_out2, w_up2, w_down2, out_d):
    with ExitStack() as ctx:
        def sb(name, shape):
            return ctx.enter_context(nc.sbuf_tensor(name, shape, F32))

        def sem(name):
            return ctx.enter_context(nc.semaphore(name))

        bank = [ctx.enter_context(nc.psum_tensor(f"bank{i}", [P, 512], F32)) for i in range(8)]

        ring = sb("ring", [P, SLOTS, SLOT])
        xT = sb("xT", [P, KD, T])
        big = sb("big", [P, 4096])
        arena = sb("arena", [P, 9216])
        att = sb("att", [P, 4, 512])
        mixT = sb("mixT", [P, KD, T])
        osb = sb("osb", [P, NT, D])
        con = sb("con", [P, NCON])
        row = sb("row", [P, NROW])
        vec = sb("vec", [P, NVEC])
        lat = sb("lat", [P, 1792])
        rstd = sb("rstd", [P, 512])
        sgw = sb("sgw", [P, H, P])
        wr = sb("wr", [P, KD, 20])
        wf = sb("wf", [P, KD, 8])
        cs = sb("cs", [P, KD, 2])
        mod = sb("mod", [P, 48, 2])
        A1 = sb("A1", [P, KD, 2])
        A2 = sb("A2", [P, KD])
        nmax = sb("nmax", [P, 48])
        rsum = sb("rsum", [P, 48])
        rinv = sb("rinv", [P, 48])
        small = sb("small", [P, 16, 32])
        zeros = sb("zeros", [P, P])

        ctxT = osb[:, :, :].rearrange("p a (b t) -> p (a b) t", t=T)
        hT = big[:, :].rearrange("p (k t) -> p k t", t=2 * T)
        qT = big[0:QK, 0:2048].rearrange("p (h t) -> p h t", t=T)
        vm = big[:, 2048:4096].rearrange("p (j n) -> p j n", n=512)
        h2 = big[:, 0:2048].rearrange("p (k t) -> p k t", t=T)
        outT = big[:, 2048:4096].rearrange("p (k t) -> p k t", t=T)
        kT = arena[0:QK, 0:4096].rearrange("p (h t) -> p h t", t=2 * T)
        bias = arena[:, 0:4096].rearrange("p (h q n) -> p h q n", q=NT, n=T)
        comb_b = arena[:, 0:4096].rearrange("p (e t) -> p e t", t=T)
        naq = arena[:, 4096:5120].rearrange("p (i t) -> p i t", t=T)
        nak = arena[:, 5120:7168].rearrange("p (i t) -> p i t", t=2 * T)
        nav = arena[:, 7168:9216].rearrange("p (j n) -> p j n", n=512)
        hidM = arena[:, 4096:6144].rearrange("p (b f t) -> p b f t", b=2, t=T)
        gsb = arena[:, 6144:6656].rearrange("p (b t) -> p b t", t=T)
        nck = arena[:, 0:2048].rearrange("p (h t) -> p h t", t=T)
        nck0 = arena[:, 2048:3072].rearrange("p (h t) -> p h t", t=P)
        lnt = arena[:, 3072:4096].rearrange("p (n c) -> p n c", c=512)
        ug = arena[:, 4096:5120].rearrange("p (n c) -> p n c", c=512)
        vg = arena[:, 5120:6144].rearrange("p (n c) -> p n c", c=512)
        q2 = arena[:, 6144:7168].rearrange("p (i t) -> p i t", t=T)
        k2 = arena[:, 7168:8192].rearrange("p (i t) -> p i t", t=T)
        v2 = arena[:, 8192:9216].rearrange("p (n c) -> p n c", c=512)
        hidF = arena[:, 0:NP * T].rearrange("p (i t) -> p i t", t=T)
        yconv = lat[:, 0:1024].rearrange("p (b g t) -> p b g t", b=2, t=T)
        qlat = lat[:, 0:768].rearrange("p (i t) -> p i t", t=T)
        kvlat = lat[:, 768:1792].rearrange("p (i t) -> p i t", t=2 * T)
        rq = mixT[:, 0, :]
        rkv = mixT[:, 2:4, :].rearrange("p a t -> p (a t)")
        kr = mixT[64:96, 4:6, :].rearrange("p a t -> p (a t)")
        rtmp = mixT[64:96, 6:8, :].rearrange("p a t -> p (a t)")
        attf = att[:, :, :].rearrange("p a b -> p (a b)")
        sq = attf.rearrange("p (k t) -> p k t", t=T)

        ident = con[:, CON["ident"]:CON["ident"] + P]
        tri = con[:, CON["tri"]:CON["tri"] + P]
        upper = con[:, CON["upper"]:CON["upper"] + P]
        upper_ones = con[:, CON["upper"]:CON["upper"] + 2 * P]
        ones = con[:, CON["ones"]:CON["ones"] + P]
        namask = con[:, CON["namask"]:CON["namask"] + 64]
        rot = con[64:96, CON["rot"]:CON["rot"] + 32]
        cos = con[64:96, CON["cos"]:CON["cos"] + 512]
        sin = con[64:96, CON["sin"]:CON["sin"] + 512]
        desc = con[:, CON["desc"]:CON["desc"] + 4]

        def v_(name, i, n=1):
            return vec[:, VEC[name] + i:VEC[name] + i + n]

        landed = [sem(f"landed{i}") for i in range(SLOTS)]
        used = sem("used")
        in_x, in_vec, in_con, in_row = sem("in_x"), sem("in_vec"), sem("in_con"), sem("in_row")
        in_sg, in_bias = sem("in_sg"), sem("in_bias")
        silu_c = sem("silu_c")
        vstep, astep, gstep = sem("vstep"), sem("astep"), sem("gstep")
        squares = [sem(f"squares{i}") for i in range(6)]
        sumsq = [sem(f"sumsq{i}") for i in range(6)]
        var = [sem(f"var{i}") for i in range(6)]
        std = [sem(f"std{i}") for i in range(6)]
        normed = [sem(f"normed{i}") for i in range(6)]
        shifted = [sem(f"shifted{i}") for i in range(2)]
        prod_ready, prod_a, prod_d = sem("prod_ready"), sem("prod_a"), sem("prod_d")
        lat_sq, lat_ss, lat_var, lat_std, lat_done = (sem("lat_sq"), sem("lat_ss"), sem("lat_var"),
                                                      sem("lat_std"), sem("lat_done"))
        kr_done, kr_spread = sem("kr_done"), sem("kr_spread")
        ATT = [{n: sem(f"{n}{i}") for n in ("scores", "maxed", "exped", "turned", "ptd", "pta", "pv")}
               for i in range(2)]
        bias_ready = sem("bias_ready")
        o_out = sem("o_out")
        mix_t, mix_a, mix_d = sem("mix_t"), sem("mix_a"), sem("mix_d")
        proj_out, resid = sem("proj_out"), sem("resid")
        logits, gdiff, gexp, ediff, eexp = sem("logits"), sem("gdiff"), sem("gexp"), sem("ediff"), sem("eexp")
        comb_done, comb_t = sem("comb_done"), sem("comb_t")
        gu, silu_g, gated, gu_free = sem("gu"), sem("silu_g"), sem("gated"), sem("gu_free")
        resid_m = sem("resid_m")
        prod2_ready, prod2_a, prod2_d = sem("prod2_ready"), sem("prod2_a"), sem("prod2_d")
        f_abs, f_ln, lf_done, nck_done = sem("f_abs"), sem("f_ln"), sem("lf_done"), sem("nck_done")
        sg_zero, ln_var, ln_std, vn_done, sg_mm, sg_done = (sem("sg_zero"), sem("ln_var"), sem("ln_std"),
                                                            sem("vn_done"), sem("sg_mm"), sem("sg_done"))
        o2_out, mix2_t, mix2_a, mix2_d = sem("o2_out"), sem("mix2_t"), sem("mix2_a"), sem("mix2_d")
        proj2_out, resid2 = sem("proj2_out"), sem("resid2")
        up_ready, conv0, tap1, tap2, silu_f, hid_done = (sem("up_ready"), sem("conv0"), sem("tap1"),
                                                         sem("tap2"), sem("silu_f"), sem("hid_done"))
        down_done, resid3, out_done = sem("down_done"), sem("resid3"), sem("out_done")

        block = ctx.enter_context(nc.Block())

        def yacc(m):
            return bank[4 + m // 2][:, (m % 2) * T:(m % 2 + 1) * T]

        NORM_BANK = [7, 7, 0, 1, 7, 0]

        @block.sync
        def _(sp):
            def issue(n, dst_cols, shape_k, src):
                prev = last_in_slot(n)
                if prev is not None:
                    sp.wait_ge(used, prev + 1)
                dst = ring[:, slot_of(n), 0:dst_cols].rearrange("p (k n) -> p k n", k=shape_k)
                sp.dma_start(dst, src).then_inc(landed[slot_of(n)], 16)

            wm = w_mod.rearrange("(k p) n -> p k n", p=P)
            wi = w_in.rearrange("(k p) n -> p k n", p=P)
            wi2 = w_in2.rearrange("(k p) n -> p k n", p=P)
            wo = w_out.rearrange("(k p) n -> p k n", p=P)
            wo2 = w_out2.rearrange("(k p) n -> p k n", p=P)
            wu2 = w_up2.rearrange("(k p) (g n) -> p k g n", p=P, g=2)
            wd2 = w_down2.rearrange("(k p) n -> p k n", p=P)
            for n in range(4):
                issue(n, 4096, KD, wm[:, :, n * 512:(n + 1) * 512])
            issue(L_QL, KD * QL, KD, wi[:, :, 0:QL])
            issue(L_KVL, KD * 288, KD, wi[:, :, 896:1184])
            issue(L_NAQ, 4096, KD, wi[:, :, 384:896])
            issue(L_NAK, 4096, KD, wi[:, :, 1184:1696])
            issue(L_NAV, 4096, KD, wi[:, :, 1696:2208])
            issue(L_UQ, 3 * 768, 3, w_uq.rearrange("(k p) n -> p k n", p=P))
            issue(L_UKV, 2 * 1024, 2, w_ukv.rearrange("(k p) n -> p k n", p=P))
            for n in range(4, N_MOD):
                issue(L_MOD2 + n - 4, 4096, KD, wm[:, :, n * 512:(n + 1) * 512])
            for n in range(2):
                issue(L_OUT + n, 4096, KD, wo[:, :, n * 512:(n + 1) * 512])
            with sp.Fori(0, NE // 2) as i:
                for e in range(2):
                    for j, w in enumerate((w_gate, w_up, w_down)):
                        n = L_MOE + 3 * e + j
                        sp.wait_ge(used, i * 6 + (n - SLOTS + 1))
                        sp.dma_start(ring[:, slot_of(n), :].rearrange("p (k n) -> p k n", k=4 if j == 2 else KD),
                                     w[i * 2 + e].rearrange("(k p) n -> p k n", p=P)
                                     ).then_inc(landed[slot_of(n)], 16)
            for n in range(5):
                issue(L_IN2 + n, 4096, KD, wi2[:, :, n * 512:(n + 1) * 512])
            for n in range(2):
                issue(L_OUT2 + n, 4096, KD, wo2[:, :, n * 512:(n + 1) * 512])

            def up_load(n, at):
                for g in range(2):
                    sp.dma_start(ring[:, slot_of(n), :].rearrange("p (k g n) -> p k g n", k=KD, g=2)[:, :, g, :],
                                 wu2[:, :, g, bass.ds(at, 256)]).then_inc(landed[slot_of(n)], 16)
            for e in range(2):
                sp.wait_ge(used, last_in_slot(L_UP + e) + 1)
                up_load(L_UP + e, 256 * e)
            with sp.Fori(1, (N_UP - 1) // 2) as i:
                for e in range(2):
                    sp.wait_ge(used, i * 2 + (L_UP + e - 1))
                    up_load(L_UP + e, i * 512 + 256 * e)
            sp.wait_ge(used, last_in_slot(L_UP + N_UP - 1) + 1)
            up_load(L_UP + N_UP - 1, 256 * (N_UP - 1))
            for n in range(N_DOWN):
                k = min(4, NP - 4 * n)
                issue(L_DOWN + n, k * D, k, wd2[:, 4 * n:4 * n + k, :])
            for m in range(KD):
                sp.wait_ge(normed[5], m + 1)
                sp.dma_start(out_d[:, m, :], outT[:, m, :]).then_inc(out_done, 16)
            sp.wait_ge(out_done, 16 * KD)

        @block.gpsimd
        def _(pool):
            pool.wait_ge(kr_done, 1)
            nc.gpsimd.tensor_copy(kT[64:96, :, :], kr.unsqueeze(1).broadcast_to([32, H, 512])).then_inc(kr_spread, 1)
            for half in range(2):
                pool.wait_ge(ATT[0]["scores"], 8 * (half + 1))
                if half == 0:
                    pool.wait_ge(kr_spread, 1)
                pool.dma_start(arena[:, 2048 * half:2048 * (half + 1)],
                               bias_d[:, 2048 * half:2048 * (half + 1)]).then_inc(in_bias, 16)
                pool.wait_ge(in_bias, 16 * (half + 1))
                b = arena[:, 2048 * half:2048 * (half + 1)].rearrange("p (a n) -> p a n", n=GRID_W)
                nc.gpsimd.tensor_tensor(b, b, namask.unsqueeze(1).broadcast_to([P, 32, GRID_W]),
                                        ALU.add).then_inc(bias_ready, 1)
                pool.wait_ge(bias_ready, half + 1)
            pool.wait_ge(in_sg, 16)
            nc.gpsimd.memset(sgw[64:128, :, 0:64], 0.0).then_inc(sg_zero, 1)
            pool.wait_ge(sg_zero, 1)
            pool.wait_ge(prod2_a, copied(PROD2, [p[0] for p in PROD2].index("nck") + 3)[1])
            nc.gpsimd.tensor_tensor(nck0[:, :, :], nck[:, :, 0:P], tri.unsqueeze(1).broadcast_to([P, H, P]),
                                    ALU.add).then_inc(nck_done, 1)
            pool.wait_ge(nck_done, 1)
            nc.gpsimd.tensor_tensor(nck[:, :, P:T], nck[:, :, P:T], tri.unsqueeze(1).broadcast_to([P, H, P]),
                                    ALU.add).then_inc(nck_done, 1)

        @block.scalar
        def _(act):
            steps = [0]

            def link(ins):
                steps[0] += 1
                ins.then_inc(astep, 1)
                act.wait_ge(astep, steps[0])

            act.dma_start(vec[:, :], vec_d).then_inc(in_vec, 16)
            act.dma_start(xT[:, :, :], xT_d).then_inc(in_x, 16)
            act.dma_start(con[:, :], con_d).then_inc(in_con, 16)
            act.dma_start(ctxT, ctxT_d).then_inc(in_x, 16)
            act.dma_start(row[:, :], row_d.broadcast_to([P, NROW])).then_inc(in_row, 16)
            act.dma_start(wr[:, :, :], wr_d).then_inc(in_row, 16)
            act.dma_start(wf[:, :, :], wf_d).then_inc(in_row, 16)
            act.dma_start(sgw[:, :, :], sgw_d).then_inc(in_sg, 16)

            act.wait_ge(in_vec, 16)
            nc.scalar.activation(cs[:, :, :].rearrange("p k c -> p (k c)"), vec[:, 0:16], ACT.Silu).then_inc(silu_c, 1)
            act.wait_ge(in_x, 32)
            nc.scalar.activation(hT[:, :, 0:T], xT[:, :, :], ACT.Square).then_inc(squares[0], 1)
            nc.scalar.activation(hT[:, :, T:2 * T], ctxT, ACT.Square).then_inc(squares[0], 1)
            act.wait_ge(var[0], 1)
            nc.scalar.activation(rstd[:, :], rstd[:, :], ACT.Sqrt).then_inc(std[0], 1)
            for k in range(KD):
                for s in range(2):
                    act.wait_ge(normed[0], 2 * k + s + 1)
                    nc.scalar.activation(hT[:, k, s * T:(s + 1) * T], hT[:, k, s * T:(s + 1) * T], ACT.Identity,
                                         bias=mod[:, k, s:s + 1]).then_inc(shifted[0], 1)

            def out_of_psum(n):
                kind, i, e = PROD[n]
                src = bank[n % 4]
                act.wait_ge(prod_ready, n + 1)
                scale = 1.0
                if kind == "ql":
                    dst, src = qlat[:, i, :], src[:, 0:T]
                elif kind == "kvl":
                    dst, src = kvlat[:, i, :], src[:, :]
                elif kind == "naq":
                    dst, src, scale = naq[:, i, :], src[:, 0:T], HD ** -0.5
                elif kind == "nak":
                    dst, src = nak[:, i, :], src[:, :]
                elif kind == "nav":
                    dst, src = nav[:, i, :], src[:, :]
                elif kind == "uq":
                    dst, src, scale = qT[:, i, :], src[0:QK, 0:T], QK ** -0.5
                elif kind == "kn":
                    dst, src = kT[0:NOPE, i, :], src[0:NOPE, :]
                elif kind == "vm":
                    dst, src = vm[:, i, :], src[:, :]
                nc.scalar.activation(dst, src, ACT.Copy, scale=scale).then_inc(prod_a, 1)

            done = 0
            for n, (kind, i, e) in enumerate(PROD):
                if n == 5:
                    act.wait_ge(prod_d, copied(PROD, 3)[1])
                    act.wait_ge(prod_a, copied(PROD, 4)[1])
                    nc.scalar.activation(attf[:, 0:1792], lat[:, :], ACT.Square).then_inc(lat_sq, 1)
                if n == N_BEFORE_LAT:
                    act.wait_ge(lat_var, 2)
                    nc.scalar.activation(rq, rq, ACT.Sqrt).then_inc(lat_std, 1)
                    nc.scalar.activation(rkv, rkv, ACT.Sqrt).then_inc(lat_std, 1)
                if e == "A":
                    out_of_psum(n)

            def exps(units, A, s):
                a, h, q, nk = units[s]
                u = 16 * a + 8 * q + h
                act.wait_ge(A["maxed"], s + 1)
                if s >= 2:
                    act.wait_ge(A["turned"], s - 1)
                nc.scalar.activation(att[:, s % 2, 0:nk * P], bank[s % 2][:, 0:nk * P], ACT.Exp,
                                     bias=nmax[:, u:u + 1], accum_out=rsum[:, u:u + 1]).then_inc(A["exped"], 1)

            def turn_copy(units, A, s):
                w = units[s][3] * P
                act.wait_ge(A["turned"], s + 1)
                if s >= 2:
                    act.wait_ge(A["pv"], s - 1)
                nc.scalar.activation(att[:, 3, 0:w], bank[3][:, 0:w], ACT.Copy).then_inc(A["pta"], 1)

            def attention(units, A):
                for s in range(len(units) + 1):
                    if s < len(units):
                        exps(units, A, s)
                    if s >= 1 and (s - 1) % 2:
                        turn_copy(units, A, s - 1)

            attention(UNITS, ATT[0])

            def mix_copy(ready, done):
                for c in (0, 2):
                    act.wait_ge(ready, c + 1)
                    nc.scalar.activation(mixT[:, 2 * c:2 * c + 2, :].rearrange("p a t -> p (a t)"), bank[c][:, :],
                                         ACT.Copy).then_inc(done, 1)

            mix_copy(mix_t, mix_a)

            def norm(r, updated):
                for k in range(KD):
                    act.wait_ge(updated, k + 1)
                    nc.scalar.activation(sq[:, k, :], xT[:, k, :], ACT.Square).then_inc(squares[r], 1)
                act.wait_ge(var[r], 1)
                nc.scalar.activation(rstd[:, 0:T], rstd[:, 0:T], ACT.Sqrt).then_inc(std[r], 1)

            norm(1, resid)
            for k in range(KD):
                act.wait_ge(normed[1], k + 1)
                nc.scalar.activation(h2[:, k, :], h2[:, k, :], ACT.Identity, bias=mod[:, 24 + k, 0:1]
                                     ).then_inc(shifted[1], 1)
            act.wait_ge(gdiff, 1)
            nc.scalar.activation(small[:, 1, 0:8], small[:, 1, 0:8], ACT.Exp).then_inc(gexp, 1)
            act.wait_ge(ediff, 1)
            nc.scalar.activation(small[:, 5, 0:8], small[:, 5, 0:8], ACT.Exp).then_inc(eexp, 1)
            with act.Fori(0, NE // 2) as i:
                for e in range(2):
                    for f in range(4):
                        act.wait_ge(gu, i * 8 + (4 * e + f + 1))
                        act.wait_ge(gu_free, i * 8 + (8 + 4 * e + f - 1))
                        nc.scalar.activation(gsb[:, f % 2, :], bank[f][:, 0:T], ACT.Silu).then_inc(silu_g, 1)
            norm(2, resid_m)
            norm(3, normed[2])

            def out_of_psum2(n):
                kind, i, e = PROD2[n]
                src = bank[n % 4]
                act.wait_ge(prod2_ready, n + 1)
                if kind == "u":
                    ins = nc.scalar.activation(ug[:, i, :], src[:, :], ACT.Gelu)
                elif kind == "va":
                    ins = nc.scalar.activation(vg[:, i, :], src[:, :], ACT.Gelu)
                elif kind == "nck":
                    ins = nc.scalar.activation(nck[:, 2 * i:2 * i + 2, :].rearrange("p a t -> p (a t)"), src[:, :],
                                               ACT.Copy, scale=-1.0)
                elif kind == "v":
                    ins = nc.scalar.activation(v2[:, i, :], src[:, :], ACT.Copy)
                ins.then_inc(prod2_a, 1)

            act.wait_ge(f_abs, 1)
            link(nc.scalar.activation(small[:, 1, 0:16], small[:, 1, 0:16], ACT.Exp))
            nc.scalar.activation(small[:, 1, 0:16], small[:, 1, 0:16], ACT.Ln, bias=1.0).then_inc(f_ln, 1)
            for n, (kind, i, e) in enumerate(PROD2):
                if e == "A":
                    out_of_psum2(n)
            act.wait_ge(ln_var, 1)
            nc.scalar.activation(small[:, 6, 0:16], small[:, 6, 0:16], ACT.Sqrt).then_inc(ln_std, 1)
            attention(UNITS2, ATT[1])
            mix_copy(mix2_t, mix2_a)
            norm(4, resid2)

            def conv(i, j, first):
                b = j % 2
                act.wait_ge(up_ready, i * 4 + (j + 1))
                if not (first and j < 2):
                    act.wait_ge(hid_done, i * 4 + (j - 1))
                for g in range(2):
                    at = i * 4 + (j + 22 * g)
                    nc.scalar.activation(yconv[:, b, g, :], bank[j % 4][:, g * T:(g + 1) * T], ACT.Identity,
                                         bias=vec[:, bass.ds(at + VEC["b_conv"], 1)],
                                         scale=vec[:, bass.ds(at + (VEC["w_conv"] + 88), 1)]).then_inc(conv0, 1)
                act.wait_ge(tap2, i * 8 + (2 * j + 1))
                nc.scalar.activation(yconv[:, b, 0, :], yconv[:, b, 0, :], ACT.Silu).then_inc(silu_f, 1)

            for j in range(4):
                conv(0, j, True)
            with act.Fori(1, NP // 4) as i:
                for j in range(4):
                    conv(i, j, False)
            for j in range(NP % 4):
                conv(NP // 4, j, False)
            norm(5, resid3)

        @block.tensor
        def _(pe):
            def slot(n, k):
                return ring[:, slot_of(n), 0:SLOT // k * k].rearrange("p (k n) -> p k n", k=k)

            def arrive(n):
                pe.wait_ge(landed[slot_of(n)], landed_count(n))

            pe.wait_ge(in_con, 16)
            pe.wait_ge(squares[0], 2)
            for k in range(KD):
                last = nc.tensor.matmul(bank[7][:, :], ones, hT[:, k, :], start=(k == 0), stop=(k == KD - 1))
            last.then_inc(sumsq[0], 1)

            def mod_half(half, n):
                arrive(n)
                w = slot(n, KD)
                for t in range(4):
                    c = 8 * half + 2 * t
                    for k in range(KD):
                        last = nc.tensor.matmul(bank[6][:, c:c + 2], w[:, k, t * P:(t + 1) * P], cs[:, k, :],
                                                start=(k == 0), stop=(k == KD - 1))
                last.then_inc(used, 1)

            pe.wait_ge(silu_c, 1)
            for half in range(4):
                mod_half(half, half)

            def bank_free(prod, n, sa, sd):
                if n >= 4:
                    e, count = copied(prod, n - 4)
                    pe.wait_ge(sa if e == "A" else sd, count)

            def latent_sums():
                pe.wait_ge(lat_sq, 1)
                for k in range(3):
                    last = nc.tensor.matmul(bank[4][:, 0:T], ones, attf[:, k * T:(k + 1) * T],
                                            start=(k == 0), stop=(k == 2))
                last.then_inc(lat_ss, 1)
                for k in range(2):
                    last = nc.tensor.matmul(bank[5][:, :], ones, attf[:, 768 + 512 * k:1280 + 512 * k],
                                            start=(k == 0), stop=(k == 1))
                last.then_inc(lat_ss, 1)

            pe.wait_ge(shifted[0], 2 * KD)
            loads = {"ql": L_QL, "kvl": L_KVL, "kr": L_KVL, "naq": L_NAQ, "nak": L_NAK, "nav": L_NAV,
                     "uq": L_UQ, "kn": L_UKV, "vm": L_UKV}
            lastuse = {"ql": 2, "kr": 0, "naq": 3, "nak": 3, "nav": 3, "uq": 7, "vm": 3}
            for n, (kind, i, _e) in enumerate(PROD):
                if n == N_BEFORE_LAT:
                    latent_sums()
                bank_free(PROD, n, prod_a, prod_d)
                dst = bank[n % 4]
                if kind in loads and i == 0:
                    arrive(loads[kind])
                if kind == "ql":
                    w = ring[:, slot_of(L_QL), 0:KD * QL].rearrange("p (k n) -> p k n", k=KD)
                    for k in range(KD):
                        last = nc.tensor.matmul(dst[:, 0:T], w[:, k, i * P:(i + 1) * P], hT[:, k, 0:T],
                                                start=(k == 0), stop=(k == KD - 1))
                elif kind in ("kvl", "kr"):
                    w = ring[:, slot_of(L_KVL), 0:KD * 288].rearrange("p (k n) -> p k n", k=KD)
                    lo, m = (i * P, P) if kind == "kvl" else (192, QK)
                    for k in range(KD):
                        last = nc.tensor.matmul(dst[0:m, :], w[:, k, lo:lo + m], hT[:, k, :],
                                                start=(k == 0), stop=(k == KD - 1))
                elif kind in ("naq", "nak"):
                    w = slot(loads[kind], KD)
                    cols = T if kind == "naq" else 2 * T
                    for k in range(KD):
                        last = nc.tensor.matmul(dst[:, 0:cols], w[:, k, i * P:(i + 1) * P], hT[:, k, 0:cols],
                                                start=(k == 0), stop=(k == KD - 1))
                elif kind == "nav":
                    w = slot(L_NAV, KD)
                    for k in range(KD):
                        last = nc.tensor.matmul(dst[:, :], hT[:, k, i * P:(i + 1) * P], w[:, k, :],
                                                start=(k == 0), stop=(k == KD - 1))
                elif kind == "uq":
                    if i == 0:
                        pe.wait_ge(lat_done, 5)
                        pe.wait_ge(prod_ready, n)
                    w = ring[:, slot_of(L_UQ), 0:2304].rearrange("p (k n) -> p k n", k=3)
                    for k in range(3):
                        last = nc.tensor.matmul(dst[0:QK, 0:T], w[:, k, i * QK:(i + 1) * QK], qlat[:, k, :],
                                                start=(k == 0), stop=(k == 2))
                elif kind == "kn":
                    w = ring[:, slot_of(L_UKV), 0:2048].rearrange("p (k n) -> p k n", k=2)
                    for k in range(2):
                        last = nc.tensor.matmul(dst[0:NOPE, :], w[:, k, i * P:i * P + NOPE], kvlat[:, k, :],
                                                start=(k == 0), stop=(k == 1))
                elif kind == "vm":
                    w = ring[:, slot_of(L_UKV), 0:2048].rearrange("p (k h n) -> p k h n", k=2, h=H)
                    for k in range(2):
                        last = nc.tensor.matmul(dst[:, :], kvlat[:, k, i * P:(i + 1) * P], w[:, k, :, NOPE:P],
                                                start=(k == 0), stop=(k == 1))
                elif kind == "rotk":
                    pe.wait_ge(prod_d, copied(PROD, 5)[1])
                    last = nc.tensor.matmul(dst[64:96, :], rot, kr, start=True, stop=True)
                elif kind == "rotq":
                    if i == 0:
                        pe.wait_ge(prod_a, copied(PROD, 24)[1])
                        pe.wait_ge(prod_d, copied(PROD, 25)[1])
                    last = nc.tensor.matmul(dst[64:96, :], rot, qT[64:96, 2 * i:2 * i + 2, :], start=True, stop=True)
                last.then_inc(prod_ready, 1)
                if lastuse.get(kind) == i:
                    pe.wait_ge(prod_ready, n + 1)
                    pe.sem_inc(used, 1)

            def scores(units, A, s):
                a, h, q, nk = units[s]
                if s >= 2:
                    pe.wait_ge(A["exped"], s - 1)
                lo = 64 * (h % 2)
                if a == 0:
                    lhs, rhs = qT[:, h, q * P:(q + 1) * P], kT[:, h, :]
                elif a == 1:
                    lhs, rhs = naq[lo:lo + 64, h // 2, q * P:(q + 1) * P], nak[lo:lo + 64, h // 2, :]
                else:
                    lhs, rhs = q2[lo:lo + 64, h // 2, q * P:(q + 1) * P], k2[lo:lo + 64, h // 2, 0:nk * P]
                nc.tensor.matmul(bank[s % 2][:, 0:nk * P], lhs, rhs, start=True, stop=True).then_inc(A["scores"], 1)

            def turns(units, A, s):
                nk = units[s][3]
                pe.wait_ge(A["exped"], s + 1)
                if s >= 2:
                    pe.wait_ge(A["pta" if s % 2 else "ptd"], s // 2)
                for j in range(nk):
                    last = nc.tensor.transpose(bank[2 + s % 2][:, j * P:(j + 1) * P], att[:, s % 2, j * P:(j + 1) * P],
                                               ident)
                last.then_inc(A["turned"], 1)

            def values(units, A, s):
                a, h, q, nk = units[s]
                v = (vm, nav, v2)[a]
                pe.wait_ge(A["pta" if s % 2 else "ptd"], s // 2 + 1)
                if a == 1 and h == 0 and q == 0:
                    pe.wait_ge(o_out, NT)
                for j in range(nk):
                    last = nc.tensor.matmul(bank[4 + q][:, h * HD:(h + 1) * HD], att[:, 2 + s % 2, j * P:(j + 1) * P],
                                            v[:, j, h * HD:(h + 1) * HD], start=(j == 0), stop=(j == nk - 1))
                last.then_inc(A["pv"], 1)

            def attention(units, A, between):
                for s in range(len(units) + 2):
                    if s < len(units):
                        scores(units, A, s)
                    if 1 <= s <= len(units):
                        turns(units, A, s - 1)
                    if s >= 2:
                        values(units, A, s - 2)
                    between(s)

            pe.wait_ge(prod_a, total(PROD, "A"))
            pe.wait_ge(prod_d, total(PROD, "D"))
            pe.wait_ge(kr_spread, 1)

            def rest_of_mod(s):
                if s % 4 == 3 and s // 4 < 8:
                    mod_half(4 + s // 4, L_MOD2 + s // 4)

            attention(UNITS, ATT[0], rest_of_mod)

            def turn_mixed(turned):
                for c in range(KD):
                    for q in range(NT):
                        last = nc.tensor.transpose(bank[c // 2][:, (c % 2) * T + q * P:(c % 2) * T + (q + 1) * P],
                                                   osb[:, q, c * P:(c + 1) * P], ident)
                    if c % 2:
                        last.then_inc(turned, 1)

            pe.wait_ge(o_out, 2 * NT)
            turn_mixed(mix_t)

            def out_projection(load, a, d, ready, freed):
                pe.wait_ge(a, 2)
                pe.wait_ge(d, 2)
                for m in range(KD):
                    if m % 4 == 0:
                        arrive(load + m // 4)
                    w = slot(load + m // 4, KD)
                    if m >= 4:
                        pe.wait_ge(freed, m - 3)
                    for k in range(KD):
                        last = nc.tensor.matmul(bank[m % 4][:, 0:T], w[:, k, (m % 4) * P:(m % 4 + 1) * P],
                                                mixT[:, k, :], start=(k == 0), stop=(k == KD - 1))
                    last.then_inc(ready, 1)
                    if m % 4 == 3:
                        pe.wait_ge(ready, m + 1)
                        pe.sem_inc(used, 1)

            out_projection(L_OUT, mix_a, mix_d, proj_out, resid)

            def norm_sum(r):
                for k in range(KD):
                    pe.wait_ge(squares[r], k + 1)
                    last = nc.tensor.matmul(bank[NORM_BANK[r]][:, 0:T], ones, sq[:, k, :],
                                            start=(k == 0), stop=(k == KD - 1))
                last.then_inc(sumsq[r], 1)

            norm_sum(1)
            pe.wait_ge(in_row, 48)
            pe.wait_ge(shifted[1], KD)
            for q in range(NT):
                for k in range(KD):
                    last = nc.tensor.matmul(bank[6][:, 128 + 20 * q:148 + 20 * q], h2[:, k, q * P:(q + 1) * P],
                                            wr[:, k, :], start=(k == 0), stop=(k == KD - 1))
            last.then_inc(logits, 1)
            pe.wait_ge(comb_done, 1)
            comb = small[:, 15, :].rearrange("p (q e) -> p q e", q=NT)
            for j in range(8):
                if j >= 4:
                    pe.wait_ge(gu_free, j - 3)
                for e in range(2):
                    for q in range(NT):
                        last = nc.tensor.matmul(bank[j % 4][:, e * T + q * P:e * T + (q + 1) * P],
                                                comb[:, q, 2 * j + e:2 * j + e + 1].broadcast_to([P, P]), ident,
                                                start=True, stop=True)
                last.then_inc(comb_t, 1)
            pe.wait_ge(var[1], 1)
            for b in range(4):
                nc.tensor.matmul(bank[4 + b][:, :], zeros[:, :], con[:, 0:512], start=True, stop=False,
                                 skip_group_check=True)
            with pe.Fori(0, NE // 2) as i:
                for e in range(2):
                    n = L_MOE + 3 * e
                    w = [ring[:, slot_of(n + j), :].rearrange("p (k n) -> p k n", k=KD if j < 2 else 4)
                         for j in range(3)]
                    pe.wait_ge(landed[slot_of(n)], i * 16 + landed_count(n))
                    pe.wait_ge(landed[slot_of(n + 1)], i * 16 + landed_count(n + 1))
                    for f in range(4):
                        pe.wait_ge(gu_free, i * 8 + (4 * e + f + 5))
                        for j in range(2):
                            for k in range(KD):
                                last = nc.tensor.matmul(bank[f][:, j * T:(j + 1) * T], w[j][:, k, f * P:(f + 1) * P],
                                                        h2[:, k, :], start=(k == 0), stop=(k == KD - 1))
                            if j == 0 and f == 3:
                                last.then_inc(used, 1)
                        last.then_inc(gu, 1)
                    pe.wait_ge(landed[slot_of(n + 2)], i * 16 + landed_count(n + 2))
                    for f in range(4):
                        pe.wait_ge(gu_free, i * 8 + (8 + 4 * e + f + 1))
                        for m in range(KD):
                            last = nc.tensor.matmul(yacc(m), w[2][:, f, m * P:(m + 1) * P], hidM[:, e, f, :],
                                                    start=False, stop=False, skip_group_check=True)
                            if f == 0 and m == 0:
                                last.then_inc(used, 1)
                    last.then_inc(used, 1)
            norm_sum(2)
            norm_sum(3)

            loads2 = {"u": L_IN2, "va": L_IN2 + 1, "q": L_IN2 + 2, "k": L_IN2 + 3, "v": L_IN2 + 4}
            lf = small[:, 2, 0:16].rearrange("p (q h) -> p q h", q=NT)
            for n, (kind, i, _e) in enumerate(PROD2):
                bank_free(PROD2, n, prod2_a, prod2_d)
                dst = bank[n % 4]
                if kind in loads2 and i == 0:
                    arrive(loads2[kind])
                if kind == "f":
                    for k in range(KD):
                        pe.wait_ge(normed[3], k + 1)
                    for q in range(NT):
                        for k in range(KD):
                            last = nc.tensor.matmul(dst[:, 8 * q:8 * q + 8], h2[:, k, q * P:(q + 1) * P], wf[:, k, :],
                                                    start=(k == 0), stop=(k == KD - 1))
                elif kind in ("u", "va", "v"):
                    w = slot(loads2[kind], KD)
                    for k in range(KD):
                        last = nc.tensor.matmul(dst[:, :], h2[:, k, i * P:(i + 1) * P], w[:, k, :],
                                                start=(k == 0), stop=(k == KD - 1))
                elif kind in ("q", "k"):
                    w = slot(loads2[kind], KD)
                    for k in range(KD):
                        last = nc.tensor.matmul(dst[:, 0:T], w[:, k, i * P:(i + 1) * P], h2[:, k, :],
                                                start=(k == 0), stop=(k == KD - 1))
                elif kind == "cq":
                    pe.wait_ge(lf_done, 1)
                    nc.tensor.matmul(dst[:, 0:8], upper, lf[:, 0, :], start=True, stop=True)
                    nc.tensor.matmul(dst[:, 8:16], ones, lf[:, 0, :], start=True, stop=False)
                    last = nc.tensor.matmul(dst[:, 8:16], upper, lf[:, 1, :], start=False, stop=True)
                elif kind == "nck":
                    for j in range(2):
                        h = 2 * i + j
                        nc.tensor.matmul(dst[:, j * T:(j + 1) * T], lf[:, 0, h:h + 1].broadcast_to([P, P]),
                                         upper_ones, start=True, stop=False)
                        last = nc.tensor.matmul(dst[:, j * T + P:(j + 1) * T], lf[:, 1, h:h + 1].broadcast_to([P, P]),
                                                upper, start=False, stop=True)
                last.then_inc(prod2_ready, 1)
                if {"u": 1, "va": 1, "q": 3, "k": 3, "v": 1}.get(kind) == i:
                    pe.wait_ge(prod2_ready, n + 1)
                    pe.sem_inc(used, 1)
            pe.wait_ge(vn_done, 1)
            pe.wait_ge(sg_zero, 1)
            for q in range(NT):
                for h in range(H):
                    last = nc.tensor.matmul(bank[6 + q][:, h * HD:(h + 1) * HD], sgw[:, h, :],
                                            vg[:, q, h * HD:(h + 1) * HD], start=True, stop=True)
                last.then_inc(sg_mm, 1)
            pe.wait_ge(prod2_a, total(PROD2, "A"))
            pe.wait_ge(prod2_d, total(PROD2, "D"))
            attention(UNITS2, ATT[1], lambda s: None)
            pe.wait_ge(o2_out, NT)
            pe.wait_ge(sg_done, NT)
            turn_mixed(mix2_t)
            out_projection(L_OUT2, mix2_a, mix2_d, proj2_out, resid2)
            norm_sum(4)

            pe.wait_ge(normed[4], KD)

            def up_pairs(i, n, count, first):
                w = ring[:, slot_of(n), :].rearrange("p (k g n) -> p k g n", k=KD, g=2)
                base = 2 * ((n - L_UP) % 2) if n < L_UP + N_UP - 1 else 0
                for j in range(base, base + count):
                    if not first:
                        pe.wait_ge(tap2, i * 8 + (2 * j - 6))
                    for g in range(2):
                        for k in range(KD):
                            last = nc.tensor.matmul(bank[j][:, g * T:(g + 1) * T],
                                                    w[:, k, g, (j - base) * P:(j - base + 1) * P], h2[:, k, :],
                                                    start=(k == 0), stop=(k == KD - 1))
                    last.then_inc(up_ready, 1)
                pe.wait_ge(up_ready, i * 4 + (base + count))
                pe.sem_inc(used, 1)

            for e in range(2):
                arrive(L_UP + e)
                up_pairs(0, L_UP + e, 2, True)
            with pe.Fori(1, (N_UP - 1) // 2) as i:
                for e in range(2):
                    pe.wait_ge(landed[slot_of(L_UP + e)], i * 32 + landed_count(L_UP + e))
                    up_pairs(i, L_UP + e, 2, False)
            arrive(L_UP + N_UP - 1)
            up_pairs((N_UP - 1) // 2, L_UP + N_UP - 1, 2, False)
            pe.wait_ge(resid2, KD)
            for kt in range(NP):
                n = L_DOWN + kt // 4
                if kt % 4 == 0:
                    arrive(n)
                k_in = min(4, NP - 4 * (kt // 4))
                w = ring[:, slot_of(n), 0:k_in * D].rearrange("p (k n) -> p k n", k=k_in)
                pe.wait_ge(hid_done, kt + 1)
                for m in range(KD):
                    last = nc.tensor.matmul(yacc(m), w[:, kt % 4, m * P:(m + 1) * P], hidF[:, kt, :],
                                            start=(kt == 0 and m % 2 == 0), stop=(kt == NP - 1),
                                            skip_group_check=True)
            last.then_inc(down_done, 1)
            norm_sum(5)

        @block.vector
        def _(dve):
            steps = [0]

            def link(ins):
                steps[0] += 1
                ins.then_inc(vstep, 1)
                dve.wait_ge(vstep, steps[0])

            V = nc.vector

            def bc(ap, axis, shape):
                return ap.unsqueeze(axis).broadcast_to(shape)

            V.memset(zeros[:, :], 0.0).then_inc(vstep, 1)
            steps[0] += 1
            dve.wait_ge(sumsq[0], 1)
            V.tensor_scalar(rstd[:, :], bank[7][:, :], 1.0 / D, EPS, ALU.mult, ALU.add).then_inc(var[0], 1)
            dve.wait_ge(std[0], 1)
            link(V.reciprocal(rstd[:, :], rstd[:, :]))
            dve.wait_ge(used, 4)
            dve.wait_ge(in_vec, 16)
            link(V.tensor_tensor(mod[:, 0:16, :], bank[6][:, 0:32].rearrange("p (n c) -> p n c", c=2),
                                 bc(v_("b_mod", 0, 16), 2, [P, 16, 2]), ALU.add))
            link(V.scalar_tensor_tensor(A1[:, :, :], mod[:, 8:16, :], 1.0, bc(v_("g_attn", 0, 8), 2, [P, 8, 2]),
                                        ALU.add, ALU.mult))
            for k in range(KD):
                for s, src in enumerate((xT[:, k, :], ctxT[:, k, :])):
                    V.scalar_tensor_tensor(hT[:, k, s * T:(s + 1) * T], src, A1[:, k, s:s + 1],
                                           rstd[:, s * T:(s + 1) * T], ALU.mult, ALU.mult).then_inc(normed[0], 1)

            def rotate(q, r, tmp, c, s):
                link(V.tensor_tensor(tmp, r, s, ALU.mult))
                link(V.tensor_tensor(q, q, c, ALU.mult))
                return V.tensor_tensor(q, q, tmp, ALU.add)

            def out_of_psum(n):
                kind, i, e = PROD[n]
                src = bank[n % 4]
                dve.wait_ge(prod_ready, n + 1)
                if kind == "ql":
                    ins = V.tensor_copy(qlat[:, i, :], src[:, 0:T])
                elif kind == "kvl":
                    ins = V.tensor_copy(kvlat[:, i, :], src[:, :])
                elif kind == "kr":
                    ins = V.tensor_copy(kr, src[64:96, :])
                elif kind == "naq":
                    ins = V.tensor_scalar(naq[:, i, :], src[:, 0:T], HD ** -0.5, None, ALU.mult)
                elif kind == "nak":
                    ins = V.tensor_copy(nak[:, i, :], src[:, :])
                elif kind == "nav":
                    ins = V.tensor_copy(nav[:, i, :], src[:, :])
                elif kind == "uq":
                    ins = V.tensor_scalar(qT[:, i, :], src[0:QK, 0:T], QK ** -0.5, None, ALU.mult)
                elif kind == "kn":
                    ins = V.tensor_copy(kT[0:NOPE, i, :], src[0:NOPE, :])
                elif kind == "vm":
                    ins = V.tensor_copy(vm[:, i, :], src[:, :])
                elif kind == "rotk":
                    ins = rotate(kr, src[64:96, :], rtmp, cos, sin)
                elif kind == "rotq":
                    q = qT[64:96, 2 * i:2 * i + 2, :]
                    ins = rotate(q, src[64:96, :].rearrange("p (a t) -> p a t", a=2),
                                 rtmp.rearrange("p (a t) -> p a t", a=2),
                                 bc(cos[:, 0:T], 1, [32, 2, T]), bc(sin[:, 0:T], 1, [32, 2, T]))
                ins.then_inc(prod_d, 1)
                if kind == "rotk":
                    dve.wait_ge(prod_d, copied(PROD, n)[1])
                    dve.sem_inc(kr_done, 1)
                if kind == "rotq" or kind == "rotk":
                    dve.wait_ge(prod_d, copied(PROD, n)[1])

            for n, (kind, i, e) in enumerate(PROD):
                if n == N_BEFORE_LAT:
                    dve.wait_ge(lat_ss, 2)
                    V.tensor_scalar(rq, bank[4][:, 0:T], 1.0 / QL, EPS, ALU.mult, ALU.add).then_inc(lat_var, 1)
                    V.tensor_scalar(rkv, bank[5][:, :], 1.0 / KVL, EPS, ALU.mult, ALU.add).then_inc(lat_var, 1)
                    dve.wait_ge(lat_std, 2)
                    link(V.reciprocal(rq, rq))
                    link(V.reciprocal(rkv, rkv))
                    dve.wait_ge(prod_a, copied(PROD, 4)[1])
                    for k in range(3):
                        V.scalar_tensor_tensor(qlat[:, k, :], qlat[:, k, :], v_("g_qa", k), rq, ALU.mult, ALU.mult
                                               ).then_inc(lat_done, 1)
                    for k in range(2):
                        V.scalar_tensor_tensor(kvlat[:, k, :], kvlat[:, k, :], v_("g_kva", k), rkv, ALU.mult, ALU.mult
                                               ).then_inc(lat_done, 1)
                if e == "D":
                    out_of_psum(n)

            def maxes(units, A, s):
                a, h, q, nk = units[s]
                u = 16 * a + 8 * q + h
                S = bank[s % 2]
                dve.wait_ge(A["scores"], s + 1)
                if a == 1:
                    if q == 0 and h % 4 == 0:
                        dve.wait_ge(bias_ready, h // 4 + 1)
                    link(V.tensor_tensor(S[:, 0:T], S[:, 0:T], bias[:, h, q, :], ALU.add))
                if a == 2:
                    if s == 0:
                        dve.wait_ge(nck_done, 2)
                    key = nck0[:, h, :] if q == 0 else nck[:, h, :]
                    link(V.scalar_tensor_tensor(S[:, 0:nk * P], S[:, 0:nk * P], cq[:, 8 * q + h:8 * q + h + 1], key,
                                                ALU.add, ALU.add))
                V.tensor_reduce(nmax[:, u:u + 1], S[:, 0:nk * P], AX, ALU.max, negate=True).then_inc(A["maxed"], 1)

            def turn_copy(units, A, s):
                w = units[s][3] * P
                dve.wait_ge(A["turned"], s + 1)
                if s >= 2:
                    dve.wait_ge(A["pv"], s - 1)
                V.tensor_copy(att[:, 2, 0:w], bank[2][:, 0:w]).then_inc(A["ptd"], 1)

            def outputs(units, A, s, a, at, done):
                dve.wait_ge(A["pv"], s)
                dve.wait_ge(A["exped"], s)
                link(V.reciprocal(rinv[:, 16 * a:16 * a + 16], rsum[:, 16 * a:16 * a + 16]))
                for q in range(NT):
                    V.tensor_tensor(osb[:, q, at:at + 512].rearrange("p (h d) -> p h d", h=H),
                                    bank[4 + q][:, :].rearrange("p (h d) -> p h d", h=H),
                                    bc(rinv[:, 16 * a + 8 * q:16 * a + 8 * q + 8], 2, [P, H, HD]),
                                    ALU.mult).then_inc(done, 1)

            cq = small[:, 3, 0:16]
            for s in range(len(UNITS) + 1):
                if s < len(UNITS):
                    maxes(UNITS, ATT[0], s)
                if s >= 1 and (s - 1) % 2 == 0:
                    turn_copy(UNITS, ATT[0], s - 1)
                if s == 17:
                    outputs(UNITS, ATT[0], 16, 0, 0, o_out)
            outputs(UNITS, ATT[0], 32, 1, 512, o_out)

            def mix_copy(ready, done):
                for c in (1, 3):
                    dve.wait_ge(ready, c + 1)
                    V.tensor_copy(mixT[:, 2 * c:2 * c + 2, :].rearrange("p a t -> p (a t)"), bank[c][:, :]
                                  ).then_inc(done, 1)

            dve.wait_ge(used, L_MOD2 + 8)
            link(V.tensor_tensor(mod[:, 16:48, :], bank[6][:, 32:96].rearrange("p (n c) -> p n c", c=2),
                                 bc(v_("b_mod", 16, 32), 2, [P, 32, 2]), ALU.add))
            link(V.scalar_tensor_tensor(A2[:, :], mod[:, 32:40, 0], 1.0, v_("g_ffn", 0, 8), ALU.add, ALU.mult))
            mix_copy(mix_t, mix_d)
            for m in range(KD):
                dve.wait_ge(proj_out, m + 1)
                V.scalar_tensor_tensor(xT[:, m, :], bank[m % 4][:, 0:T], mod[:, 16 + m, 0:1], xT[:, m, :],
                                       ALU.mult, ALU.add).then_inc(resid, 1)

            def norm(r, gain, dst, updated):
                dve.wait_ge(sumsq[r], 1)
                V.tensor_scalar(rstd[:, 0:T], bank[NORM_BANK[r]][:, 0:T], 1.0 / D, EPS, ALU.mult, ALU.add
                                ).then_inc(var[r], 1)
                dve.wait_ge(std[r], 1)
                link(V.reciprocal(rstd[:, 0:T], rstd[:, 0:T]))
                dve.wait_ge(updated, KD)
                for k in range(KD):
                    V.scalar_tensor_tensor(dst[:, k, :], xT[:, k, :], gain(k), rstd[:, 0:T], ALU.mult, ALU.mult
                                           ).then_inc(normed[r], 1)

            norm(1, lambda k: A2[:, k:k + 1], h2, resid)

            S_ = small

            def t3(i, n=4):
                return S_[:, i, 0:2 * n].rearrange("p (q n) -> p q n", q=NT)

            def top(values, scratch, onehot):
                link(V.tensor_reduce(S_[:, 8, 0:2], values, AX, ALU.max))
                link(V.tensor_tensor(scratch, values, bc(S_[:, 8, 0:2], 2, [P, NT, 4]), ALU.is_equal))
                link(V.tensor_tensor(scratch, scratch, bc(desc, 1, [P, NT, 4]), ALU.mult))
                link(V.tensor_reduce(S_[:, 9, 0:2], scratch, AX, ALU.max))
                link(V.tensor_tensor(onehot, scratch, bc(S_[:, 9, 0:2], 2, [P, NT, 4]), ALU.is_equal))

            dve.wait_ge(logits, 1)
            dve.wait_ge(in_row, 48)
            L = small[:, 10:12, 0:20]
            link(V.tensor_tensor(L, bank[6][:, 128:168].rearrange("p (q n) -> p q n", q=NT),
                                 bc(row[:, ROW["b_router"]:ROW["b_router"] + 20], 1, [P, NT, 20]), ALU.add))
            G, E = L[:, :, 0:4], L[:, :, 4:20].rearrange("p q (g e) -> p q g e", g=NG)
            top(G, t3(2), t3(3))
            V.tensor_tensor(t3(1), G, bc(S_[:, 8, 0:2], 2, [P, NT, 4]), ALU.subtract).then_inc(gdiff, 1)
            wide = small[:, 12:14, 0:16].rearrange("p q (g e) -> p q g e", g=NG)
            for q in range(NT):
                link(V.tensor_tensor(wide[:, q], E[:, q], bc(t3(3)[:, q, :], 2, [P, NG, EG]), ALU.mult))
                link(V.tensor_reduce(t3(4)[:, q, :], wide[:, q].rearrange("p g e -> p e g"), AX, ALU.add))
            link(V.tensor_reduce(S_[:, 6, 0:2], t3(4), AX, ALU.max))
            V.tensor_tensor(t3(5), t3(4), bc(S_[:, 6, 0:2], 2, [P, NT, 4]), ALU.subtract).then_inc(ediff, 1)
            dve.wait_ge(gexp, 1)
            link(V.tensor_reduce(S_[:, 7, 0:2], t3(1), AX, ALU.add))
            link(V.reciprocal(S_[:, 7, 0:2], S_[:, 7, 0:2]))
            dve.wait_ge(eexp, 1)
            link(V.tensor_reduce(S_[:, 6, 0:2], t3(5), AX, ALU.add))
            link(V.reciprocal(S_[:, 6, 0:2], S_[:, 6, 0:2]))
            link(V.tensor_tensor(t3(5), t3(5), bc(S_[:, 6, 0:2], 2, [P, NT, 4]), ALU.mult))
            top(t3(5), t3(2), t3(4))
            link(V.scalar_tensor_tensor(t3(1), t3(4), -2.0, t3(5), ALU.mult, ALU.add))
            top(t3(1), t3(2), t3(0))
            link(V.tensor_tensor(t3(4), t3(4), t3(0), ALU.add))
            link(V.tensor_tensor(t3(4), t3(4), t3(5), ALU.mult))
            link(V.tensor_reduce(S_[:, 6, 0:2], t3(4), AX, ALU.add))
            link(V.reciprocal(S_[:, 6, 0:2], S_[:, 6, 0:2]))
            link(V.tensor_tensor(t3(4), t3(4), bc(S_[:, 6, 0:2], 2, [P, NT, 4]), ALU.mult))
            link(V.tensor_tensor(t3(4), t3(4), bc(S_[:, 7, 0:2], 2, [P, NT, 4]), ALU.mult))
            comb = small[:, 15, :].rearrange("p (q g e) -> p q g e", q=NT, g=NG)
            for q in range(NT):
                ins = V.tensor_tensor(comb[:, q], bc(t3(3)[:, q, :], 2, [P, NG, EG]),
                                      bc(t3(4)[:, q, :], 1, [P, NG, EG]), ALU.mult)
                if q == 0:
                    link(ins)
            ins.then_inc(comb_done, 1)
            for j in range(8):
                dve.wait_ge(comb_t, j + 1)
                V.tensor_copy(comb_b[:, 2 * j:2 * j + 2, :].rearrange("p a t -> p (a t)"), bank[j % 4][:, :]
                              ).then_inc(gu_free, 1)
            dve.wait_ge(gu_free, 8)
            with dve.Fori(0, NE // 2) as i:
                for e in range(2):
                    dve.wait_ge(used, i * 6 + (L_MOE + 3 * e - 3))
                    for f in range(4):
                        n = 4 * e + f
                        dve.wait_ge(silu_g, i * 8 + (n + 1))
                        V.tensor_tensor(gsb[:, f % 2, :], gsb[:, f % 2, :], bank[f][:, T:2 * T], ALU.mult
                                        ).then_inc(gated, 1)
                        dve.wait_ge(gated, i * 8 + (n + 1))
                        V.tensor_tensor(hidM[:, e, f, :], gsb[:, f % 2, :], comb_b[:, i * 2 + e, :], ALU.mult
                                        ).then_inc(gu_free, 1)
            dve.wait_ge(used, L_MOE + 3 * NE)
            for m in range(KD):
                V.scalar_tensor_tensor(xT[:, m, :], yacc(m), mod[:, 40 + m, 0:1], xT[:, m, :], ALU.mult, ALU.add
                                       ).then_inc(resid_m, 1)
            norm(2, lambda k: v_("g_final", k), xT, resid_m)
            norm(3, lambda k: v_("g_mix2", k), h2, normed[2])

            f2, fa, lfr = small[:, 0, 0:16], small[:, 1, 0:16], small[:, 2, 0:16]

            def out_of_psum2(n):
                kind, i, e = PROD2[n]
                src = bank[n % 4]
                dve.wait_ge(prod2_ready, n + 1)
                if kind == "f":
                    V.tensor_tensor(f2.rearrange("p (q h) -> p q h", q=NT),
                                    src[:, 0:16].rearrange("p (q h) -> p q h", q=NT),
                                    bc(row[:, ROW["f_bias"]:ROW["f_bias"] + 8], 1, [P, NT, 8]), ALU.add
                                    ).then_inc(prod2_d, 1)
                    dve.wait_ge(prod2_d, 1)
                    V.scalar_tensor_tensor(fa, f2, -1.0, f2, ALU.mult, ALU.min).then_inc(f_abs, 1)
                    link(V.tensor_scalar(f2, f2, 0.0, None, ALU.min))
                    dve.wait_ge(f_ln, 1)
                    V.tensor_tensor(lfr, f2, fa, ALU.subtract).then_inc(lf_done, 1)
                    return
                if kind == "q":
                    ins = V.tensor_scalar(q2[:, i, :], src[:, 0:T], HD ** -0.5, None, ALU.mult)
                elif kind == "k":
                    ins = V.tensor_copy(k2[:, i, :], src[:, 0:T])
                elif kind == "cq":
                    ins = V.tensor_copy(cq, src[:, 0:16])
                ins.then_inc(prod2_d, 1)

            def heads(t):
                return t.rearrange("p (h d) -> p h d", h=H)

            def layer_norm():
                dve.wait_ge(prod2_a, 4)
                mu, vr = small[:, 5, 0:16], small[:, 6, 0:16]
                v3 = vg[:, :, :].rearrange("p n (h d) -> p (n h) d", h=H)
                l3 = lnt[:, :, :].rearrange("p n (h d) -> p (n h) d", h=H)
                link(V.tensor_reduce(mu, v3, AX, ALU.add))
                link(V.tensor_scalar(mu, mu, 1.0 / HD, None, ALU.mult))
                link(V.tensor_tensor(v3, v3, bc(mu, 2, [P, 16, HD]), ALU.subtract))
                link(V.tensor_tensor(l3, v3, v3, ALU.mult))
                link(V.tensor_reduce(vr, l3, AX, ALU.add))
                V.tensor_scalar(vr, vr, 1.0 / HD, EPS, ALU.mult, ALU.add).then_inc(ln_var, 1)

            def layer_norm_end():
                vr = small[:, 6, 0:16]
                v3 = vg[:, :, :].rearrange("p n (h d) -> p (n h) d", h=H)
                dve.wait_ge(ln_std, 1)
                link(V.reciprocal(vr, vr))
                link(V.tensor_tensor(v3, v3, bc(vr, 2, [P, 16, HD]), ALU.mult))
                V.tensor_tensor(vg[:, :, :], vg[:, :, :], bc(row[:, ROW["sg_ln"]:ROW["sg_ln"] + 512], 1, [P, NT, 512]),
                                ALU.mult).then_inc(vn_done, 1)

            for n, (kind, i, e) in enumerate(PROD2):
                if kind == "k" and i == 0:
                    layer_norm()
                if e == "D":
                    out_of_psum2(n)
            layer_norm_end()
            for q in range(NT):
                dve.wait_ge(sg_mm, q + 1)
                link(V.tensor_tensor(heads(osb[:, q, 0:512]), heads(bank[6 + q][:, :]),
                                     bc(v_("sg_b", 0, 8), 2, [P, H, HD]), ALU.add))
                V.tensor_tensor(osb[:, q, 0:512], osb[:, q, 0:512], ug[:, q, :], ALU.mult).then_inc(sg_done, 1)
            dve.wait_ge(prod2_d, total(PROD2, "D"))
            for s in range(len(UNITS2) + 1):
                if s < len(UNITS2):
                    maxes(UNITS2, ATT[1], s)
                if s >= 1 and (s - 1) % 2 == 0:
                    turn_copy(UNITS2, ATT[1], s - 1)
            outputs(UNITS2, ATT[1], 16, 2, 512, o2_out)
            mix_copy(mix2_t, mix2_d)
            for m in range(KD):
                dve.wait_ge(proj2_out, m + 1)
                V.tensor_tensor(xT[:, m, :], bank[m % 4][:, 0:T], xT[:, m, :], ALU.add).then_inc(resid2, 1)
            norm(4, lambda k: v_("g_ffn2", k), h2, resid2)

            def taps(i, j):
                b = j % 2
                dve.wait_ge(conv0, i * 8 + (2 * j + 2))
                for g in range(2):
                    y, a = yconv[:, b, g, :], bank[j % 4][:, g * T:(g + 1) * T]
                    V.scalar_tensor_tensor(y[:, 1:T], a[:, 0:T - 1],
                                           vec[:, bass.ds(i * 4 + (j + 22 * g + VEC["w_conv"] + 44), 1)], y[:, 1:T],
                                           ALU.mult, ALU.add).then_inc(tap1, 1)
                for g in range(2):
                    y, a = yconv[:, b, g, :], bank[j % 4][:, g * T:(g + 1) * T]
                    dve.wait_ge(tap1, i * 8 + (2 * j + g + 1))
                    V.scalar_tensor_tensor(y[:, 2:T], a[:, 0:T - 2],
                                           vec[:, bass.ds(i * 4 + (j + 22 * g + VEC["w_conv"]), 1)], y[:, 2:T],
                                           ALU.mult, ALU.add).then_inc(tap2, 1)
                dve.wait_ge(tap2, i * 8 + (2 * j + 2))
                dve.wait_ge(silu_f, i * 4 + (j + 1))
                V.tensor_tensor(hidF[:, i * 4 + j, :], yconv[:, b, 0, :], yconv[:, b, 1, :], ALU.mult
                                ).then_inc(hid_done, 1)

            with dve.Fori(0, NP // 4) as i:
                for j in range(4):
                    taps(i, j)
            for j in range(NP % 4):
                taps(NP // 4, j)
            dve.wait_ge(down_done, 1)
            for m in range(KD):
                V.tensor_tensor(xT[:, m, :], yacc(m), xT[:, m, :], ALU.add).then_inc(resid3, 1)
            norm(5, lambda k: v_("g_final2", k), outT, resid3)


def kernel(**inputs):
    import numpy as _np
    import concourse.bacc as _bacc
    from concourse import mybir as _mybir
    from concourse.bass_utils import run_bass_kernel_spmd as _run

    a = {k: _np.asarray(v) for k, v in inputs.items()}

    def tiles(v):
        return v.reshape(-1, P).T

    def featuremajor(x):
        return _np.ascontiguousarray(x.T.reshape(KD, P, T).transpose(1, 0, 2))

    vec = _np.concatenate([
        _np.stack([tiles(a["c"][0]), tiles(a["c_ctx"])], axis=2).reshape(P, 16), tiles(a["b_mod"][0]),
        tiles(a["norm_attn_g"][0]), tiles(a["norm_ffn_g"][0]), tiles(a["q_a_norm_g"][0]), tiles(a["kv_a_norm_g"][0]),
        tiles(a["final_norm_g"]), tiles(a["norm_mix_g_2"][0]), tiles(a["norm_ffn_g_2"][0]), tiles(a["b_conv_2"][0]),
        tiles(a["w_conv_2"][0].reshape(-1)), tiles(a["norm_final_g_2"]), a["sg_b_2"][0].T], axis=1)
    row = _np.concatenate([a["b_router_group"][0], a["b_router_expert"][0], a["f_bias_2"][0],
                           a["sg_ln_g_2"][0].reshape(-1)])[None]
    wr = _np.concatenate([a["w_router_group"][0], a["w_router_expert"][0]], axis=1).reshape(KD, P, 20)
    i, j = _np.arange(P)[:, None], _np.arange(P)[None]
    con = _np.zeros((P, NCON), _np.float32)
    con[:, CON["ident"]:CON["ident"] + P] = i == j
    con[:, CON["tri"]:CON["tri"] + P] = _np.where(j <= i, 0.0, -BIG)
    con[:, CON["upper"]:CON["upper"] + P] = i <= j
    con[:, CON["ones"]:CON["ones"] + P] = 1.0
    col, key = (i % GRID_W), _np.arange(GRID_W)[None]
    start = _np.clip(col - 8, 0, GRID_W - 16)
    con[:, CON["namask"]:CON["namask"] + GRID_W] = _np.where((key >= start) & (key < start + 16), 0.0, -BIG)
    r, m = _np.arange(32)[:, None], _np.arange(32)[None]
    con[64:96, CON["rot"]:CON["rot"] + 32] = _np.where(r == m + 16, -1.0, 0.0) + _np.where(r == m - 16, 1.0, 0.0)
    half = ROPE // 2
    inv = (_np.float32(10000.0) ** (-_np.arange(0, half, 2, dtype=_np.float32) / _np.float32(half))).astype(_np.float32)
    pos = _np.arange(T)
    ang = _np.concatenate([(pos // GRID_W).astype(_np.float32)[:, None] * inv,
                           (pos % GRID_W).astype(_np.float32)[:, None] * inv], axis=1).T
    con[64:96, CON["cos"]:CON["cos"] + 512] = 1.0
    con[64:96, CON["cos"]:CON["cos"] + T] = _np.tile(_np.cos(ang), (2, 1))
    con[64:96, CON["sin"]:CON["sin"] + T] = _np.tile(_np.sin(ang), (2, 1))
    con[:, CON["desc"]:CON["desc"] + 4] = [4.0, 3.0, 2.0, 1.0]
    q, k = _np.arange(T), _np.arange(T)
    dr = k[None] // GRID_W - q[:, None] // GRID_W + 7
    dc = _np.clip(k[None] % GRID_W - q[:, None] % GRID_W + 15, 0, 30)
    bias = a["na_rel_bias"][0][:, dr, dc].reshape(H, NT, P, T).transpose(2, 0, 1, 3).reshape(P, -1)

    feeds = {
        "xT": featuremajor(a["x"][0]), "ctxT": featuremajor(a["ctx"][0]), "vec": vec, "row": row, "con": con,
        "w_mod": a["w_mod"][0], "w_in": a["w_in"][0], "w_uq": a["w_uq"][0], "w_ukv": a["w_ukv"][0],
        "bias": bias, "w_out": a["w_out"][0], "wr": wr.transpose(1, 0, 2),
        "w_gate": a["w_gate"][0], "w_up": a["w_up"][0], "w_down": a["w_down"][0],
        "w_in2": a["w_in_2"][0], "wf": a["w_in_2"][0][:, 2560:].reshape(KD, P, 8).transpose(1, 0, 2),
        "sgw": a["sg_w_2"][0].transpose(2, 0, 1), "w_out2": a["w_out_2"][0],
        "w_up2": a["w_up_2"][0], "w_down2": a["w_down_2"][0],
    }
    nc = _bacc.Bacc("TRN2", target_bir_lowering=False, num_devices=1)
    arrays, args = {}, []
    for name, v in feeds.items():
        v = _np.ascontiguousarray(v)
        arrays[f"in_{name}"] = v
        args.append(nc.dram_tensor(f"in_{name}", v.shape, _mybir.dt.from_np(v.dtype), kind="ExternalInput").ap())
    args.append(nc.dram_tensor("out_T", (P, KD, T), F32, kind="ExternalOutput").ap())
    block_pair_kernel(nc, *args)
    got = _run(nc, [arrays], core_ids=[0]).results[0]["out_T"]
    return _np.ascontiguousarray(got.transpose(1, 0, 2).reshape(D, T).T)[None]
```

```python
from contextlib import ExitStack

import concourse.bass as bass
from concourse import mybir

P = 128
T = 256
D = 1024
KD = D // P
NT = T // P
H = 8
HD = 64
QK = 96
NOPE, ROPE = 64, 32
QL, KVL = 384, 256
GRID_W = 64
NE, NG, EG = 16, 4, 4
FE = 512
FF = 2816
NP = FF // P
EPS = 1e-6
BIG = 1e30

ALU = mybir.AluOpType
ACT = mybir.ActivationFunctionType
F32 = mybir.dt.float32
AX = mybir.AxisListType.X

SLOTS = 6
SLOT = 4096
CAP = 64
NPAIR = NE // 2
N_MOD = 12
L_QL, L_KVL, L_NAQ, L_NAK, L_NAV, L_UQ, L_UKV = range(4, 11)
L_MOD2 = 11
L_OUT = 19
L_MOE = 21
L_IN2 = L_MOE + 3 * NE
L_OUT2 = L_IN2 + 5
L_UP = L_OUT2 + 2
N_UP = NP // 2
L_DOWN = L_UP + N_UP
N_DOWN = (NP + 3) // 4
N_LOADS = L_DOWN + N_DOWN


def slot_of(n):
    if L_UP <= n < L_UP + N_UP - 1:
        return 4 + (n - L_UP) % 2
    if n == L_UP + N_UP - 1:
        return 0
    if n >= L_DOWN:
        return (n - L_DOWN + 1) % SLOTS
    return n % SLOTS


def last_in_slot(n):
    before = [m for m in range(n) if slot_of(m) == slot_of(n)]
    return before[-1] if before else None


def dmas_of(n):
    return 2 if L_UP <= n < L_DOWN else 1


def landed_count(n):
    first = L_IN2 if n >= L_IN2 else 0
    return 16 * sum(dmas_of(m) for m in range(first, n + 1) if slot_of(m) == slot_of(n))


def columns(widths):
    at, out = 0, {}
    for name, w in widths:
        out[name] = at
        at += w
    return out, at


VEC, NVEC = columns([("c", 16), ("b_mod", 48), ("g_attn", 8), ("g_ffn", 8), ("g_qa", 3), ("g_kva", 2),
                     ("g_final", 8), ("g_mix2", 8), ("g_ffn2", 8), ("b_conv", 44), ("w_conv", 132),
                     ("g_final2", 8), ("sg_b", 8)])
ROW, NROW = columns([("b_router", 20), ("f_bias", 8), ("sg_ln", 512)])
CON, NCON = columns([("ident", 128), ("tri", 128), ("upper", 128), ("ones", 128), ("namask", 64),
                     ("rot", 32), ("cos", 512), ("sin", 512), ("desc", 4), ("iota", 64),
                     ("pick", 2)])

PROD = ([("ql", i, "AD"[i % 2]) for i in range(3)] + [("kvl", 0, "D"), ("kvl", 1, "A"), ("kr", 0, "D")]
        + [("naq", i, "AD"[i % 2]) for i in range(4)]
        + [("nak", i, "AD"[i % 2]) for i in range(4)] + [("nav", i, "AD"[i % 2]) for i in range(4)]
        + [("uq", i, "AD"[i % 2]) for i in range(8)] + [("kn", i, "A") for i in range(2)]
        + [("rotk", 0, "D")] + [("rotq", i, "D") for i in range(4)]
        + [("kn", i, "A") for i in range(2, 8)] + [("vm", i, "AD"[i % 2]) for i in range(4)])
N_BEFORE_LAT = 10
PROD2 = ([("f", 0, "D")] + [("u", i, "A") for i in range(2)] + [("va", i, "A") for i in range(2)]
         + [("q", i, "D") for i in range(4)] + [("cq", 0, "D")] + [("nck", i, "A") for i in range(4)]
         + [("k", i, "D") for i in range(4)] + [("v", i, "A") for i in range(2)])


def copied(prod, n):
    e = prod[n][2]
    return e, sum(1 for p in prod[:n + 1] if p[2] == e)


def total(prod, e):
    return sum(1 for p in prod if p[2] == e)


UNITS = [(a, h, q, 4) for a in range(2) for h in range(H) for q in range(NT)]
UNITS2 = [(2, h, q, q + 1) for h in range(H) for q in range(NT)]


def block_pair_kernel(nc, xT_d, ctxT_d, vec_d, row_d, con_d, w_mod, w_in, w_uq, w_ukv, bias_d, w_out,
                      wr_d, w_gate, w_up, w_down, w_in2, wf_d, sgw_d, w_out2, w_up2, w_down2, out_d):
    with ExitStack() as ctx:
        def sb(name, shape):
            return ctx.enter_context(nc.sbuf_tensor(name, shape, F32))

        def sem(name):
            return ctx.enter_context(nc.semaphore(name))

        bank = [ctx.enter_context(nc.psum_tensor(f"bank{i}", [P, 512], F32)) for i in range(8)]

        ring = sb("ring", [P, SLOTS, SLOT])
        xT = sb("xT", [P, KD, T])
        big = sb("big", [P, 4096])
        arena = sb("arena", [P, 9216])
        att = sb("att", [P, 4, 512])
        mixT = sb("mixT", [P, KD, T])
        osb = sb("osb", [P, NT, D])
        con = sb("con", [P, NCON])
        row = sb("row", [P, NROW])
        vec = sb("vec", [P, NVEC])
        lat = sb("lat", [P, 1792])
        rstd = sb("rstd", [P, 512])
        wr = sb("wr", [P, KD, 20])
        wf = sb("wf", [P, KD, 8])
        cs = sb("cs", [P, KD, 32])
        mod = sb("mod", [P, 48, 2])
        A1 = sb("A1", [P, KD, 2])
        A2 = sb("A2", [P, KD])
        nmax = sb("nmax", [P, 48])
        rsum = sb("rsum", [P, 48])
        rinv = sb("rinv", [P, 48])
        small = sb("small", [P, 16, 32])
        posm = sb("posm", [P, 2 * NE])
        turns_f = sb("turns_f", [P, 2])
        turns_i = ctx.enter_context(nc.sbuf_tensor("turns_i", [P, 1], mybir.dt.int32))

        ctxT = osb[:, :, :].rearrange("p a (b t) -> p (a b) t", t=T)
        hT = big[:, :].rearrange("p (k t) -> p k t", t=2 * T)
        qT = big[0:QK, 0:2048].rearrange("p (h t) -> p h t", t=T)
        vm = big[:, 2048:4096].rearrange("p (j n) -> p j n", n=512)
        h2 = big[:, 0:2048].rearrange("p (k t) -> p k t", t=T)
        sgw = big[:, 2048:3072].rearrange("p (h t) -> p h t", t=P)
        outT = big[:, 2048:4096].rearrange("p (k t) -> p k t", t=T)
        kT = arena[0:QK, 0:4096].rearrange("p (h t) -> p h t", t=2 * T)
        bias = arena[:, 0:4096].rearrange("p (h q n) -> p h q n", q=NT, n=T)
        modp = mixT[:, :, :].rearrange("p a t -> p (a t)")
        modp2 = lat[:, 0:512]
        h2tok = osb
        pick_t = arena[:, 0:2048].rearrange("p (q e s) -> p q e s", q=NT, s=CAP)
        pick_w = arena[:, 2048:4096].rearrange("p (q e s) -> p q e s", q=NT, s=CAP)
        place = arena[:, 4096:6400].rearrange("p (i t) -> p i t", t=T)
        ysb = arena[:, 6400:7424]
        xs = att[:, 0:2, :].rearrange("p a (k s) -> p (a k) s", s=2 * CAP)
        hid = att[:, 2, :]
        hidT = att[:, 3, :].rearrange("p (f s) -> p f s", s=2 * CAP)
        naq = arena[:, 4096:5120].rearrange("p (i t) -> p i t", t=T)
        nak = arena[:, 5120:7168].rearrange("p (i t) -> p i t", t=2 * T)
        nav = arena[:, 7168:9216].rearrange("p (j n) -> p j n", n=512)
        nck = arena[:, 0:2048].rearrange("p (h t) -> p h t", t=T)
        nck0 = arena[:, 2048:3072].rearrange("p (h t) -> p h t", t=P)
        lnt = arena[:, 3072:4096].rearrange("p (n c) -> p n c", c=512)
        ug = arena[:, 4096:5120].rearrange("p (n c) -> p n c", c=512)
        vg = arena[:, 5120:6144].rearrange("p (n c) -> p n c", c=512)
        q2 = arena[:, 6144:7168].rearrange("p (i t) -> p i t", t=T)
        k2 = arena[:, 7168:8192].rearrange("p (i t) -> p i t", t=T)
        v2 = arena[:, 8192:9216].rearrange("p (n c) -> p n c", c=512)
        hidF = arena[:, 0:NP * T].rearrange("p (i t) -> p i t", t=T)
        yconv = lat[:, 0:1024].rearrange("p (b g t) -> p b g t", b=2, t=T)
        qlat = lat[:, 0:768].rearrange("p (i t) -> p i t", t=T)
        kvlat = lat[:, 768:1792].rearrange("p (i t) -> p i t", t=2 * T)
        rq = mixT[:, 0, :]
        rkv = mixT[:, 2:4, :].rearrange("p a t -> p (a t)")
        kr = mixT[64:96, 4:6, :].rearrange("p a t -> p (a t)")
        rtmp = mixT[64:96, 6:8, :].rearrange("p a t -> p (a t)")
        attf = att[:, :, :].rearrange("p a b -> p (a b)")
        sq = attf.rearrange("p (k t) -> p k t", t=T)

        ident = con[:, CON["ident"]:CON["ident"] + P]
        tri = con[:, CON["tri"]:CON["tri"] + P]
        upper = con[:, CON["upper"]:CON["upper"] + P]
        upper_ones = con[:, CON["upper"]:CON["upper"] + 2 * P]
        ones = con[:, CON["ones"]:CON["ones"] + P]
        namask = con[:, CON["namask"]:CON["namask"] + 64]
        rot = con[64:96, CON["rot"]:CON["rot"] + 32]
        cos = con[64:96, CON["cos"]:CON["cos"] + 512]
        sin = con[64:96, CON["sin"]:CON["sin"] + 512]
        iota = con[:, CON["iota"]:CON["iota"] + CAP]
        pick = con[:, CON["pick"]:CON["pick"] + 2]
        desc = con[:, CON["desc"]:CON["desc"] + 4]

        def v_(name, i, n=1):
            return vec[:, VEC[name] + i:VEC[name] + i + n]

        landed = [sem(f"landed{i}") for i in range(SLOTS)]
        used = sem("used")
        landed2 = [sem(f"landed2_{i}") for i in range(SLOTS)]
        used2 = sem("used2")
        mod_streamed, mod_copied, mod_picked = sem("mod_streamed"), sem("mod_copied"), sem("mod_picked")
        mod_first = sem("mod_first")
        in_x, in_vec, in_con, in_row = sem("in_x"), sem("in_vec"), sem("in_con"), sem("in_row")
        in_sg, in_bias = sem("in_sg"), sem("in_bias")
        silu_c = sem("silu_c")
        vstep, astep, gstep = sem("vstep"), sem("astep"), sem("gstep")
        squares = [sem(f"squares{i}") for i in range(6)]
        sumsq = [sem(f"sumsq{i}") for i in range(6)]
        var = [sem(f"var{i}") for i in range(6)]
        std = [sem(f"std{i}") for i in range(6)]
        normed = [sem(f"normed{i}") for i in range(6)]
        shifted = [sem(f"shifted{i}") for i in range(2)]
        prod_ready, prod_a, prod_d = sem("prod_ready"), sem("prod_a"), sem("prod_d")
        lat_sq, lat_ss, lat_var, lat_std, lat_done = (sem("lat_sq"), sem("lat_ss"), sem("lat_var"),
                                                      sem("lat_std"), sem("lat_done"))
        kr_done, kr_spread = sem("kr_done"), sem("kr_spread")
        ATT = [{n: sem(f"{n}{i}") for n in ("scores", "maxed", "exped", "turned", "ptd", "pta", "pv")}
               for i in range(2)]
        bias_ready = sem("bias_ready")
        o_out = sem("o_out")
        mix_t, mix_a, mix_d = sem("mix_t"), sem("mix_a"), sem("mix_d")
        proj_out, resid = sem("proj_out"), sem("resid")
        logits, gdiff, gexp, ediff, eexp = sem("logits"), sem("gdiff"), sem("gexp"), sem("ediff"), sem("eexp")
        comb_done, counted, turns_ready = sem("comb_done"), sem("counted"), sem("turns_ready")
        tok_t, tok_a, tok_d = sem("tok_t"), sem("tok_a"), sem("tok_d")
        picked_t, posm_moved = sem("picked_t"), sem("posm_moved")
        picked, place_t, place_done = sem("picked"), sem("place_t"), sem("place_done")
        gathered, xs_a, xs_d = sem("gathered"), sem("xs_a"), sem("xs_d")
        silu_g, hid_made, hid_t, hidT_done = sem("silu_g"), sem("hid_made"), sem("hid_t"), sem("hidT_done")
        y_half, y_a, y_d, scattered = sem("y_half"), sem("y_a"), sem("y_d"), sem("scattered")
        resid_m = sem("resid_m")
        prod2_ready, prod2_a, prod2_d = sem("prod2_ready"), sem("prod2_a"), sem("prod2_d")
        f_abs, f_ln, lf_done, nck_done = sem("f_abs"), sem("f_ln"), sem("lf_done"), sem("nck_done")
        sg_zero, ln_var, ln_std, vn_done, sg_mm, sg_done = (sem("sg_zero"), sem("ln_var"), sem("ln_std"),
                                                            sem("vn_done"), sem("sg_mm"), sem("sg_done"))
        o2_out, mix2_t, mix2_a, mix2_d = sem("o2_out"), sem("mix2_t"), sem("mix2_a"), sem("mix2_d")
        proj2_out, resid2 = sem("proj2_out"), sem("resid2")
        up_ready, conv0, tap1, tap2, silu_f, hid_done = (sem("up_ready"), sem("conv0"), sem("tap1"),
                                                         sem("tap2"), sem("silu_f"), sem("hid_done"))
        down_done, resid3, out_done = sem("down_done"), sem("resid3"), sem("out_done")

        block = ctx.enter_context(nc.Block())

        def yacc(m):
            return bank[4 + m // 2][:, (m % 2) * T:(m % 2 + 1) * T]

        NORM_BANK = [7, 7, 0, 1, 7, 0]

        @block.sync
        def _(sp):
            def issue(n, dst_cols, shape_k, src):
                prev = last_in_slot(n)
                if prev is not None and not L_IN2 - SLOTS <= prev < L_IN2:
                    sp.wait_ge(used2 if n >= L_IN2 else used, prev + 1 - (L_IN2 if n >= L_IN2 else 0))
                dst = ring[:, slot_of(n), 0:dst_cols].rearrange("p (k n) -> p k n", k=shape_k)
                sp.dma_start(dst, src).then_inc((landed2 if n >= L_IN2 else landed)[slot_of(n)], 16)

            wm = w_mod.rearrange("(k p) n -> p k n", p=P)
            wi = w_in.rearrange("(k p) n -> p k n", p=P)
            wi2 = w_in2.rearrange("(k p) n -> p k n", p=P)
            wo = w_out.rearrange("(k p) n -> p k n", p=P)
            wo2 = w_out2.rearrange("(k p) n -> p k n", p=P)
            wu2 = w_up2.rearrange("(k p) (g n) -> p k g n", p=P, g=2)
            wd2 = w_down2.rearrange("(k p) n -> p k n", p=P)
            for n in range(4):
                issue(n, 4096, KD, wm[:, :, n * 512:(n + 1) * 512])
            issue(L_QL, KD * QL, KD, wi[:, :, 0:QL])
            issue(L_KVL, KD * 288, KD, wi[:, :, 896:1184])
            issue(L_NAQ, 4096, KD, wi[:, :, 384:896])
            issue(L_NAK, 4096, KD, wi[:, :, 1184:1696])
            issue(L_NAV, 4096, KD, wi[:, :, 1696:2208])
            issue(L_UQ, 3 * 768, 3, w_uq.rearrange("(k p) n -> p k n", p=P))
            issue(L_UKV, 2 * 1024, 2, w_ukv.rearrange("(k p) n -> p k n", p=P))
            for n in range(4, N_MOD):
                issue(L_MOD2 + n - 4, 4096, KD, wm[:, :, n * 512:(n + 1) * 512])
            for n in range(2):
                issue(L_OUT + n, 4096, KD, wo[:, :, n * 512:(n + 1) * 512])
            sp.wait_ge(turns_ready, 1)
            windows = sp.value_load(turns_i[0:1, 0:1], min_val=1, max_val=T // CAP)
            with sp.Fori(0, windows) as w:
                with sp.Fori(0, NPAIR) as i:
                    for j in range(6):
                        n = L_MOE + j
                        sp.wait_ge(used, w * 48 + i * 6 + (n - SLOTS + 1))
                        src = (w_gate, w_up, w_down)[j // 2][i * 2 + j % 2]
                        sp.dma_start(ring[:, slot_of(n), :].rearrange("p (k n) -> p k n", k=4 if j >= 4 else KD),
                                     src.rearrange("(k p) n -> p k n", p=P)).then_inc(landed[slot_of(n)], 16)
            for n in range(5):
                sp.wait_ge(used, windows * 48 + (L_MOE - SLOTS + n + 1))
                issue(L_IN2 + n, 4096, KD, wi2[:, :, n * 512:(n + 1) * 512])
            sp.wait_ge(used, windows * 48 + L_MOE)
            for n in range(2):
                issue(L_OUT2 + n, 4096, KD, wo2[:, :, n * 512:(n + 1) * 512])

            def up_load(n, at):
                for g in range(2):
                    sp.dma_start(ring[:, slot_of(n), :].rearrange("p (k g n) -> p k g n", k=KD, g=2)[:, :, g, :],
                                 wu2[:, :, g, bass.ds(at, 256)]).then_inc(landed2[slot_of(n)], 16)
            for e in range(2):
                sp.wait_ge(used2, last_in_slot(L_UP + e) + 1 - L_IN2)
                up_load(L_UP + e, 256 * e)
            with sp.Fori(1, (N_UP - 1) // 2) as i:
                for e in range(2):
                    sp.wait_ge(used2, i * 2 + (L_UP + e - 1 - L_IN2))
                    up_load(L_UP + e, i * 512 + 256 * e)
            sp.wait_ge(used2, last_in_slot(L_UP + N_UP - 1) + 1 - L_IN2)
            up_load(L_UP + N_UP - 1, 256 * (N_UP - 1))
            for n in range(N_DOWN):
                k = min(4, NP - 4 * n)
                issue(L_DOWN + n, k * D, k, wd2[:, 4 * n:4 * n + k, :])
            for m in range(KD):
                sp.wait_ge(normed[5], m + 1)
                sp.dma_start(out_d[:, m, :], outT[:, m, :]).then_inc(out_done, 16)
            sp.wait_ge(out_done, 16 * KD)

        @block.gpsimd
        def _(pool):
            pool.wait_ge(kr_done, 1)
            nc.gpsimd.tensor_copy(kT[64:96, :, :], kr.unsqueeze(1).broadcast_to([32, H, 512])).then_inc(kr_spread, 1)
            for half in range(2):
                pool.wait_ge(ATT[0]["scores"], 8 * (half + 1))
                if half == 0:
                    pool.wait_ge(kr_spread, 1)
                pool.dma_start(arena[:, 2048 * half:2048 * (half + 1)],
                               bias_d[:, 2048 * half:2048 * (half + 1)]).then_inc(in_bias, 16)
                pool.wait_ge(in_bias, 16 * (half + 1))
                b = arena[:, 2048 * half:2048 * (half + 1)].rearrange("p (a n) -> p a n", n=GRID_W)
                nc.gpsimd.tensor_tensor(b, b, namask.unsqueeze(1).broadcast_to([P, 32, GRID_W]),
                                        ALU.add).then_inc(bias_ready, 1)
                pool.wait_ge(bias_ready, half + 1)
            pool.wait_ge(mix_t, 4)
            pool.dma_start(sgw[:, :, :], sgw_d).then_inc(in_sg, 16)
            pool.wait_ge(in_sg, 16)
            nc.gpsimd.memset(sgw[64:128, :, 0:64], 0.0).then_inc(sg_zero, 1)
            pool.wait_ge(sg_zero, 1)
            pool.wait_ge(prod2_a, copied(PROD2, [p[0] for p in PROD2].index("nck") + 3)[1])
            nc.gpsimd.tensor_tensor(nck0[:, :, :], nck[:, :, 0:P], tri.unsqueeze(1).broadcast_to([P, H, P]),
                                    ALU.add).then_inc(nck_done, 1)
            pool.wait_ge(nck_done, 1)
            nc.gpsimd.tensor_tensor(nck[:, :, P:T], nck[:, :, P:T], tri.unsqueeze(1).broadcast_to([P, H, P]),
                                    ALU.add).then_inc(nck_done, 1)

        @block.scalar
        def _(act):
            steps = [0]

            def link(ins):
                steps[0] += 1
                ins.then_inc(astep, 1)
                act.wait_ge(astep, steps[0])

            act.dma_start(vec[:, :], vec_d).then_inc(in_vec, 16)
            act.dma_start(xT[:, :, :], xT_d).then_inc(in_x, 16)
            act.dma_start(con[:, :], con_d).then_inc(in_con, 16)
            act.dma_start(ctxT, ctxT_d).then_inc(in_x, 16)
            act.dma_start(row[:, :], row_d.broadcast_to([P, NROW])).then_inc(in_row, 16)
            act.dma_start(wr[:, :, :], wr_d).then_inc(in_row, 16)
            act.dma_start(wf[:, :, :], wf_d).then_inc(in_row, 16)

            act.wait_ge(in_vec, 16)
            act.wait_ge(mod_first, 1)
            nc.scalar.activation(cs[:, :, 0:2], vec[:, 0:16].rearrange("p (k c) -> p k c", c=2), ACT.Silu
                                 ).then_inc(silu_c, 1)
            act.wait_ge(in_x, 32)
            nc.scalar.activation(hT[:, :, 0:T], xT[:, :, :], ACT.Square).then_inc(squares[0], 1)
            nc.scalar.activation(hT[:, :, T:2 * T], ctxT, ACT.Square).then_inc(squares[0], 1)
            act.wait_ge(var[0], 1)
            nc.scalar.activation(rstd[:, :], rstd[:, :], ACT.Sqrt).then_inc(std[0], 1)
            for half in range(4):
                act.wait_ge(mod_streamed, half + 1)
                nc.scalar.activation(modp[:, half * 512:(half + 1) * 512], bank[half][:, :], ACT.Copy
                                     ).then_inc(mod_copied, 1)
            for k in range(KD):
                for s in range(2):
                    act.wait_ge(normed[0], 2 * k + s + 1)
                    nc.scalar.activation(hT[:, k, s * T:(s + 1) * T], hT[:, k, s * T:(s + 1) * T], ACT.Identity,
                                         bias=mod[:, k, s:s + 1]).then_inc(shifted[0], 1)

            def out_of_psum(n):
                kind, i, e = PROD[n]
                src = bank[n % 4]
                act.wait_ge(prod_ready, n + 1)
                scale = 1.0
                if kind == "ql":
                    dst, src = qlat[:, i, :], src[:, 0:T]
                elif kind == "kvl":
                    dst, src = kvlat[:, i, :], src[:, :]
                elif kind == "naq":
                    dst, src, scale = naq[:, i, :], src[:, 0:T], HD ** -0.5
                elif kind == "nak":
                    dst, src = nak[:, i, :], src[:, :]
                elif kind == "nav":
                    dst, src = nav[:, i, :], src[:, :]
                elif kind == "uq":
                    dst, src, scale = qT[:, i, :], src[0:QK, 0:T], QK ** -0.5
                elif kind == "kn":
                    dst, src = kT[0:NOPE, i, :], src[0:NOPE, :]
                elif kind == "vm":
                    dst, src = vm[:, i, :], src[:, :]
                nc.scalar.activation(dst, src, ACT.Copy, scale=scale).then_inc(prod_a, 1)

            done = 0
            for n, (kind, i, e) in enumerate(PROD):
                if n == 5:
                    act.wait_ge(prod_d, copied(PROD, 3)[1])
                    act.wait_ge(prod_a, copied(PROD, 4)[1])
                    nc.scalar.activation(attf[:, 0:1792], lat[:, :], ACT.Square).then_inc(lat_sq, 1)
                if n == N_BEFORE_LAT:
                    act.wait_ge(lat_var, 2)
                    nc.scalar.activation(rq, rq, ACT.Sqrt).then_inc(lat_std, 1)
                    nc.scalar.activation(rkv, rkv, ACT.Sqrt).then_inc(lat_std, 1)
                if e == "A":
                    out_of_psum(n)

            def exps(units, A, s):
                a, h, q, nk = units[s]
                u = 16 * a + 8 * q + h
                act.wait_ge(A["maxed"], s + 1)
                if s >= 2:
                    act.wait_ge(A["turned"], s - 1)
                nc.scalar.activation(att[:, s % 2, 0:nk * P], bank[s % 2][:, 0:nk * P], ACT.Exp,
                                     bias=nmax[:, u:u + 1], accum_out=rsum[:, u:u + 1]).then_inc(A["exped"], 1)

            def turn_copy(units, A, s):
                w = units[s][3] * P
                act.wait_ge(A["turned"], s + 1)
                if s >= 2:
                    act.wait_ge(A["pv"], s - 1)
                nc.scalar.activation(att[:, 3, 0:w], bank[3][:, 0:w], ACT.Copy).then_inc(A["pta"], 1)

            def attention(units, A):
                for s in range(len(units) + 1):
                    if s < len(units):
                        exps(units, A, s)
                    if units is UNITS and s % 4 == 2:
                        act.wait_ge(mod_streamed, 5 + s // 4)
                        if s // 4:
                            act.wait_ge(mod_picked, 4 + s // 4)
                        nc.scalar.activation(modp2, bank[7][:, :], ACT.Copy).then_inc(mod_copied, 1)
                    if s >= 1 and (s - 1) % 2:
                        turn_copy(units, A, s - 1)

            attention(UNITS, ATT[0])

            def mix_copy(ready, done):
                for c in (0, 2):
                    act.wait_ge(ready, c + 1)
                    nc.scalar.activation(mixT[:, 2 * c:2 * c + 2, :].rearrange("p a t -> p (a t)"), bank[c][:, :],
                                         ACT.Copy).then_inc(done, 1)

            mix_copy(mix_t, mix_a)

            def norm(r, updated):
                for k in range(KD):
                    act.wait_ge(updated, k + 1)
                    nc.scalar.activation(sq[:, k, :], xT[:, k, :], ACT.Square).then_inc(squares[r], 1)
                act.wait_ge(var[r], 1)
                nc.scalar.activation(rstd[:, 0:T], rstd[:, 0:T], ACT.Sqrt).then_inc(std[r], 1)

            norm(1, resid)
            for k in range(KD):
                act.wait_ge(normed[1], k + 1)
                nc.scalar.activation(h2[:, k, :], h2[:, k, :], ACT.Identity, bias=mod[:, 24 + k, 0:1]
                                     ).then_inc(shifted[1], 1)
            act.wait_ge(gdiff, 1)
            nc.scalar.activation(small[:, 1, 0:8], small[:, 1, 0:8], ACT.Exp).then_inc(gexp, 1)
            act.wait_ge(ediff, 1)
            nc.scalar.activation(small[:, 5, 0:8], small[:, 5, 0:8], ACT.Exp).then_inc(eexp, 1)
            for b in (0, 2):
                act.wait_ge(tok_t, b + 1)
                nc.scalar.activation(h2tok[:, b // 2, (b % 2) * 512:(b % 2 + 1) * 512], bank[b][:, :], ACT.Copy
                                     ).then_inc(tok_a, 1)
            act.wait_ge(turns_ready, 1)
            windows = act.value_load(turns_i[0:1, 0:1], min_val=1, max_val=T // CAP)
            with act.Fori(0, windows) as w:
                with act.Fori(0, NPAIR) as i:
                    act.wait_ge(gathered, w * 16 + i * 2 + 1)
                    nc.scalar.activation(xs[:, 0:4, :], bank[0][:, :].rearrange("p (k s) -> p k s", k=4), ACT.Copy
                                         ).then_inc(xs_a, 1)
                    act.wait_ge(used, w * 48 + i * 6 + (L_MOE + 2))
                    nc.scalar.activation(hid, bank[2][:, :], ACT.Silu).then_inc(silu_g, 1)
                    act.wait_ge(y_half, w * 8 + i + 1)
                    act.wait_ge(scattered, w * 9 + i + 2)
                    nc.scalar.activation(ysb[:, 0:512], bank[2][:, :], ACT.Copy).then_inc(y_a, 1)
            norm(2, resid_m)
            norm(3, normed[2])

            def out_of_psum2(n):
                kind, i, e = PROD2[n]
                src = bank[n % 4]
                act.wait_ge(prod2_ready, n + 1)
                if kind == "u":
                    ins = nc.scalar.activation(ug[:, i, :], src[:, :], ACT.Gelu)
                elif kind == "va":
                    ins = nc.scalar.activation(vg[:, i, :], src[:, :], ACT.Gelu)
                elif kind == "nck":
                    ins = nc.scalar.activation(nck[:, 2 * i:2 * i + 2, :].rearrange("p a t -> p (a t)"), src[:, :],
                                               ACT.Copy, scale=-1.0)
                elif kind == "v":
                    ins = nc.scalar.activation(v2[:, i, :], src[:, :], ACT.Copy)
                ins.then_inc(prod2_a, 1)

            act.wait_ge(f_abs, 1)
            link(nc.scalar.activation(small[:, 1, 0:16], small[:, 1, 0:16], ACT.Exp))
            nc.scalar.activation(small[:, 1, 0:16], small[:, 1, 0:16], ACT.Ln, bias=1.0).then_inc(f_ln, 1)
            for n, (kind, i, e) in enumerate(PROD2):
                if e == "A":
                    out_of_psum2(n)
            act.wait_ge(ln_var, 1)
            nc.scalar.activation(small[:, 6, 0:16], small[:, 6, 0:16], ACT.Sqrt).then_inc(ln_std, 1)
            attention(UNITS2, ATT[1])
            mix_copy(mix2_t, mix2_a)
            norm(4, resid2)

            def conv(i, j, first):
                b = j % 2
                act.wait_ge(up_ready, i * 4 + (j + 1))
                if not (first and j < 2):
                    act.wait_ge(hid_done, i * 4 + (j - 1))
                for g in range(2):
                    at = i * 4 + (j + 22 * g)
                    nc.scalar.activation(yconv[:, b, g, :], bank[j % 4][:, g * T:(g + 1) * T], ACT.Identity,
                                         bias=vec[:, bass.ds(at + VEC["b_conv"], 1)],
                                         scale=vec[:, bass.ds(at + (VEC["w_conv"] + 88), 1)]).then_inc(conv0, 1)
                act.wait_ge(tap2, i * 8 + (2 * j + 1))
                nc.scalar.activation(yconv[:, b, 0, :], yconv[:, b, 0, :], ACT.Silu).then_inc(silu_f, 1)

            for j in range(4):
                conv(0, j, True)
            with act.Fori(1, NP // 4) as i:
                for j in range(4):
                    conv(i, j, False)
            for j in range(NP % 4):
                conv(NP // 4, j, False)
            norm(5, resid3)

        @block.tensor
        def _(pe):
            def slot(n, k):
                return ring[:, slot_of(n), 0:SLOT // k * k].rearrange("p (k n) -> p k n", k=k)

            def arrive(n):
                pe.wait_ge((landed2 if n >= L_IN2 else landed)[slot_of(n)], landed_count(n))

            pe.wait_ge(in_con, 16)
            pe.wait_ge(squares[0], 2)
            for k in range(KD):
                last = nc.tensor.matmul(bank[7][:, :], ones, hT[:, k, :], start=(k == 0), stop=(k == KD - 1))
            last.then_inc(sumsq[0], 1)

            def mod_stream(n, b):
                arrive(n)
                w = slot(n, KD)
                for k in range(KD):
                    g = 32 * (k % 4)
                    last = nc.tensor.matmul(bank[b][g:g + 32, :], cs[:, k, :], w[:, k, :],
                                            start=(k < 4), stop=(k >= 4))
                last.then_inc(mod_streamed, 1)
                pe.wait_ge(mod_streamed, n - (0 if n < 4 else L_MOD2 - 4) + 1)
                pe.sem_inc(used, 1)

            def mod_pick(half, src):
                pe.wait_ge(mod_copied, half + 1)
                for t in range(4):
                    c = 8 * half + 2 * t
                    last = nc.tensor.matmul(bank[6][:, c:c + 2], src[:, t * P:(t + 1) * P], pick, start=True, stop=True)
                last.then_inc(mod_picked, 1)

            pe.wait_ge(silu_c, 1)
            for half in range(4):
                mod_stream(half, half)
            for half in range(4):
                mod_pick(half, modp[:, half * 512:(half + 1) * 512])

            def bank_free(prod, n, sa, sd):
                if n >= 4:
                    e, count = copied(prod, n - 4)
                    pe.wait_ge(sa if e == "A" else sd, count)

            def latent_sums():
                pe.wait_ge(lat_sq, 1)
                for k in range(3):
                    last = nc.tensor.matmul(bank[4][:, 0:T], ones, attf[:, k * T:(k + 1) * T],
                                            start=(k == 0), stop=(k == 2))
                last.then_inc(lat_ss, 1)
                for k in range(2):
                    last = nc.tensor.matmul(bank[5][:, :], ones, attf[:, 768 + 512 * k:1280 + 512 * k],
                                            start=(k == 0), stop=(k == 1))
                last.then_inc(lat_ss, 1)

            pe.wait_ge(shifted[0], 2 * KD)
            loads = {"ql": L_QL, "kvl": L_KVL, "kr": L_KVL, "naq": L_NAQ, "nak": L_NAK, "nav": L_NAV,
                     "uq": L_UQ, "kn": L_UKV, "vm": L_UKV}
            lastuse = {"ql": 2, "kr": 0, "naq": 3, "nak": 3, "nav": 3, "uq": 7, "vm": 3}
            for n, (kind, i, _e) in enumerate(PROD):
                if n == N_BEFORE_LAT:
                    latent_sums()
                bank_free(PROD, n, prod_a, prod_d)
                dst = bank[n % 4]
                if kind in loads and i == 0:
                    arrive(loads[kind])
                if kind == "ql":
                    w = ring[:, slot_of(L_QL), 0:KD * QL].rearrange("p (k n) -> p k n", k=KD)
                    for k in range(KD):
                        last = nc.tensor.matmul(dst[:, 0:T], w[:, k, i * P:(i + 1) * P], hT[:, k, 0:T],
                                                start=(k == 0), stop=(k == KD - 1))
                elif kind in ("kvl", "kr"):
                    w = ring[:, slot_of(L_KVL), 0:KD * 288].rearrange("p (k n) -> p k n", k=KD)
                    lo, m = (i * P, P) if kind == "kvl" else (192, QK)
                    for k in range(KD):
                        last = nc.tensor.matmul(dst[0:m, :], w[:, k, lo:lo + m], hT[:, k, :],
                                                start=(k == 0), stop=(k == KD - 1))
                elif kind in ("naq", "nak"):
                    w = slot(loads[kind], KD)
                    cols = T if kind == "naq" else 2 * T
                    for k in range(KD):
                        last = nc.tensor.matmul(dst[:, 0:cols], w[:, k, i * P:(i + 1) * P], hT[:, k, 0:cols],
                                                start=(k == 0), stop=(k == KD - 1))
                elif kind == "nav":
                    w = slot(L_NAV, KD)
                    for k in range(KD):
                        last = nc.tensor.matmul(dst[:, :], hT[:, k, i * P:(i + 1) * P], w[:, k, :],
                                                start=(k == 0), stop=(k == KD - 1))
                elif kind == "uq":
                    if i == 0:
                        pe.wait_ge(lat_done, 5)
                        pe.wait_ge(prod_ready, n)
                    w = ring[:, slot_of(L_UQ), 0:2304].rearrange("p (k n) -> p k n", k=3)
                    for k in range(3):
                        last = nc.tensor.matmul(dst[0:QK, 0:T], w[:, k, i * QK:(i + 1) * QK], qlat[:, k, :],
                                                start=(k == 0), stop=(k == 2))
                elif kind == "kn":
                    w = ring[:, slot_of(L_UKV), 0:2048].rearrange("p (k n) -> p k n", k=2)
                    for k in range(2):
                        last = nc.tensor.matmul(dst[0:NOPE, :], w[:, k, i * P:i * P + NOPE], kvlat[:, k, :],
                                                start=(k == 0), stop=(k == 1))
                elif kind == "vm":
                    w = ring[:, slot_of(L_UKV), 0:2048].rearrange("p (k h n) -> p k h n", k=2, h=H)
                    for k in range(2):
                        last = nc.tensor.matmul(dst[:, :], kvlat[:, k, i * P:(i + 1) * P], w[:, k, :, NOPE:P],
                                                start=(k == 0), stop=(k == 1))
                elif kind == "rotk":
                    pe.wait_ge(prod_d, copied(PROD, 5)[1])
                    last = nc.tensor.matmul(dst[64:96, :], rot, kr, start=True, stop=True)
                elif kind == "rotq":
                    if i == 0:
                        pe.wait_ge(prod_a, copied(PROD, 24)[1])
                        pe.wait_ge(prod_d, copied(PROD, 25)[1])
                    last = nc.tensor.matmul(dst[64:96, :], rot, qT[64:96, 2 * i:2 * i + 2, :], start=True, stop=True)
                last.then_inc(prod_ready, 1)
                if lastuse.get(kind) == i:
                    pe.wait_ge(prod_ready, n + 1)
                    pe.sem_inc(used, 1)

            def scores(units, A, s):
                a, h, q, nk = units[s]
                if s >= 2:
                    pe.wait_ge(A["exped"], s - 1)
                lo = 64 * (h % 2)
                if a == 0:
                    lhs, rhs = qT[:, h, q * P:(q + 1) * P], kT[:, h, :]
                elif a == 1:
                    lhs, rhs = naq[lo:lo + 64, h // 2, q * P:(q + 1) * P], nak[lo:lo + 64, h // 2, :]
                else:
                    lhs, rhs = q2[lo:lo + 64, h // 2, q * P:(q + 1) * P], k2[lo:lo + 64, h // 2, 0:nk * P]
                nc.tensor.matmul(bank[s % 2][:, 0:nk * P], lhs, rhs, start=True, stop=True).then_inc(A["scores"], 1)

            def turns(units, A, s):
                nk = units[s][3]
                pe.wait_ge(A["exped"], s + 1)
                if s >= 2:
                    pe.wait_ge(A["pta" if s % 2 else "ptd"], s // 2)
                for j in range(nk):
                    last = nc.tensor.transpose(bank[2 + s % 2][:, j * P:(j + 1) * P], att[:, s % 2, j * P:(j + 1) * P],
                                               ident)
                last.then_inc(A["turned"], 1)

            def values(units, A, s):
                a, h, q, nk = units[s]
                v = (vm, nav, v2)[a]
                pe.wait_ge(A["pta" if s % 2 else "ptd"], s // 2 + 1)
                if a == 1 and h == 0 and q == 0:
                    pe.wait_ge(o_out, NT)
                for j in range(nk):
                    last = nc.tensor.matmul(bank[4 + q][:, h * HD:(h + 1) * HD], att[:, 2 + s % 2, j * P:(j + 1) * P],
                                            v[:, j, h * HD:(h + 1) * HD], start=(j == 0), stop=(j == nk - 1))
                last.then_inc(A["pv"], 1)

            def attention(units, A, between):
                for s in range(len(units) + 2):
                    if s < len(units):
                        scores(units, A, s)
                    if 1 <= s <= len(units):
                        turns(units, A, s - 1)
                    if s >= 2:
                        values(units, A, s - 2)
                    between(s)

            pe.wait_ge(prod_a, total(PROD, "A"))
            pe.wait_ge(prod_d, total(PROD, "D"))
            pe.wait_ge(kr_spread, 1)

            def rest_of_mod(s):
                if s % 4 == 1 and s // 4 < 8:
                    if s // 4:
                        pe.wait_ge(mod_copied, 4 + s // 4)
                    mod_stream(L_MOD2 + s // 4, 7)
                if s % 4 == 3 and s // 4 < 8:
                    mod_pick(4 + s // 4, modp2)

            attention(UNITS, ATT[0], rest_of_mod)

            def turn_mixed(turned):
                for c in range(KD):
                    for q in range(NT):
                        last = nc.tensor.transpose(bank[c // 2][:, (c % 2) * T + q * P:(c % 2) * T + (q + 1) * P],
                                                   osb[:, q, c * P:(c + 1) * P], ident)
                    if c % 2:
                        last.then_inc(turned, 1)

            pe.wait_ge(o_out, 2 * NT)
            turn_mixed(mix_t)

            def out_projection(load, a, d, ready, freed):
                pe.wait_ge(a, 2)
                pe.wait_ge(d, 2)
                for m in range(KD):
                    if m % 4 == 0:
                        arrive(load + m // 4)
                    w = slot(load + m // 4, KD)
                    if m >= 4:
                        pe.wait_ge(freed, m - 3)
                    for k in range(KD):
                        last = nc.tensor.matmul(bank[m % 4][:, 0:T], w[:, k, (m % 4) * P:(m % 4 + 1) * P],
                                                mixT[:, k, :], start=(k == 0), stop=(k == KD - 1))
                    last.then_inc(ready, 1)
                    if m % 4 == 3:
                        pe.wait_ge(ready, m + 1)
                        pe.sem_inc(used2 if load >= L_IN2 else used, 1)

            out_projection(L_OUT, mix_a, mix_d, proj_out, resid)

            def norm_sum(r):
                for k in range(KD):
                    pe.wait_ge(squares[r], k + 1)
                    last = nc.tensor.matmul(bank[NORM_BANK[r]][:, 0:T], ones, sq[:, k, :],
                                            start=(k == 0), stop=(k == KD - 1))
                last.then_inc(sumsq[r], 1)

            norm_sum(1)
            pe.wait_ge(in_row, 48)
            pe.wait_ge(shifted[1], KD)
            for q in range(NT):
                for k in range(KD):
                    last = nc.tensor.matmul(bank[6][:, 128 + 20 * q:148 + 20 * q], h2[:, k, q * P:(q + 1) * P],
                                            wr[:, k, :], start=(k == 0), stop=(k == KD - 1))
            last.then_inc(logits, 1)
            for b in range(4):
                for k in range(4):
                    last = nc.tensor.transpose(bank[b][:, k * P:(k + 1) * P],
                                               h2[:, 4 * (b % 2) + k, (b // 2) * P:(b // 2 + 1) * P], ident)
                last.then_inc(tok_t, 1)
            pe.wait_ge(comb_done, NT)
            chosen = small[:, 14, :].rearrange("p (q e) -> p q e", q=NT)
            nc.tensor.matmul(bank[6][:, 192:208], upper, chosen[:, 0, :], start=True, stop=True)
            nc.tensor.matmul(bank[6][:, 208:224], ones, chosen[:, 0, :], start=True, stop=False)
            nc.tensor.matmul(bank[6][:, 208:224], upper, chosen[:, 1, :], start=False, stop=True)
            for q in range(NT):
                last = nc.tensor.matmul(bank[6][:, 224:240], ones, chosen[:, q, :], start=(q == 0), stop=(q == 1))
            last.then_inc(counted, 1)
            pe.wait_ge(turns_ready, 1)
            windows = pe.value_load(turns_i[0:1, 0:1], min_val=1, max_val=T // CAP)
            for b in range(4):
                last = nc.tensor.matmul(bank[4 + b][:, :], cs[:, 0, 31:32].broadcast_to([P, P]), con[:, 0:512],
                                        start=True, stop=False, skip_group_check=True)
            last.then_inc(scattered, 1)
            pe.wait_ge(tok_a, 2)
            pe.wait_ge(tok_d, 2)

            def scatter(i):
                for m in range(KD):
                    last = nc.tensor.matmul(yacc(m), ysb[:, m * P:(m + 1) * P], place[:, i, :],
                                            start=False, stop=False, skip_group_check=True)
                last.then_inc(scattered, 1)

            with pe.Fori(0, windows) as w:
                pe.wait_ge(picked, w + 1)
                for b in range(4):
                    for c in range(2):
                        for q in range(NT):
                            i = 2 * b + c
                            last = nc.tensor.transpose(bank[b][:, c * T + q * P:c * T + (q + 1) * P],
                                                       pick_w[:, q, 2 * i:2 * i + 2, :], ident)
                    last.then_inc(place_t, 1)
                with pe.Fori(0, NPAIR) as i:
                    pe.wait_ge(place_done, w * 4 + 4)
                    for k in range(KD):
                        for q in range(NT):
                            last = nc.tensor.matmul(bank[k // 4][:, (k % 4) * P:(k % 4 + 1) * P],
                                                    h2tok[:, q, k * P:(k + 1) * P],
                                                    arena[:, bass.ds(i * P + q * 1024, P)],
                                                    start=(q == 0), stop=(q == NT - 1))
                        if k % 4 == 3:
                            last.then_inc(gathered, 1)
                    pe.wait_ge(xs_a, w * 8 + i + 1)
                    pe.wait_ge(xs_d, w * 8 + i + 1)
                    for j in range(2):
                        n = L_MOE + 2 * j
                        for e in range(2):
                            pe.wait_ge(landed[slot_of(n + e)], w * 128 + i * 16 + landed_count(n + e))
                        if j == 0:
                            pe.wait_ge(y_a, w * 9 + i + 1)
                            pe.wait_ge(y_d, w * 9 + i + 1)
                        for k in range(KD):
                            for e in range(2):
                                last = nc.tensor.matmul(bank[2 + j][CAP * e:CAP * (e + 1), :],
                                                        xs[:, k, CAP * e:CAP * (e + 1)], slot(n + e, KD)[:, k, :],
                                                        start=(k == 0), stop=(k == KD - 1))
                                if k == KD - 1:
                                    last.then_inc(used, 1)
                    scatter(i)
                    pe.wait_ge(hid_made, w * 8 + i + 1)
                    for f in range(4):
                        last = nc.tensor.transpose(bank[0][:, f * P:(f + 1) * P], hid[:, f * P:(f + 1) * P], ident)
                    last.then_inc(hid_t, 1)
                    pe.wait_ge(hidT_done, w * 8 + i + 1)
                    for e in range(2):
                        pe.wait_ge(landed[slot_of(L_MOE + 4 + e)], w * 128 + i * 16 + landed_count(L_MOE + 4 + e))
                    for half in range(2):
                        for f in range(4):
                            for e in range(2):
                                last = nc.tensor.matmul(bank[2 + half][CAP * e:CAP * (e + 1), :],
                                                        hidT[:, f, CAP * e:CAP * (e + 1)],
                                                        slot(L_MOE + 4 + e, 4)[:, f, half * 512:(half + 1) * 512],
                                                        start=(f == 0), stop=(f == 3))
                                if half == 1 and f == 3:
                                    last.then_inc(used, 1)
                        if half == 0:
                            last.then_inc(y_half, 1)
                pe.wait_ge(y_a, w * 9 + 9)
                pe.wait_ge(y_d, w * 9 + 9)
                scatter(NPAIR)
            norm_sum(2)
            norm_sum(3)

            loads2 = {"u": L_IN2, "va": L_IN2 + 1, "q": L_IN2 + 2, "k": L_IN2 + 3, "v": L_IN2 + 4}
            lf = small[:, 2, 0:16].rearrange("p (q h) -> p q h", q=NT)
            for n, (kind, i, _e) in enumerate(PROD2):
                bank_free(PROD2, n, prod2_a, prod2_d)
                dst = bank[n % 4]
                if kind in loads2 and i == 0:
                    arrive(loads2[kind])
                if kind == "f":
                    for k in range(KD):
                        pe.wait_ge(normed[3], k + 1)
                    for q in range(NT):
                        for k in range(KD):
                            last = nc.tensor.matmul(dst[:, 8 * q:8 * q + 8], h2[:, k, q * P:(q + 1) * P], wf[:, k, :],
                                                    start=(k == 0), stop=(k == KD - 1))
                elif kind in ("u", "va", "v"):
                    w = slot(loads2[kind], KD)
                    for k in range(KD):
                        last = nc.tensor.matmul(dst[:, :], h2[:, k, i * P:(i + 1) * P], w[:, k, :],
                                                start=(k == 0), stop=(k == KD - 1))
                elif kind in ("q", "k"):
                    w = slot(loads2[kind], KD)
                    for k in range(KD):
                        last = nc.tensor.matmul(dst[:, 0:T], w[:, k, i * P:(i + 1) * P], h2[:, k, :],
                                                start=(k == 0), stop=(k == KD - 1))
                elif kind == "cq":
                    pe.wait_ge(lf_done, 1)
                    nc.tensor.matmul(dst[:, 0:8], upper, lf[:, 0, :], start=True, stop=True)
                    nc.tensor.matmul(dst[:, 8:16], ones, lf[:, 0, :], start=True, stop=False)
                    last = nc.tensor.matmul(dst[:, 8:16], upper, lf[:, 1, :], start=False, stop=True)
                elif kind == "nck":
                    for j in range(2):
                        h = 2 * i + j
                        nc.tensor.matmul(dst[:, j * T:(j + 1) * T], lf[:, 0, h:h + 1].broadcast_to([P, P]),
                                         upper_ones, start=True, stop=False)
                        last = nc.tensor.matmul(dst[:, j * T + P:(j + 1) * T], lf[:, 1, h:h + 1].broadcast_to([P, P]),
                                                upper, start=False, stop=True)
                last.then_inc(prod2_ready, 1)
                if {"u": 1, "va": 1, "q": 3, "k": 3, "v": 1}.get(kind) == i:
                    pe.wait_ge(prod2_ready, n + 1)
                    pe.sem_inc(used2, 1)
            pe.wait_ge(vn_done, 1)
            pe.wait_ge(sg_zero, 1)
            for q in range(NT):
                for h in range(H):
                    last = nc.tensor.matmul(bank[6 + q][:, h * HD:(h + 1) * HD], sgw[:, h, :],
                                            vg[:, q, h * HD:(h + 1) * HD], start=True, stop=True)
                last.then_inc(sg_mm, 1)
            pe.wait_ge(prod2_a, total(PROD2, "A"))
            pe.wait_ge(prod2_d, total(PROD2, "D"))
            attention(UNITS2, ATT[1], lambda s: None)
            pe.wait_ge(o2_out, NT)
            pe.wait_ge(sg_done, NT)
            turn_mixed(mix2_t)
            out_projection(L_OUT2, mix2_a, mix2_d, proj2_out, resid2)
            norm_sum(4)

            pe.wait_ge(normed[4], KD)

            def up_pairs(i, n, count, first):
                w = ring[:, slot_of(n), :].rearrange("p (k g n) -> p k g n", k=KD, g=2)
                base = 2 * ((n - L_UP) % 2) if n < L_UP + N_UP - 1 else 0
                for j in range(base, base + count):
                    if not first:
                        pe.wait_ge(tap2, i * 8 + (2 * j - 6))
                    for g in range(2):
                        for k in range(KD):
                            last = nc.tensor.matmul(bank[j][:, g * T:(g + 1) * T],
                                                    w[:, k, g, (j - base) * P:(j - base + 1) * P], h2[:, k, :],
                                                    start=(k == 0), stop=(k == KD - 1))
                    last.then_inc(up_ready, 1)
                pe.wait_ge(up_ready, i * 4 + (base + count))
                pe.sem_inc(used2, 1)

            for e in range(2):
                arrive(L_UP + e)
                up_pairs(0, L_UP + e, 2, True)
            with pe.Fori(1, (N_UP - 1) // 2) as i:
                for e in range(2):
                    pe.wait_ge(landed2[slot_of(L_UP + e)], i * 32 + landed_count(L_UP + e))
                    up_pairs(i, L_UP + e, 2, False)
            arrive(L_UP + N_UP - 1)
            up_pairs((N_UP - 1) // 2, L_UP + N_UP - 1, 2, False)
            pe.wait_ge(resid2, KD)
            for kt in range(NP):
                n = L_DOWN + kt // 4
                if kt % 4 == 0:
                    arrive(n)
                k_in = min(4, NP - 4 * (kt // 4))
                w = ring[:, slot_of(n), 0:k_in * D].rearrange("p (k n) -> p k n", k=k_in)
                pe.wait_ge(hid_done, kt + 1)
                for m in range(KD):
                    last = nc.tensor.matmul(yacc(m), w[:, kt % 4, m * P:(m + 1) * P], hidF[:, kt, :],
                                            start=(kt == 0 and m % 2 == 0), stop=(kt == NP - 1),
                                            skip_group_check=True)
            last.then_inc(down_done, 1)
            norm_sum(5)

        @block.vector
        def _(dve):
            steps = [0]

            def link(ins):
                steps[0] += 1
                ins.then_inc(vstep, 1)
                dve.wait_ge(vstep, steps[0])

            V = nc.vector

            def bc(ap, axis, shape):
                return ap.unsqueeze(axis).broadcast_to(shape)

            V.memset(cs[:, :, :], 0.0).then_inc(mod_first, 1)
            dve.wait_ge(sumsq[0], 1)
            V.tensor_scalar(rstd[:, :], bank[7][:, :], 1.0 / D, EPS, ALU.mult, ALU.add).then_inc(var[0], 1)
            dve.wait_ge(std[0], 1)
            link(V.reciprocal(rstd[:, :], rstd[:, :]))
            dve.wait_ge(mod_picked, 4)
            dve.wait_ge(in_vec, 16)
            link(V.tensor_tensor(mod[:, 0:16, :], bank[6][:, 0:32].rearrange("p (n c) -> p n c", c=2),
                                 bc(v_("b_mod", 0, 16), 2, [P, 16, 2]), ALU.add))
            link(V.scalar_tensor_tensor(A1[:, :, :], mod[:, 8:16, :], 1.0, bc(v_("g_attn", 0, 8), 2, [P, 8, 2]),
                                        ALU.add, ALU.mult))
            for k in range(KD):
                for s, src in enumerate((xT[:, k, :], ctxT[:, k, :])):
                    V.scalar_tensor_tensor(hT[:, k, s * T:(s + 1) * T], src, A1[:, k, s:s + 1],
                                           rstd[:, s * T:(s + 1) * T], ALU.mult, ALU.mult).then_inc(normed[0], 1)

            def rotate(q, r, tmp, c, s):
                link(V.tensor_tensor(tmp, r, s, ALU.mult))
                link(V.tensor_tensor(q, q, c, ALU.mult))
                return V.tensor_tensor(q, q, tmp, ALU.add)

            def out_of_psum(n):
                kind, i, e = PROD[n]
                src = bank[n % 4]
                dve.wait_ge(prod_ready, n + 1)
                if kind == "ql":
                    ins = V.tensor_copy(qlat[:, i, :], src[:, 0:T])
                elif kind == "kvl":
                    ins = V.tensor_copy(kvlat[:, i, :], src[:, :])
                elif kind == "kr":
                    ins = V.tensor_copy(kr, src[64:96, :])
                elif kind == "naq":
                    ins = V.tensor_scalar(naq[:, i, :], src[:, 0:T], HD ** -0.5, None, ALU.mult)
                elif kind == "nak":
                    ins = V.tensor_copy(nak[:, i, :], src[:, :])
                elif kind == "nav":
                    ins = V.tensor_copy(nav[:, i, :], src[:, :])
                elif kind == "uq":
                    ins = V.tensor_scalar(qT[:, i, :], src[0:QK, 0:T], QK ** -0.5, None, ALU.mult)
                elif kind == "kn":
                    ins = V.tensor_copy(kT[0:NOPE, i, :], src[0:NOPE, :])
                elif kind == "vm":
                    ins = V.tensor_copy(vm[:, i, :], src[:, :])
                elif kind == "rotk":
                    ins = rotate(kr, src[64:96, :], rtmp, cos, sin)
                elif kind == "rotq":
                    q = qT[64:96, 2 * i:2 * i + 2, :]
                    ins = rotate(q, src[64:96, :].rearrange("p (a t) -> p a t", a=2),
                                 rtmp.rearrange("p (a t) -> p a t", a=2),
                                 bc(cos[:, 0:T], 1, [32, 2, T]), bc(sin[:, 0:T], 1, [32, 2, T]))
                ins.then_inc(prod_d, 1)
                if kind == "rotk":
                    dve.wait_ge(prod_d, copied(PROD, n)[1])
                    dve.sem_inc(kr_done, 1)
                if kind == "rotq" or kind == "rotk":
                    dve.wait_ge(prod_d, copied(PROD, n)[1])

            for n, (kind, i, e) in enumerate(PROD):
                if n == N_BEFORE_LAT:
                    dve.wait_ge(lat_ss, 2)
                    V.tensor_scalar(rq, bank[4][:, 0:T], 1.0 / QL, EPS, ALU.mult, ALU.add).then_inc(lat_var, 1)
                    V.tensor_scalar(rkv, bank[5][:, :], 1.0 / KVL, EPS, ALU.mult, ALU.add).then_inc(lat_var, 1)
                    dve.wait_ge(lat_std, 2)
                    link(V.reciprocal(rq, rq))
                    link(V.reciprocal(rkv, rkv))
                    dve.wait_ge(prod_a, copied(PROD, 4)[1])
                    for k in range(3):
                        V.scalar_tensor_tensor(qlat[:, k, :], qlat[:, k, :], v_("g_qa", k), rq, ALU.mult, ALU.mult
                                               ).then_inc(lat_done, 1)
                    for k in range(2):
                        V.scalar_tensor_tensor(kvlat[:, k, :], kvlat[:, k, :], v_("g_kva", k), rkv, ALU.mult, ALU.mult
                                               ).then_inc(lat_done, 1)
                if e == "D":
                    out_of_psum(n)

            def maxes(units, A, s):
                a, h, q, nk = units[s]
                u = 16 * a + 8 * q + h
                S = bank[s % 2]
                dve.wait_ge(A["scores"], s + 1)
                if a == 1:
                    if q == 0 and h % 4 == 0:
                        dve.wait_ge(bias_ready, h // 4 + 1)
                    link(V.tensor_tensor(S[:, 0:T], S[:, 0:T], bias[:, h, q, :], ALU.add))
                if a == 2:
                    if s == 0:
                        dve.wait_ge(nck_done, 2)
                    key = nck0[:, h, :] if q == 0 else nck[:, h, :]
                    link(V.scalar_tensor_tensor(S[:, 0:nk * P], S[:, 0:nk * P], cq[:, 8 * q + h:8 * q + h + 1], key,
                                                ALU.add, ALU.add))
                V.tensor_reduce(nmax[:, u:u + 1], S[:, 0:nk * P], AX, ALU.max, negate=True).then_inc(A["maxed"], 1)

            def turn_copy(units, A, s):
                w = units[s][3] * P
                dve.wait_ge(A["turned"], s + 1)
                if s >= 2:
                    dve.wait_ge(A["pv"], s - 1)
                V.tensor_copy(att[:, 2, 0:w], bank[2][:, 0:w]).then_inc(A["ptd"], 1)

            def outputs(units, A, s, a, at, done):
                dve.wait_ge(A["pv"], s)
                dve.wait_ge(A["exped"], s)
                link(V.reciprocal(rinv[:, 16 * a:16 * a + 16], rsum[:, 16 * a:16 * a + 16]))
                for q in range(NT):
                    V.tensor_tensor(osb[:, q, at:at + 512].rearrange("p (h d) -> p h d", h=H),
                                    bank[4 + q][:, :].rearrange("p (h d) -> p h d", h=H),
                                    bc(rinv[:, 16 * a + 8 * q:16 * a + 8 * q + 8], 2, [P, H, HD]),
                                    ALU.mult).then_inc(done, 1)

            cq = small[:, 3, 0:16]
            for s in range(len(UNITS) + 1):
                if s < len(UNITS):
                    maxes(UNITS, ATT[0], s)
                if s >= 1 and (s - 1) % 2 == 0:
                    turn_copy(UNITS, ATT[0], s - 1)
                if s == 17:
                    outputs(UNITS, ATT[0], 16, 0, 0, o_out)
            outputs(UNITS, ATT[0], 32, 1, 512, o_out)

            def mix_copy(ready, done):
                for c in (1, 3):
                    dve.wait_ge(ready, c + 1)
                    V.tensor_copy(mixT[:, 2 * c:2 * c + 2, :].rearrange("p a t -> p (a t)"), bank[c][:, :]
                                  ).then_inc(done, 1)

            dve.wait_ge(mod_picked, N_MOD)
            link(V.tensor_tensor(mod[:, 16:48, :], bank[6][:, 32:96].rearrange("p (n c) -> p n c", c=2),
                                 bc(v_("b_mod", 16, 32), 2, [P, 32, 2]), ALU.add))
            link(V.scalar_tensor_tensor(A2[:, :], mod[:, 32:40, 0], 1.0, v_("g_ffn", 0, 8), ALU.add, ALU.mult))
            mix_copy(mix_t, mix_d)
            for m in range(KD):
                dve.wait_ge(proj_out, m + 1)
                V.scalar_tensor_tensor(xT[:, m, :], bank[m % 4][:, 0:T], mod[:, 16 + m, 0:1], xT[:, m, :],
                                       ALU.mult, ALU.add).then_inc(resid, 1)

            def norm(r, gain, dst, updated):
                dve.wait_ge(sumsq[r], 1)
                V.tensor_scalar(rstd[:, 0:T], bank[NORM_BANK[r]][:, 0:T], 1.0 / D, EPS, ALU.mult, ALU.add
                                ).then_inc(var[r], 1)
                dve.wait_ge(std[r], 1)
                link(V.reciprocal(rstd[:, 0:T], rstd[:, 0:T]))
                dve.wait_ge(updated, KD)
                for k in range(KD):
                    V.scalar_tensor_tensor(dst[:, k, :], xT[:, k, :], gain(k), rstd[:, 0:T], ALU.mult, ALU.mult
                                           ).then_inc(normed[r], 1)

            norm(1, lambda k: A2[:, k:k + 1], h2, resid)

            S_ = small

            def t3(i, n=4):
                return S_[:, i, 0:2 * n].rearrange("p (q n) -> p q n", q=NT)

            def top(values, scratch, onehot):
                link(V.tensor_reduce(S_[:, 8, 0:2], values, AX, ALU.max))
                link(V.tensor_tensor(scratch, values, bc(S_[:, 8, 0:2], 2, [P, NT, 4]), ALU.is_equal))
                link(V.tensor_tensor(scratch, scratch, bc(desc, 1, [P, NT, 4]), ALU.mult))
                link(V.tensor_reduce(S_[:, 9, 0:2], scratch, AX, ALU.max))
                link(V.tensor_tensor(onehot, scratch, bc(S_[:, 9, 0:2], 2, [P, NT, 4]), ALU.is_equal))

            dve.wait_ge(logits, 1)
            dve.wait_ge(in_row, 48)
            L = small[:, 10:12, 0:20]
            link(V.tensor_tensor(L, bank[6][:, 128:168].rearrange("p (q n) -> p q n", q=NT),
                                 bc(row[:, ROW["b_router"]:ROW["b_router"] + 20], 1, [P, NT, 20]), ALU.add))
            G, E = L[:, :, 0:4], L[:, :, 4:20].rearrange("p q (g e) -> p q g e", g=NG)
            top(G, t3(2), t3(3))
            V.tensor_tensor(t3(1), G, bc(S_[:, 8, 0:2], 2, [P, NT, 4]), ALU.subtract).then_inc(gdiff, 1)
            wide = small[:, 12:14, 0:16].rearrange("p q (g e) -> p q g e", g=NG)
            for q in range(NT):
                link(V.tensor_tensor(wide[:, q], E[:, q], bc(t3(3)[:, q, :], 2, [P, NG, EG]), ALU.mult))
                link(V.tensor_reduce(t3(4)[:, q, :], wide[:, q].rearrange("p g e -> p e g"), AX, ALU.add))
            link(V.tensor_reduce(S_[:, 6, 0:2], t3(4), AX, ALU.max))
            V.tensor_tensor(t3(5), t3(4), bc(S_[:, 6, 0:2], 2, [P, NT, 4]), ALU.subtract).then_inc(ediff, 1)
            dve.wait_ge(gexp, 1)
            link(V.tensor_reduce(S_[:, 7, 0:2], t3(1), AX, ALU.add))
            link(V.reciprocal(S_[:, 7, 0:2], S_[:, 7, 0:2]))
            dve.wait_ge(eexp, 1)
            link(V.tensor_reduce(S_[:, 6, 0:2], t3(5), AX, ALU.add))
            link(V.reciprocal(S_[:, 6, 0:2], S_[:, 6, 0:2]))
            link(V.tensor_tensor(t3(5), t3(5), bc(S_[:, 6, 0:2], 2, [P, NT, 4]), ALU.mult))
            top(t3(5), t3(2), t3(4))
            link(V.scalar_tensor_tensor(t3(1), t3(4), -2.0, t3(5), ALU.mult, ALU.add))
            top(t3(1), t3(2), t3(0))
            link(V.tensor_tensor(t3(0), t3(4), t3(0), ALU.add))
            link(V.tensor_tensor(t3(4), t3(0), t3(5), ALU.mult))
            link(V.tensor_reduce(S_[:, 6, 0:2], t3(4), AX, ALU.add))
            link(V.reciprocal(S_[:, 6, 0:2], S_[:, 6, 0:2]))
            link(V.tensor_tensor(t3(4), t3(4), bc(S_[:, 6, 0:2], 2, [P, NT, 4]), ALU.mult))
            link(V.tensor_tensor(t3(4), t3(4), bc(S_[:, 7, 0:2], 2, [P, NT, 4]), ALU.mult))
            comb = small[:, 15, :].rearrange("p (q g e) -> p q g e", q=NT, g=NG)
            chosen = small[:, 14, :].rearrange("p (q g e) -> p q g e", q=NT, g=NG)
            for q in range(NT):
                V.tensor_tensor(chosen[:, q], bc(t3(3)[:, q, :], 2, [P, NG, EG]), bc(t3(0)[:, q, :], 1, [P, NG, EG]),
                                ALU.mult).then_inc(comb_done, 1)
            for q in range(NT):
                link(V.tensor_tensor(comb[:, q], bc(t3(3)[:, q, :], 2, [P, NG, EG]),
                                     bc(t3(4)[:, q, :], 1, [P, NG, EG]), ALU.mult))
            for b in (1, 3):
                dve.wait_ge(tok_t, b + 1)
                V.tensor_copy(h2tok[:, b // 2, (b % 2) * 512:(b % 2 + 1) * 512], bank[b][:, :]).then_inc(tok_d, 1)
            dve.wait_ge(counted, 1)
            top_n, windows_f = turns_f[:, 0:1], turns_f[:, 1:2]
            link(V.tensor_tensor(posm[:, :], bank[6][:, 192:224], small[:, 14, :], ALU.mult))
            link(V.tensor_scalar(posm[:, :], posm[:, :], -1.0, None, ALU.add))
            link(V.tensor_reduce(top_n, bank[6][:, 224:240], AX, ALU.max))
            link(V.tensor_scalar(windows_f, top_n, float(CAP), 1.0, ALU.is_gt, ALU.add))
            for c in range(2, T // CAP):
                link(V.scalar_tensor_tensor(windows_f, top_n, float(c * CAP), windows_f, ALU.is_gt, ALU.add))
            V.tensor_copy(turns_i[:, :], windows_f).then_inc(turns_ready, 1)
            link(V.memset(place[:, 0, :], 0.0))
            dve.wait_ge(turns_ready, 1)
            windows = dve.value_load(turns_i[0:1, 0:1], min_val=1, max_val=T // CAP)
            with dve.Fori(0, windows) as w:
                dve.wait_ge(scattered, w * 9 + 1)
                V.memset(ysb[:, 0:512], 0.0).then_inc(y_a, 1)
                V.memset(ysb[:, 512:1024], 0.0).then_inc(y_d, 1)
                for q in range(NT):
                    V.tensor_tensor(pick_t[:, q], bc(iota, 1, [P, NE, CAP]),
                                    bc(posm[:, NE * q:NE * (q + 1)], 2, [P, NE, CAP]), ALU.is_equal
                                    ).then_inc(picked_t, 1)
                for q in range(NT):
                    dve.wait_ge(picked_t, w * 2 + (q + 1))
                    ins = V.tensor_tensor(pick_w[:, q], pick_t[:, q],
                                          bc(small[:, 15, NE * q:NE * (q + 1)], 2, [P, NE, CAP]), ALU.mult)
                ins.then_inc(picked, 1)
                V.tensor_scalar(posm[:, :], posm[:, :], -float(CAP), None, ALU.add).then_inc(posm_moved, 1)
                for b in range(4):
                    dve.wait_ge(place_t, w * 4 + (b + 1))
                    V.tensor_copy(place[:, 1 + 2 * b:3 + 2 * b, :].rearrange("p a t -> p (a t)"), bank[b][:, :]
                                  ).then_inc(place_done, 1)
                with dve.Fori(0, NPAIR) as i:
                    dve.wait_ge(posm_moved, w + 1)
                    dve.wait_ge(gathered, w * 16 + i * 2 + 2)
                    V.tensor_copy(xs[:, 4:8, :], bank[1][:, :].rearrange("p (k s) -> p k s", k=4)).then_inc(xs_d, 1)
                    dve.wait_ge(silu_g, w * 8 + i + 1)
                    dve.wait_ge(used, w * 48 + i * 6 + (L_MOE + 4))
                    V.tensor_tensor(hid, hid, bank[3][:, :], ALU.mult).then_inc(hid_made, 1)
                    dve.wait_ge(hid_t, w * 8 + i + 1)
                    V.tensor_copy(hidT[:, :, :].rearrange("p f s -> p (f s)"), bank[0][:, :]).then_inc(hidT_done, 1)
                    dve.wait_ge(used, w * 48 + i * 6 + (L_MOE + 6))
                    dve.wait_ge(scattered, w * 9 + i + 2)
                    V.tensor_copy(ysb[:, 512:1024], bank[3][:, :]).then_inc(y_d, 1)
            dve.wait_ge(scattered, windows * 9 + 1)
            for m in range(KD):
                V.scalar_tensor_tensor(xT[:, m, :], yacc(m), mod[:, 40 + m, 0:1], xT[:, m, :], ALU.mult, ALU.add
                                       ).then_inc(resid_m, 1)
            norm(2, lambda k: v_("g_final", k), xT, resid_m)
            norm(3, lambda k: v_("g_mix2", k), h2, normed[2])

            f2, fa, lfr = small[:, 0, 0:16], small[:, 1, 0:16], small[:, 2, 0:16]

            def out_of_psum2(n):
                kind, i, e = PROD2[n]
                src = bank[n % 4]
                dve.wait_ge(prod2_ready, n + 1)
                if kind == "f":
                    V.tensor_tensor(f2.rearrange("p (q h) -> p q h", q=NT),
                                    src[:, 0:16].rearrange("p (q h) -> p q h", q=NT),
                                    bc(row[:, ROW["f_bias"]:ROW["f_bias"] + 8], 1, [P, NT, 8]), ALU.add
                                    ).then_inc(prod2_d, 1)
                    dve.wait_ge(prod2_d, 1)
                    V.scalar_tensor_tensor(fa, f2, -1.0, f2, ALU.mult, ALU.min).then_inc(f_abs, 1)
                    link(V.tensor_scalar(f2, f2, 0.0, None, ALU.min))
                    dve.wait_ge(f_ln, 1)
                    V.tensor_tensor(lfr, f2, fa, ALU.subtract).then_inc(lf_done, 1)
                    return
                if kind == "q":
                    ins = V.tensor_scalar(q2[:, i, :], src[:, 0:T], HD ** -0.5, None, ALU.mult)
                elif kind == "k":
                    ins = V.tensor_copy(k2[:, i, :], src[:, 0:T])
                elif kind == "cq":
                    ins = V.tensor_copy(cq, src[:, 0:16])
                ins.then_inc(prod2_d, 1)

            def heads(t):
                return t.rearrange("p (h d) -> p h d", h=H)

            def layer_norm():
                dve.wait_ge(prod2_a, 4)
                mu, vr = small[:, 5, 0:16], small[:, 6, 0:16]
                v3 = vg[:, :, :].rearrange("p n (h d) -> p (n h) d", h=H)
                l3 = lnt[:, :, :].rearrange("p n (h d) -> p (n h) d", h=H)
                link(V.tensor_reduce(mu, v3, AX, ALU.add))
                link(V.tensor_scalar(mu, mu, 1.0 / HD, None, ALU.mult))
                link(V.tensor_tensor(v3, v3, bc(mu, 2, [P, 16, HD]), ALU.subtract))
                link(V.tensor_tensor(l3, v3, v3, ALU.mult))
                link(V.tensor_reduce(vr, l3, AX, ALU.add))
                V.tensor_scalar(vr, vr, 1.0 / HD, EPS, ALU.mult, ALU.add).then_inc(ln_var, 1)

            def layer_norm_end():
                vr = small[:, 6, 0:16]
                v3 = vg[:, :, :].rearrange("p n (h d) -> p (n h) d", h=H)
                dve.wait_ge(ln_std, 1)
                link(V.reciprocal(vr, vr))
                link(V.tensor_tensor(v3, v3, bc(vr, 2, [P, 16, HD]), ALU.mult))
                V.tensor_tensor(vg[:, :, :], vg[:, :, :], bc(row[:, ROW["sg_ln"]:ROW["sg_ln"] + 512], 1, [P, NT, 512]),
                                ALU.mult).then_inc(vn_done, 1)

            for n, (kind, i, e) in enumerate(PROD2):
                if kind == "k" and i == 0:
                    layer_norm()
                if e == "D":
                    out_of_psum2(n)
            layer_norm_end()
            for q in range(NT):
                dve.wait_ge(sg_mm, q + 1)
                link(V.tensor_tensor(heads(osb[:, q, 0:512]), heads(bank[6 + q][:, :]),
                                     bc(v_("sg_b", 0, 8), 2, [P, H, HD]), ALU.add))
                V.tensor_tensor(osb[:, q, 0:512], osb[:, q, 0:512], ug[:, q, :], ALU.mult).then_inc(sg_done, 1)
            dve.wait_ge(prod2_d, total(PROD2, "D"))
            for s in range(len(UNITS2) + 1):
                if s < len(UNITS2):
                    maxes(UNITS2, ATT[1], s)
                if s >= 1 and (s - 1) % 2 == 0:
                    turn_copy(UNITS2, ATT[1], s - 1)
            outputs(UNITS2, ATT[1], 16, 2, 512, o2_out)
            mix_copy(mix2_t, mix2_d)
            for m in range(KD):
                dve.wait_ge(proj2_out, m + 1)
                V.tensor_tensor(xT[:, m, :], bank[m % 4][:, 0:T], xT[:, m, :], ALU.add).then_inc(resid2, 1)
            norm(4, lambda k: v_("g_ffn2", k), h2, resid2)

            def taps(i, j):
                b = j % 2
                dve.wait_ge(conv0, i * 8 + (2 * j + 2))
                for g in range(2):
                    y, a = yconv[:, b, g, :], bank[j % 4][:, g * T:(g + 1) * T]
                    V.scalar_tensor_tensor(y[:, 1:T], a[:, 0:T - 1],
                                           vec[:, bass.ds(i * 4 + (j + 22 * g + VEC["w_conv"] + 44), 1)], y[:, 1:T],
                                           ALU.mult, ALU.add).then_inc(tap1, 1)
                for g in range(2):
                    y, a = yconv[:, b, g, :], bank[j % 4][:, g * T:(g + 1) * T]
                    dve.wait_ge(tap1, i * 8 + (2 * j + g + 1))
                    V.scalar_tensor_tensor(y[:, 2:T], a[:, 0:T - 2],
                                           vec[:, bass.ds(i * 4 + (j + 22 * g + VEC["w_conv"]), 1)], y[:, 2:T],
                                           ALU.mult, ALU.add).then_inc(tap2, 1)
                dve.wait_ge(tap2, i * 8 + (2 * j + 2))
                dve.wait_ge(silu_f, i * 4 + (j + 1))
                V.tensor_tensor(hidF[:, i * 4 + j, :], yconv[:, b, 0, :], yconv[:, b, 1, :], ALU.mult
                                ).then_inc(hid_done, 1)

            with dve.Fori(0, NP // 4) as i:
                for j in range(4):
                    taps(i, j)
            for j in range(NP % 4):
                taps(NP // 4, j)
            dve.wait_ge(down_done, 1)
            for m in range(KD):
                V.tensor_tensor(xT[:, m, :], yacc(m), xT[:, m, :], ALU.add).then_inc(resid3, 1)
            norm(5, lambda k: v_("g_final2", k), outT, resid3)


def kernel(**inputs):
    import numpy as _np
    import concourse.bacc as _bacc
    from concourse import mybir as _mybir
    from concourse.bass_utils import run_bass_kernel_spmd as _run

    a = {k: _np.asarray(v) for k, v in inputs.items()}

    def tiles(v):
        return v.reshape(-1, P).T

    def featuremajor(x):
        return _np.ascontiguousarray(x.T.reshape(KD, P, T).transpose(1, 0, 2))

    vec = _np.concatenate([
        _np.stack([tiles(a["c"][0]), tiles(a["c_ctx"])], axis=2).reshape(P, 16), tiles(a["b_mod"][0]),
        tiles(a["norm_attn_g"][0]), tiles(a["norm_ffn_g"][0]), tiles(a["q_a_norm_g"][0]), tiles(a["kv_a_norm_g"][0]),
        tiles(a["final_norm_g"]), tiles(a["norm_mix_g_2"][0]), tiles(a["norm_ffn_g_2"][0]), tiles(a["b_conv_2"][0]),
        tiles(a["w_conv_2"][0].reshape(-1)), tiles(a["norm_final_g_2"]), a["sg_b_2"][0].T], axis=1)
    row = _np.concatenate([a["b_router_group"][0], a["b_router_expert"][0], a["f_bias_2"][0],
                           a["sg_ln_g_2"][0].reshape(-1)])[None]
    wr = _np.concatenate([a["w_router_group"][0], a["w_router_expert"][0]], axis=1).reshape(KD, P, 20)
    i, j = _np.arange(P)[:, None], _np.arange(P)[None]
    con = _np.zeros((P, NCON), _np.float32)
    con[:, CON["ident"]:CON["ident"] + P] = i == j
    con[:, CON["tri"]:CON["tri"] + P] = _np.where(j <= i, 0.0, -BIG)
    con[:, CON["upper"]:CON["upper"] + P] = i <= j
    con[:, CON["ones"]:CON["ones"] + P] = 1.0
    col, key = (i % GRID_W), _np.arange(GRID_W)[None]
    start = _np.clip(col - 8, 0, GRID_W - 16)
    con[:, CON["namask"]:CON["namask"] + GRID_W] = _np.where((key >= start) & (key < start + 16), 0.0, -BIG)
    r, m = _np.arange(32)[:, None], _np.arange(32)[None]
    con[64:96, CON["rot"]:CON["rot"] + 32] = _np.where(r == m + 16, -1.0, 0.0) + _np.where(r == m - 16, 1.0, 0.0)
    half = ROPE // 2
    inv = (_np.float32(10000.0) ** (-_np.arange(0, half, 2, dtype=_np.float32) / _np.float32(half))).astype(_np.float32)
    pos = _np.arange(T)
    ang = _np.concatenate([(pos // GRID_W).astype(_np.float32)[:, None] * inv,
                           (pos % GRID_W).astype(_np.float32)[:, None] * inv], axis=1).T
    con[64:96, CON["cos"]:CON["cos"] + 512] = 1.0
    con[64:96, CON["cos"]:CON["cos"] + T] = _np.tile(_np.cos(ang), (2, 1))
    con[64:96, CON["sin"]:CON["sin"] + T] = _np.tile(_np.sin(ang), (2, 1))
    con[:, CON["desc"]:CON["desc"] + 4] = [4.0, 3.0, 2.0, 1.0]
    con[:, CON["iota"]:CON["iota"] + CAP] = _np.arange(CAP)
    con[:, CON["pick"]] = i[:, 0] % 32 == 0
    con[:, CON["pick"] + 1] = i[:, 0] % 32 == 1
    q, k = _np.arange(T), _np.arange(T)
    dr = k[None] // GRID_W - q[:, None] // GRID_W + 7
    dc = _np.clip(k[None] % GRID_W - q[:, None] % GRID_W + 15, 0, 30)
    bias = a["na_rel_bias"][0][:, dr, dc].reshape(H, NT, P, T).transpose(2, 0, 1, 3).reshape(P, -1)

    feeds = {
        "xT": featuremajor(a["x"][0]), "ctxT": featuremajor(a["ctx"][0]), "vec": vec, "row": row, "con": con,
        "w_mod": a["w_mod"][0], "w_in": a["w_in"][0], "w_uq": a["w_uq"][0], "w_ukv": a["w_ukv"][0],
        "bias": bias, "w_out": a["w_out"][0], "wr": wr.transpose(1, 0, 2),
        "w_gate": a["w_gate"][0], "w_up": a["w_up"][0], "w_down": a["w_down"][0],
        "w_in2": a["w_in_2"][0], "wf": a["w_in_2"][0][:, 2560:].reshape(KD, P, 8).transpose(1, 0, 2),
        "sgw": a["sg_w_2"][0].transpose(2, 0, 1), "w_out2": a["w_out_2"][0],
        "w_up2": a["w_up_2"][0], "w_down2": a["w_down_2"][0],
    }
    nc = _bacc.Bacc("TRN2", target_bir_lowering=False, num_devices=1)
    arrays, args = {}, []
    for name, v in feeds.items():
        v = _np.ascontiguousarray(v)
        arrays[f"in_{name}"] = v
        args.append(nc.dram_tensor(f"in_{name}", v.shape, _mybir.dt.from_np(v.dtype), kind="ExternalInput").ap())
    args.append(nc.dram_tensor("out_T", (P, KD, T), F32, kind="ExternalOutput").ap())
    block_pair_kernel(nc, *args)
    got = _run(nc, [arrays], core_ids=[0]).results[0]["out_T"]
    return _np.ascontiguousarray(got.transpose(1, 0, 2).reshape(D, T).T)[None]
```

```python
from contextlib import ExitStack

import concourse.bass as bass
from concourse import mybir

P = 128
T = 256
D = 1024
KD = D // P
NT = T // P
H = 8
HD = 64
QK = 96
NOPE, ROPE = 64, 32
QL, KVL = 384, 256
GRID_W = 64
NE, NG, EG = 16, 4, 4
FE = 512
FF = 2816
NP = FF // P
EPS = 1e-6
BIG = 1e30

ALU = mybir.AluOpType
ACT = mybir.ActivationFunctionType
F32 = mybir.dt.float32
F32R = mybir.dt.float32r
AX = mybir.AxisListType.X

SLOTS = 6
SLOT = 4096
CAP = 64
NPAIR = NE // 2
N_MOD = 12
L_QL, L_KVL, L_NAQ, L_NAK, L_NAV, L_UQ, L_UKV = range(4, 11)
L_MOD2 = 11
L_OUT = 19
L_MOE = 21
L_IN2 = L_MOE + 3 * NE
L_OUT2 = L_IN2 + 5
L_UP = L_OUT2 + 2
N_UP = NP // 2
L_DOWN = L_UP + N_UP
N_DOWN = (NP + 3) // 4
N_LOADS = L_DOWN + N_DOWN


def slot_of(n):
    if n < L_MOE:
        return (3, 4, 5, 2,  3, 4, 5, 3, 4, 5, 3,  4, 5, 3, 4, 5, 3, 4, 5,  3, 4)[n]
    if n < L_IN2:
        return (3, 4, 5, 0, 1, 2)[(n - L_MOE) % 6]
    if n < L_UP:
        return (3, 4, 5, 2, 3,  4, 5)[n - L_IN2]
    if n < L_DOWN:
        return 2 + (n - L_UP) % 2
    return (4, 5, 3, 2, 4, 5)[n - L_DOWN]


def last_in_slot(n):
    before = [m for m in range(n) if slot_of(m) == slot_of(n)]
    return before[-1] if before else None


def dmas_of(n):
    return 2 if L_UP <= n < L_DOWN else 1


def landed_count(n):
    first = L_IN2 if n >= L_IN2 else 0
    return 16 * sum(dmas_of(m) for m in range(first, n + 1) if slot_of(m) == slot_of(n))


def columns(widths):
    at, out = 0, {}
    for name, w in widths:
        out[name] = at
        at += w
    return out, at


VEC, NVEC = columns([("c", 16), ("b_mod", 48), ("g_attn", 8), ("g_ffn", 8), ("g_qa", 3), ("g_kva", 2),
                     ("g_final", 8), ("g_mix2", 8), ("g_ffn2", 8), ("b_conv", 44), ("w_conv", 132),
                     ("g_final2", 8), ("sg_b", 8)])
ROW, NROW = columns([("b_router", 20), ("f_bias", 8), ("sg_ln", 512)])
CON, NCON = columns([("upper", 128), ("ones", 128), ("pick", 2), ("pick20", 20), ("ident", 128), ("tri", 128),
                     ("namask", 64), ("rot", 32), ("cos", 512), ("sin", 512), ("desc", 4), ("iota", 64)])
CON_FIRST = CON["ident"]

PROD = ([("ql", i, "AD"[i % 2]) for i in range(3)] + [("kvl", 0, "D"), ("kvl", 1, "A"), ("kr", 0, "D")]
        + [("naq", i, "AD"[i % 2]) for i in range(4)]
        + [("nak", i, "AD"[i % 2]) for i in range(4)] + [("nav", i, "AD"[i % 2]) for i in range(4)]
        + [("rotk", 0, "D")] + [("uq", i, "AD"[i % 2]) for i in range(8)] + [("kn", i, "A") for i in range(4)]
        + [p for i in range(4) for p in (("rotq", i, "D"), ("kn", i + 4, "A"))]
        + [("vm", i, "AD"[i % 2]) for i in range(4)])
N_BEFORE_LAT = 10
PROD2 = ([("f", 0, "D")] + [("u", i, "A") for i in range(2)] + [("va", i, "A") for i in range(2)]
         + [("q", i, "D") for i in range(4)] + [("cq", 0, "D")] + [("nck", i, "A") for i in range(4)]
         + [("k", i, "D") for i in range(4)] + [("v", i, "A") for i in range(2)])


def chunks(prod, loads, narrow):
    out = []
    for n, (kind, i, _e) in enumerate(prod):
        if kind in narrow:
            first, cols = narrow[kind]
            out.append((loads[kind], 0, KD, first + i * cols, cols, n))
        elif kind in loads and i == 0:
            last = max(m for m, p in enumerate(prod) if p[0] == kind)
            out += [(loads[kind], 2 * j, 2, 0, 512, last) for j in range(4)]
    return out


CHUNK1 = chunks(PROD, {"ql": L_QL, "kvl": L_KVL, "kr": L_KVL, "naq": L_NAQ, "nak": L_NAK, "nav": L_NAV},
                {"ql": (0, P), "kvl": (0, P), "kr": (192, QK), "naq": (0, P), "nak": (0, P)})
CHUNK2 = chunks(PROD2, {"u": L_IN2, "va": L_IN2 + 1, "q": L_IN2 + 2, "k": L_IN2 + 3, "v": L_IN2 + 4},
                {"q": (0, P), "k": (0, P)})


OUT1, OUT2 = len(CHUNK1), len(CHUNK2)
CHUNK1 += [(L_OUT + m // 4, 0, KD, (m % 4) * P, P, None) for m in range(KD)]
CHUNK2 += [(L_OUT2 + m // 4, 0, KD, (m % 4) * P, P, None) for m in range(KD)]


def chunks_of(chunk, n):
    return [c for c in range(len(chunk)) if chunk[c][5] == n]


def chunks_after(chunk, n):
    return [c + 4 for c in chunks_of(chunk, n) if chunk[c + 4][5] is not None]


def copied(prod, n):
    e = prod[n][2]
    return e, sum(1 for p in prod[:n + 1] if p[2] == e)


def total(prod, e):
    return sum(1 for p in prod if p[2] == e)


UNITS = [(a, h, q, 4) for a in range(2) for h in range(H) for q in range(NT)]
UNITS2 = [(2, h, q, q + 1) for h in range(H) for q in range(NT)]


def block_pair_kernel(nc, xT_d, ctxT_d, vec_d, row_d, con_d, w_mod, w_in, w_uq, w_ukv, bias_d, w_out,
                      wr_d, w_gate, w_up, w_down, w_in2, wf_d, sgw_d, w_out2, w_up2, w_down2, out_d):
    with ExitStack() as ctx:
        def sb(name, shape):
            return ctx.enter_context(nc.sbuf_tensor(name, shape, F32))

        def sem(name):
            return ctx.enter_context(nc.semaphore(name))

        bank = [ctx.enter_context(nc.psum_tensor(f"bank{i}", [P, 512], F32)) for i in range(8)]

        with ExitStack() as first:
            def sb_first(name, shape):
                return first.enter_context(nc.sbuf_tensor(name, shape, F32))

            ring = sb_first("ring", [P, SLOTS, SLOT])
            mixT = sb_first("mixT", [P, KD, T])
            osb = sb_first("osb", [P, NT, D])
            big = sb_first("big", [P, 4096])
            arena = sb_first("arena", [P, 9216])

        with ExitStack() as early:
            def sb_early(name, shape):
                return early.enter_context(nc.sbuf_tensor(name, shape, F32R))

            sb_early("below_slot_2", [P, 2, SLOT])
            hT_lo = sb_early("hT_lo", [P, KD, 2 * T])
            sb_early("below_big", [P, 3 * SLOT + 2 * KD * T])
            hT_hi = sb_early("hT_hi", [P, KD, 2 * T])

        def sb_r(name, shape):
            return ctx.enter_context(nc.sbuf_tensor(name, shape, F32R))

        w_hi = sb_r("w_hi", [P, 2, 2, 1024])
        w_lo = sb_r("w_lo", [P, 2, 2, 1024])
        sb_r("over_slots_2_to_5", [P, 4, SLOT])
        h2_hi = sb_r("h2_hi", [P, KD, T])
        h2_lo = sb_r("h2_lo", [P, KD, T])
        hid_hi = sb_r("hid_hi", [P, NP, T])
        hid_lo = sb_r("hid_lo", [P, NP, T])
        sb_r("over_the_rest_of_arena", [P, 4096 + 9216 - 2 * NP * T])
        xT = sb("xT", [P, KD, T])
        att = sb("att", [P, 4, 512])
        con = sb("con", [P, NCON])
        row = sb("row", [P, NROW])
        vec = sb("vec", [P, NVEC])
        lat = sb("lat", [P, 1792])
        rstd = sb("rstd", [P, 512])
        rs = sb("rs", [P, 8])
        g_both = sb("g_both", [P, KD])
        g_sq = sb("g_sq", [P, KD, 2])
        wr = sb("wr", [P, KD, 32])
        wf = sb("wf", [P, KD, 8])
        cs = sb("cs", [P, KD, 32])
        mod = sb("mod", [P, 48, 2])
        A1 = sb("A1", [P, KD, 2])
        A2 = sb("A2", [P, KD])
        nmax = sb("nmax", [P, 48])
        rsum = sb("rsum", [P, 48])
        rinv = sb("rinv", [P, 48])
        small = sb("small", [P, 16, 32])
        posm = sb("posm", [P, 2 * NE])
        turns_f = sb("turns_f", [P, 3])
        tiny = sb("tiny", [P, 16])
        turns_i = ctx.enter_context(nc.sbuf_tensor("turns_i", [P, 2], mybir.dt.int32))

        ctxT = osb[:, :, :].rearrange("p a (b t) -> p (a b) t", t=T)
        hT = arena[:, 0:4096].rearrange("p (k t) -> p k t", t=2 * T)
        qT = big[0:QK, 0:2048].rearrange("p (h t) -> p h t", t=T)
        vm = big[:, 2048:4096].rearrange("p (j n) -> p j n", n=512)
        h2 = big[:, 0:2048].rearrange("p (k t) -> p k t", t=T)
        sgw = big[:, 2048:3072].rearrange("p (h t) -> p h t", t=P)
        outT = ring[:, 2, 0:2048].rearrange("p (k t) -> p k t", t=T)
        kT = arena[0:QK, 0:4096].rearrange("p (h t) -> p h t", t=2 * T)
        bias = arena[:, 0:4096].rearrange("p (h q n) -> p h q n", q=NT, n=T)
        modp = mixT[:, :, :].rearrange("p a t -> p (a t)")
        modp2 = lat[:, 0:512]
        logit_parts = lat[:, 512:768]
        h2tok = osb
        pick_t = arena[:, 0:2048].rearrange("p (q e s) -> p q e s", q=NT, s=CAP)
        pick_w = arena[:, 2048:2304].rearrange("p (q e s) -> p q e s", q=NT, s=CAP)
        place = arena[:, 4096:6400].rearrange("p (i t) -> p i t", t=T)
        ysb = arena[:, 6400:7424]
        xs = att[:, 0:2, :].rearrange("p a (k s) -> p (a k) s", s=2 * CAP)
        hid = att[:, 2, :]
        hidT = att[:, 3, :].rearrange("p (f s) -> p f s", s=2 * CAP)
        naq = arena[:, 4096:5120].rearrange("p (i t) -> p i t", t=T)
        nak = arena[:, 5120:7168].rearrange("p (i t) -> p i t", t=2 * T)
        nav = arena[:, 7168:9216].rearrange("p (j n) -> p j n", n=512)
        nck = arena[:, 0:2048].rearrange("p (h t) -> p h t", t=T)
        nck0 = arena[:, 2048:3072].rearrange("p (h t) -> p h t", t=P)
        lnt = arena[:, 3072:4096].rearrange("p (n c) -> p n c", c=512)
        ug = arena[:, 4096:5120].rearrange("p (n c) -> p n c", c=512)
        vg = arena[:, 5120:6144].rearrange("p (n c) -> p n c", c=512)
        q2 = arena[:, 6144:7168].rearrange("p (i t) -> p i t", t=T)
        k2 = arena[:, 7168:8192].rearrange("p (i t) -> p i t", t=T)
        v2 = arena[:, 8192:9216].rearrange("p (n c) -> p n c", c=512)
        yconv = lat[:, 0:1024].rearrange("p (b g t) -> p b g t", b=2, t=T)
        qlat = lat[:, 0:768].rearrange("p (i t) -> p i t", t=T)
        kvlat = lat[:, 768:1792].rearrange("p (i t) -> p i t", t=2 * T)
        rq = mixT[:, 0, :]
        rkv = mixT[:, 2:4, :].rearrange("p a t -> p (a t)")
        kr = mixT[64:96, 4:6, :].rearrange("p a t -> p (a t)")
        rtmp = mixT[64:96, 6:8, :].rearrange("p a t -> p (a t)")
        attf = att[:, :, :].rearrange("p a b -> p (a b)")
        sq = attf.rearrange("p (k t) -> p k t", t=T)

        ident = con[:, CON["ident"]:CON["ident"] + P]
        tri = con[:, CON["tri"]:CON["tri"] + P]
        upper = con[:, CON["upper"]:CON["upper"] + P]
        upper_ones = con[:, CON["upper"]:CON["upper"] + 2 * P]
        ones = con[:, CON["ones"]:CON["ones"] + P]
        namask = con[:, CON["namask"]:CON["namask"] + 64]
        rot = con[64:96, CON["rot"]:CON["rot"] + 32]
        cos = con[64:96, CON["cos"]:CON["cos"] + 512]
        sin = con[64:96, CON["sin"]:CON["sin"] + 512]
        iota = con[:, CON["iota"]:CON["iota"] + CAP]
        pick20 = con[:, CON["pick20"]:CON["pick20"] + 20]
        pick = con[:, CON["pick"]:CON["pick"] + 2]
        desc = con[:, CON["desc"]:CON["desc"] + 4]

        def ptT(a, h):
            if a < 2:
                return osb[:, h % 2, :].rearrange("p (j t) -> p j t", t=T)
            return big[:, 3072 + 512 * (h % 2):3584 + 512 * (h % 2)].rearrange("p (j t) -> p j t", t=T)

        def chunk_src(chunk, c):
            load, k, nk, col, cols, _ = chunk[c]
            width = {L_QL: QL, L_KVL: 288}.get(load, 512)
            w = ring[:, slot_of(load), 0:KD * width].rearrange("p (k n) -> p k n", k=KD)
            return w[:, k:k + nk, col:col + cols]

        def chunk_part(part, chunk, c):
            _, _, nk, _, cols, _ = chunk[c]
            return part[:, (c % 4) // 2, c % 2, 0:nk * cols].rearrange("p (k n) -> p k n", k=nk)

        def granule(part, j, half):
            return part[:, j % 2, half, :].rearrange("p (k n) -> p k n", n=P)

        def up_half_of(j, half):
            w = ring[:, 2 + j // 2, :].rearrange("p (k g n) -> p k g n", k=KD, g=2)
            return w[:, :, half, (j % 2) * P:(j % 2 + 1) * P]

        def down_half_of(d, half):
            at = (2 * (d % 2) + half) * D
            return ring[:, slot_of(L_DOWN + d // 2), at:at + D]

        mix_lo = (hT_lo[:, :, 0:T], hid_hi[:, 0:KD, :])

        def v_(name, i, n=1):
            return vec[:, VEC[name] + i:VEC[name] + i + n]

        landed = [sem(f"landed{i}") for i in range(SLOTS)]
        used = sem("used")
        landed2 = [sem(f"landed2_{i}") for i in range(SLOTS)]
        mod_streamed, mod_copied, mod_picked = sem("mod_streamed"), sem("mod_copied"), sem("mod_picked")
        mod_first = sem("mod_first")

        in_x, in_ctx, in_vec, in_con, in_row = sem("in_x"), sem("in_ctx"), sem("in_vec"), sem("in_con"), sem("in_row")
        in_sg, in_bias = sem("in_sg"), sem("in_bias")
        silu_c = sem("silu_c")
        vstep, astep = sem("vstep"), sem("astep")
        squares = [sem(f"squares{i}") for i in range(5)]
        sumsq = [sem(f"sumsq{i}") for i in range(5)]
        var = [sem(f"var{i}") for i in range(5)]
        std = [sem(f"std{i}") for i in range(5)]
        normed = [sem(f"normed{i}") for i in range(5)]
        in_rest = sem("in_rest")
        spread, y_made = sem("spread"), sem("y_made")
        shifted, shifted_lo = [sem(f"shifted{i}") for i in range(2)], sem("shifted_lo")
        chunk_hi, chunk_lo = [sem(f"chunk_hi{i}") for i in range(2)], [sem(f"chunk_lo{i}") for i in range(2)]
        strip_read = sem("strip_read")
        prod_ready, prod_a, prod_d = sem("prod_ready"), sem("prod_a"), sem("prod_d")
        lat_sq, lat_ss, lat_var, lat_std, lat_done = (sem("lat_sq"), sem("lat_ss"), sem("lat_var"),
                                                      sem("lat_std"), sem("lat_done"))
        kr_done, kr_spread = sem("kr_done"), sem("kr_spread")
        ATT = [{n: sem(f"{n}{i}") for n in ("scores", "maxed", "exped", "scaled", "turned", "pt", "pv", "out")}
               for i in range(2)]
        bias_ready = sem("bias_ready")
        proj_out, resid = sem("proj_out"), sem("resid")
        logits_part, logits_copied = sem("logits_part"), sem("logits_copied")
        logits, gdiff, gexp, ediff, eexp = sem("logits"), sem("gdiff"), sem("gexp"), sem("ediff"), sem("eexp")
        comb_done, counted, turns_ready = sem("comb_done"), sem("counted"), sem("turns_ready")
        tok_t, tok_a, tok_d = sem("tok_t"), sem("tok_a"), sem("tok_d")
        picked_t, posm_moved = sem("picked_t"), sem("posm_moved")
        picked, place_t, place_done = sem("picked"), sem("place_t"), sem("place_done")
        gathered, xs_a, xs_d = sem("gathered"), sem("xs_a"), sem("xs_d")
        silu_g, hid_made, hid_t, hidT_done = sem("silu_g"), sem("hid_made"), sem("hid_t"), sem("hidT_done")
        y_half, y_a, y_d, scattered = sem("y_half"), sem("y_a"), sem("y_d"), sem("scattered")
        resid_m = sem("resid_m")
        prod2_ready, prod2_a, prod2_d = sem("prod2_ready"), sem("prod2_a"), sem("prod2_d")
        f_abs, f_ln, lf_done, nck_done = sem("f_abs"), sem("f_ln"), sem("lf_done"), sem("nck_done")
        sg_zero, ln_var, ln_std, vn_done, sg_mm, sg_done = (sem("sg_zero"), sem("ln_var"), sem("ln_std"),
                                                            sem("vn_done"), sem("sg_mm"), sem("sg_done"))
        sg_t, sg_a, sg_d = sem("sg_t"), sem("sg_a"), sem("sg_d")
        proj2_out, resid2 = sem("proj2_out"), sem("resid2")
        wide_hi, wide_lo = sem("wide_hi"), sem("wide_lo")
        h2_hi_done, h2_lo_done = sem("h2_hi_done"), sem("h2_lo_done")
        up_half, conv0, tap1, tap2, silu_f = (sem("up_half"), sem("conv0"), sem("tap1"), sem("tap2"),
                                              sem("silu_f"))
        hid_done, hid_hi_done, hid_lo_done = sem("hid_done"), sem("hid_hi_done"), sem("hid_lo_done")
        down_half = sem("down_half")
        resid3, out_done = sem("resid3"), sem("out_done")

        def through(n):
            def product(prod, kind, i):
                return [p[:2] for p in prod].index((kind, i)) + 1

            if n < 4:
                return mod_streamed, n + 1
            if n < L_UQ:
                return chunk_lo[0], max(c for c in range(len(CHUNK1)) if CHUNK1[c][0] == n) + 1
            if n < L_MOD2:
                return prod_ready, product(PROD, *{L_UQ: ("uq", 7), L_UKV: ("vm", 3)}[n])
            if n < L_OUT:
                return mod_streamed, n - L_MOD2 + 5
            if n < L_MOE:
                return chunk_lo[0], OUT1 + 4 * (n - L_OUT + 1)
            if n < L_OUT2:
                return chunk_lo[1], 4 * (n - L_IN2 + 1)
            if n < L_UP:
                return chunk_lo[1], OUT2 + 4 * (n - L_OUT2 + 1)
            return wide_lo, 4 * (n - L_UP + 1)

        block = ctx.enter_context(nc.Block())

        def yacc(m):
            return bank[4 + m // 2][:, (m % 2) * T:(m % 2 + 1) * T]

        NORM_BANK = [7, 7, 0, 7, 0]
        NAV_DONE = [p[:2] for p in PROD].index(("nav", 3)) + 1

        @block.sync
        def _(sp):
            def issue(n, dst_cols, shape_k, src):
                prev = last_in_slot(n)
                if prev is not None and not L_MOE <= prev < L_IN2:
                    sp.wait_ge(*through(prev))
                dst = ring[:, slot_of(n), 0:dst_cols].rearrange("p (k n) -> p k n", k=shape_k)
                sp.dma_start(dst, src).then_inc((landed2 if n >= L_IN2 else landed)[slot_of(n)], 16)

            wm = w_mod.rearrange("(k p) n -> p k n", p=P)
            wi = w_in.rearrange("(k p) n -> p k n", p=P)
            wi2 = w_in2.rearrange("(k p) n -> p k n", p=P)
            wo = w_out.rearrange("(k p) n -> p k n", p=P)
            wo2 = w_out2.rearrange("(k p) n -> p k n", p=P)
            wu2 = w_up2.rearrange("(k p) (g n) -> p k g n", p=P, g=2)
            wd2 = w_down2.rearrange("(k p) n -> p k n", p=P)
            sp.dma_start(xT[:, :, :], xT_d).then_inc(in_x, 16)
            for n in range(4):
                issue(n, 4096, KD, wm[:, :, n * 512:(n + 1) * 512])
            sp.dma_start(ctxT, ctxT_d).then_inc(in_ctx, 16)
            issue(L_QL, KD * QL, KD, wi[:, :, 0:QL])
            issue(L_KVL, KD * 288, KD, wi[:, :, 896:1184])
            sp.dma_start(con[:, CON_FIRST:NCON], con_d[:, CON_FIRST:NCON]).then_inc(in_rest, 16)
            issue(L_NAQ, 4096, KD, wi[:, :, 384:896])
            sp.dma_start(row[:, :], row_d.broadcast_to([P, NROW])).then_inc(in_row, 16)
            sp.dma_start(wr[:, :, :], wr_d).then_inc(in_row, 16)
            sp.dma_start(wf[:, :, :], wf_d).then_inc(in_row, 16)
            issue(L_NAK, 4096, KD, wi[:, :, 1184:1696])
            issue(L_NAV, 4096, KD, wi[:, :, 1696:2208])
            issue(L_UQ, 3 * 768, 3, w_uq.rearrange("(k p) n -> p k n", p=P))
            issue(L_UKV, 2 * 1024, 2, w_ukv.rearrange("(k p) n -> p k n", p=P))
            for n in range(4, N_MOD):
                issue(L_MOD2 + n - 4, 4096, KD, wm[:, :, n * 512:(n + 1) * 512])
            for n in range(2):
                issue(L_OUT + n, 4096, KD, wo[:, :, n * 512:(n + 1) * 512])
            def expert_loads(i, before=None):
                for j in range(6):
                    n = L_MOE + j
                    if before is None:
                        sp.wait_ge(*((proj_out, KD) if slot_of(n) < 3 else through(last_in_slot(n))))
                    else:
                        sp.wait_ge(used, before + (j + 1))
                    src = (w_gate, w_up, w_down)[j // 2][i * 2 + j % 2]
                    sp.dma_start(ring[:, slot_of(n), :].rearrange("p (k n) -> p k n", k=4 if j >= 4 else KD),
                                 src.rearrange("(k p) n -> p k n", p=P)).then_inc(landed[slot_of(n)], 16)

            expert_loads(0)
            with sp.Fori(0, NPAIR - 1) as i:
                expert_loads(i + 1, i * 6)
            sp.wait_ge(turns_ready, 1)
            more = sp.value_load(turns_i[0:1, 1:2], min_val=0, max_val=T // CAP - 1)
            with sp.If(more > 0):
                with sp.Fori(0, more) as w:
                    with sp.Fori(0, NPAIR) as i:
                        expert_loads(i, w * 48 + i * 6 + 42)
            for n in range(5):
                if n < 4:
                    sp.wait_ge(used, more * 48 + (43, 44, 45, 48)[n])
                issue(L_IN2 + n, 4096, KD, wi2[:, :, n * 512:(n + 1) * 512])
            for n in range(2):
                issue(L_OUT2 + n, 4096, KD, wo2[:, :, n * 512:(n + 1) * 512])

            def up_load(n, at):
                for g in range(2):
                    sp.dma_start(ring[:, slot_of(n), :].rearrange("p (k g n) -> p k g n", k=KD, g=2)[:, :, g, :],
                                 wu2[:, :, g, bass.ds(at, 256)]).then_inc(landed2[slot_of(n)], 16)
            for e in range(2):
                sp.wait_ge(*through(last_in_slot(L_UP + e)))
                up_load(L_UP + e, 256 * e)
            with sp.Fori(0, (N_UP - 1) // 2 - 1) as i:
                for e in range(2):
                    sp.wait_ge(wide_lo, i * 8 + (4 * e + 4))
                    up_load(L_UP + e, i * 512 + (512 + 256 * e))
            sp.wait_ge(*through(last_in_slot(L_UP + N_UP - 1)))
            up_load(L_UP + N_UP - 1, 256 * (N_UP - 1))
            for n in range(N_DOWN):
                k = min(4, NP - 4 * n)
                issue(L_DOWN + n, k * D, k, wd2[:, 4 * n:4 * n + k, :])
            for m in range(KD):
                sp.wait_ge(normed[4], m + 1)
                sp.dma_start(out_d[:, m, :], outT[:, m, :]).then_inc(out_done, 16)
            sp.wait_ge(out_done, 16 * KD)

        @block.gpsimd
        def _(pool):
            pool.wait_ge(kr_done, 1)
            nc.gpsimd.tensor_copy(kT[64:96, :, :], kr.unsqueeze(1).broadcast_to([32, H, 512])).then_inc(kr_spread, 1)
            for half in range(2):
                pool.wait_ge(ATT[0]["scores"], 8 * (half + 1))
                if half == 0:
                    pool.wait_ge(kr_spread, 1)
                pool.dma_start(arena[:, 2048 * half:2048 * (half + 1)],
                               bias_d[:, 2048 * half:2048 * (half + 1)]).then_inc(in_bias, 16)
                pool.wait_ge(in_bias, 16 * (half + 1))
                b = arena[:, 2048 * half:2048 * (half + 1)].rearrange("p (a n) -> p a n", n=GRID_W)
                nc.gpsimd.tensor_tensor(b, b, namask.unsqueeze(1).broadcast_to([P, 32, GRID_W]),
                                        ALU.add).then_inc(bias_ready, 1)
                pool.wait_ge(bias_ready, half + 1)
            pool.wait_ge(ATT[0]["pv"], 4)
            pool.dma_start(sgw[:, :, :], sgw_d).then_inc(in_sg, 16)
            pool.wait_ge(in_sg, 16)
            nc.gpsimd.memset(sgw[64:128, :, 0:64], 0.0).then_inc(sg_zero, 1)
            pool.wait_ge(sg_zero, 1)
            pool.wait_ge(prod2_a, copied(PROD2, [p[0] for p in PROD2].index("nck") + 3)[1])
            nc.gpsimd.tensor_tensor(nck0[:, :, :], nck[:, :, 0:P], tri.unsqueeze(1).broadcast_to([P, H, P]),
                                    ALU.add).then_inc(nck_done, 1)
            pool.wait_ge(nck_done, 1)
            nc.gpsimd.tensor_tensor(nck[:, :, P:T], nck[:, :, P:T], tri.unsqueeze(1).broadcast_to([P, H, P]),
                                    ALU.add).then_inc(nck_done, 1)

        @block.scalar
        def _(act):
            steps = [0]

            def link(ins):
                steps[0] += 1
                ins.then_inc(astep, 1)
                act.wait_ge(astep, steps[0])

            act.dma_start(vec[:, :], vec_d).then_inc(in_vec, 16)
            act.dma_start(con[:, 0:CON_FIRST], con_d[:, 0:CON_FIRST]).then_inc(in_con, 16)

            act.wait_ge(in_vec, 16)
            act.wait_ge(mod_first, 2)
            nc.scalar.activation(cs[:, :, 0:2], vec[:, 0:16].rearrange("p (k c) -> p k c", c=2), ACT.Silu
                                 ).then_inc(silu_c, 1)
            act.wait_ge(in_x, 16)
            nc.scalar.activation(hT[:, :, 0:T], xT[:, :, :], ACT.Square).then_inc(squares[0], 1)
            act.wait_ge(var[0], 1)
            nc.scalar.activation(rstd[:, 0:T], rstd[:, 0:T], ACT.Sqrt).then_inc(std[0], 1)
            for half in range(4):
                act.wait_ge(mod_streamed, half + 1)
                nc.scalar.activation(modp[:, half * 512:(half + 1) * 512], bank[half][:, :], ACT.Copy
                                     ).then_inc(mod_copied, 1)

            def chunk_to_hi(stage, chunk, c):
                load = chunk[c][0]
                if c == 0 or chunk[c - 1][0] != load:
                    act.wait_ge((landed2 if load >= L_IN2 else landed)[slot_of(load)], landed_count(load))
                nc.scalar.activation(chunk_part(w_hi, chunk, c), chunk_src(chunk, c), ACT.Copy
                                     ).then_inc(chunk_hi[stage], 1)

            for c in range(3):
                chunk_to_hi(0, CHUNK1, c)
            for s in range(2):
                if s == 1:
                    chunk_to_hi(0, CHUNK1, 3)
                    act.wait_ge(var[0], 2)
                    nc.scalar.activation(rstd[:, T:2 * T], rstd[:, T:2 * T], ACT.Sqrt).then_inc(std[0], 1)
                for k in range(KD):
                    act.wait_ge(normed[0], KD * s + k + 1)
                    nc.scalar.activation(hT_hi[:, k, s * T:(s + 1) * T], hT[:, k, s * T:(s + 1) * T], ACT.Identity,
                                         bias=mod[:, k, s:s + 1]).then_inc(shifted[0], 1)

            def out_of_psum(n):
                kind, i, e = PROD[n]
                src = bank[n % 4]
                act.wait_ge(prod_ready, n + 1)
                scale = 1.0
                if kind == "ql":
                    dst, src = qlat[:, i, :], src[:, 0:T]
                elif kind == "kvl":
                    dst, src = kvlat[:, i, :], src[:, :]
                elif kind == "naq":
                    dst, src, scale = naq[:, i, :], src[:, 0:T], HD ** -0.5
                elif kind == "nak":
                    dst, src = nak[:, i, :], src[:, :]
                elif kind == "nav":
                    dst, src = nav[:, i, :], src[:, :]
                elif kind == "uq":
                    dst, src, scale = qT[:, i, :], src[0:QK, 0:T], QK ** -0.5
                elif kind == "kn":
                    dst, src = kT[0:NOPE, i, :], src[0:NOPE, :]
                elif kind == "vm":
                    dst, src = vm[:, i, :], src[:, :]
                nc.scalar.activation(dst, src, ACT.Copy, scale=scale).then_inc(prod_a, 1)

            done = 0
            for n, (kind, i, e) in enumerate(PROD):
                if n == 5:
                    act.wait_ge(prod_d, copied(PROD, 3)[1])
                    act.wait_ge(prod_a, copied(PROD, 4)[1])
                    nc.scalar.activation(attf[:, 0:1792], lat[:, :], ACT.Square).then_inc(lat_sq, 1)
                if n == N_BEFORE_LAT:
                    act.wait_ge(lat_var, 2)
                    nc.scalar.activation(rq, rq, ACT.Sqrt).then_inc(lat_std, 1)
                    nc.scalar.activation(rkv, rkv, ACT.Sqrt).then_inc(lat_std, 1)
                for c in chunks_after(CHUNK1, n):
                    act.wait_ge(prod_ready, n + 1)
                    chunk_to_hi(0, CHUNK1, c)
                if e == "A":
                    out_of_psum(n)

            def exps(units, A, s):
                a, h, q, nk = units[s]
                u = 16 * a + 8 * q + h
                act.wait_ge(A["maxed"], s + 1)
                if s >= 3:
                    act.wait_ge(A["turned"], s - 2)
                nc.scalar.activation(att[:, s % 3, 0:nk * P], bank[s % 2][:, 0:nk * P], ACT.Exp,
                                     bias=nmax[:, u:u + 1], accum_out=rsum[:, u:u + 1]).then_inc(A["exped"], 1)

            def turn_copy(units, A, s):
                a, h, q, nk = units[s]
                act.wait_ge(A["turned"], s + 1)
                if s >= 4:
                    act.wait_ge(A["pv"], s // 4)
                nc.scalar.activation(ptT(a, h)[:, 0:nk, q * P:(q + 1) * P],
                                     bank[2 + s % 2][:, 0:nk * P].rearrange("p (j t) -> p j t", t=P), ACT.Copy
                                     ).then_inc(A["pt"], 1)

            def attention(units, A):
                for s in range(len(units) + 2):
                    if s < len(units):
                        exps(units, A, s)
                    if units is UNITS and s % 4 == 2 and s // 4 < 8:
                        act.wait_ge(mod_streamed, 5 + s // 4)
                        if s // 4:
                            act.wait_ge(mod_picked, 4 + s // 4)
                        nc.scalar.activation(modp2, bank[7][:, :], ACT.Copy).then_inc(mod_copied, 1)
                    if units is UNITS2 and s == 5:
                        act.wait_ge(sg_t, 1)
                        nc.scalar.activation(h2_hi[:, 0:2, :].rearrange("p a t -> p (a t)"), bank[6][:, :],
                                             ACT.Copy).then_inc(sg_a, 1)
                    if s >= 2:
                        turn_copy(units, A, s - 2)

            attention(UNITS, ATT[0])
            act.wait_ge(prod_ready, NAV_DONE)
            for c in range(OUT1, OUT1 + 4):
                chunk_to_hi(0, CHUNK1, c)

            def prefetch(func):
                tables[0] += 1
                nc.scalar.activation(tiny[:, tables[0]:tables[0] + 1], tiny[:, 0:1], func)

            tables = [0]

            def norm(r, updated, after=lambda k: None):
                prefetch(ACT.Sqrt)
                for k in range(KD):
                    act.wait_ge(updated, k + 1)
                    nc.scalar.activation(sq[:, k, :], xT[:, k, :], ACT.Square).then_inc(squares[r], 1)
                    after(k)
                act.wait_ge(var[r], 1)
                n = 4 if r == 2 else 2
                nc.scalar.activation(rs[:, 0:n], rs[:, 0:n], ACT.Sqrt).then_inc(std[r], 1)

            def rest_of_out(m):
                if m < 4:
                    act.wait_ge(proj_out, m + 1)
                    chunk_to_hi(0, CHUNK1, OUT1 + 4 + m)

            norm(1, resid, rest_of_out)
            for k in range(KD):
                act.wait_ge(normed[1], k + 1)
                nc.scalar.activation(h2[:, k, :], h2[:, k, :], ACT.Identity, bias=mod[:, 24 + k, 0:1]
                                     ).then_inc(shifted[1], 1)
            act.wait_ge(logits_part, 1)
            nc.scalar.activation(logit_parts, bank[6][:, 0:T], ACT.Copy).then_inc(logits_copied, 1)
            prefetch(ACT.Exp)
            act.wait_ge(gdiff, 1)
            nc.scalar.activation(small[:, 1, 0:8], small[:, 1, 0:8], ACT.Exp).then_inc(gexp, 1)
            act.wait_ge(ediff, 1)
            nc.scalar.activation(small[:, 5, 0:8], small[:, 5, 0:8], ACT.Exp).then_inc(eexp, 1)
            for b in (0, 2):
                act.wait_ge(tok_t, b + 1)
                nc.scalar.activation(h2tok[:, b // 2, (b % 2) * 512:(b % 2 + 1) * 512], bank[b][:, :], ACT.Copy
                                     ).then_inc(tok_a, 1)
            prefetch(ACT.Silu)
            act.wait_ge(turns_ready, 1)
            windows = act.value_load(turns_i[0:1, 0:1], min_val=1, max_val=T // CAP)
            with act.Fori(0, windows) as w:
                def inputs(p):
                    act.wait_ge(gathered, p)
                    nc.scalar.activation(xs[:, 0:4, :], bank[0][:, :].rearrange("p (k s) -> p k s", k=4), ACT.Identity
                                         ).then_inc(xs_a, 1)

                def pair(i, last=False):
                    act.wait_ge(used, w * 48 + i * 6 + 2)
                    nc.scalar.activation(hid, bank[2][:, :], ACT.Silu).then_inc(silu_g, 1)
                    if not last:
                        inputs(w * 16 + i * 2 + 3)
                    act.wait_ge(place_t, w * 8 + i + 1)
                    nc.scalar.activation(arena[:, bass.ds(i * T + (4096 + T), T)], bank[3][:, 0:T], ACT.Identity
                                         ).then_inc(place_done, 1)
                    act.wait_ge(y_half, w * 8 + i + 1)
                    act.wait_ge(scattered, w * 9 + i + 2)
                    nc.scalar.activation(ysb[:, 0:512], bank[2][:, :], ACT.Identity).then_inc(y_a, 1)

                inputs(w * 16 + 1)
                with act.Fori(0, NPAIR - 1) as i:
                    pair(i)
                pair(NPAIR - 1, last=True)
            norm(2, resid_m)
            act.wait_ge(used, windows * 48)
            chunk_to_hi(1, CHUNK2, 0)
            for k in range(KD):
                act.wait_ge(normed[2], k + 1)
                nc.scalar.activation(h2_hi[:, k, :], h2[:, k, :], ACT.Copy).then_inc(h2_hi_done, 1)
            for c in range(1, 4):
                chunk_to_hi(1, CHUNK2, c)

            def out_of_psum2(n):
                kind, i, e = PROD2[n]
                src = bank[n % 4]
                act.wait_ge(prod2_ready, n + 1)
                if kind == "u":
                    ins = nc.scalar.activation(ug[:, i, :], src[:, :], ACT.Gelu)
                elif kind == "va":
                    ins = nc.scalar.activation(vg[:, i, :], src[:, :], ACT.Gelu)
                elif kind == "nck":
                    ins = nc.scalar.activation(nck[:, 2 * i:2 * i + 2, :].rearrange("p a t -> p (a t)"), src[:, :],
                                               ACT.Copy, scale=-1.0)
                elif kind == "v":
                    ins = nc.scalar.activation(v2[:, i, :], src[:, :], ACT.Copy)
                ins.then_inc(prod2_a, 1)

            prefetch(ACT.Exp)
            act.wait_ge(f_abs, 1)
            link(nc.scalar.activation(small[:, 1, 0:16], small[:, 1, 0:16], ACT.Exp))
            nc.scalar.activation(small[:, 1, 0:16], small[:, 1, 0:16], ACT.Ln, bias=1.0).then_inc(f_ln, 1)
            for n, (kind, i, e) in enumerate(PROD2):
                for c in chunks_after(CHUNK2, n):
                    if kind in ("u", "va") and c % 4 < 3:
                        act.wait_ge(strip_read, 3 * (c // 4 - 1) + c % 4 + 1)
                    else:
                        act.wait_ge(prod2_ready, n + 1)
                    chunk_to_hi(1, CHUNK2, c)
                if (kind, i) == ("v", 0):
                    act.wait_ge(ln_var, 1)
                    nc.scalar.activation(small[:, 6, 0:16], small[:, 6, 0:16], ACT.Sqrt).then_inc(ln_std, 1)
                    prefetch(ACT.Exp)
                if e == "A":
                    out_of_psum2(n)
            attention(UNITS2, ATT[1])

            def up_hi(j, half):
                nc.scalar.activation(granule(w_hi, j, half), up_half_of(j, half), ACT.Copy).then_inc(wide_hi, 1)

            def down_hi(d, half):
                if d % 2 == 0 and half == 0:
                    act.wait_ge(landed2[slot_of(L_DOWN + d // 2)], landed_count(L_DOWN + d // 2))
                nc.scalar.activation(w_hi[:, d % 2, half, :], down_half_of(d, half), ACT.Copy).then_inc(wide_hi, 1)

            def hidden_hi(at, b, n):
                act.wait_ge(hid_done, n)
                nc.scalar.activation(hid_hi[:, at, :], yconv[:, b, 1, :], ACT.Copy).then_inc(hid_hi_done, 1)

            act.wait_ge(prod2_ready, len(PROD2))
            for c in range(OUT2, OUT2 + 4):
                chunk_to_hi(1, CHUNK2, c)

            def after_out2(m):
                act.wait_ge(proj2_out, m + 1)
                if m < 4:
                    chunk_to_hi(1, CHUNK2, OUT2 + 4 + m)
                elif m < 6:
                    if m == 4:
                        act.wait_ge(landed2[slot_of(L_UP)], landed_count(L_UP))
                    up_hi(0, m - 4)

            norm(3, resid2, after_out2)
            for k in range(KD):
                act.wait_ge(normed[3], k + 1)
                nc.scalar.activation(h2_hi[:, k, :], h2[:, k, :], ACT.Copy).then_inc(h2_hi_done, 1)
            for half in range(2):
                up_hi(1, half)

            def pair(i, j, first=False, last=False):
                b = j % 2
                for half in range(2):
                    act.wait_ge(up_half, i * 8 + (2 * j + half + 1))
                    if last:
                        down_hi(j, half)
                    else:
                        if b == 0 and half == 0:
                            act.wait_ge(landed2[3 - j // 2], i * 32 + landed_count(L_UP + 1 + j // 2))
                        up_hi((j + 2) % 4, half)
                if not (first and j == 0):
                    hidden_hi(i * 4 + (j - 1), 1 - b, i * 4 + j)
                if not (first and j < 2):
                    act.wait_ge(hid_lo_done, i * 4 + (j - 1))
                for g in range(2):
                    at = i * 4 + (j + 22 * g)
                    nc.scalar.activation(yconv[:, b, g, :], bank[j % 4][:, g * T:(g + 1) * T], ACT.Identity,
                                         bias=vec[:, bass.ds(at + VEC["b_conv"], 1)],
                                         scale=vec[:, bass.ds(at + (VEC["w_conv"] + 88), 1)]).then_inc(conv0, 1)
                act.wait_ge(tap2, i * 8 + (2 * j + 1))
                nc.scalar.activation(yconv[:, b, 0, :], yconv[:, b, 0, :], ACT.Silu).then_inc(silu_f, 1)

            for j in range(4):
                pair(0, j, first=True)
            with act.Fori(1, NP // 4) as i:
                for j in range(4):
                    pair(i, j)
            for j in range(NP % 4):
                pair(NP // 4, j, last=True)
            hidden_hi(NP - 1, (NP - 1) % 2, NP)
            for d in range(2, NP // 2):
                for half in range(2):
                    act.wait_ge(down_half, 2 * (d - 2) + half + 1)
                    down_hi(d, half)
            norm(4, resid3)

        @block.tensor
        def _(pe):
            def slot(n, k):
                return ring[:, slot_of(n), 0:SLOT // k * k].rearrange("p (k n) -> p k n", k=k)

            def arrive(n):
                pe.wait_ge((landed2 if n >= L_IN2 else landed)[slot_of(n)], landed_count(n))

            def mod_stream(n, b):
                arrive(n)
                w = slot(n, KD)
                for k in range(KD):
                    g = 32 * (k % 4)
                    last = nc.tensor.matmul(bank[b][g:g + 32, :], cs[:, k, :], w[:, k, :],
                                            start=(k < 4), stop=(k >= 4))
                last.then_inc(mod_streamed, 1)

            def mod_pick(half, src):
                pe.wait_ge(mod_copied, half + 1)
                for t in range(4):
                    c = 8 * half + 2 * t
                    last = nc.tensor.matmul(bank[6][:, c:c + 2], src[:, t * P:(t + 1) * P], pick, start=True, stop=True)
                last.then_inc(mod_picked, 1)

            pe.wait_ge(silu_c, 1)
            def square_sum(part):
                pe.wait_ge(squares[0], part + 1)
                at = slice(part * T, (part + 1) * T)
                for k in range(KD):
                    last = nc.tensor.matmul(bank[7][:, at], ones, hT[:, k, at], start=(k == 0), stop=(k == KD - 1))
                last.then_inc(sumsq[0], 1)

            for half in range(4):
                mod_stream(half, half)
                if half == 0:
                    pe.wait_ge(in_con, 16)
                    square_sum(0)
                else:
                    mod_pick(half - 1, modp[:, (half - 1) * 512:half * 512])
            mod_pick(3, modp[:, 3 * 512:4 * 512])
            square_sum(1)

            def bank_free(prod, n, sa, sd):
                if n >= 4:
                    e, count = copied(prod, n - 4)
                    pe.wait_ge(sa if e == "A" else sd, count)

            def latent_sums():
                pe.wait_ge(lat_sq, 1)
                for k in range(3):
                    last = nc.tensor.matmul(bank[4][:, 0:T], ones, attf[:, k * T:(k + 1) * T],
                                            start=(k == 0), stop=(k == 2))
                last.then_inc(lat_ss, 1)
                for k in range(2):
                    last = nc.tensor.matmul(bank[5][:, :], ones, attf[:, 768 + 512 * k:1280 + 512 * k],
                                            start=(k == 0), stop=(k == 1))
                last.then_inc(lat_ss, 1)

            loads = {"uq": L_UQ, "kn": L_UKV, "vm": L_UKV}
            def tile_product(stage, chunk, c, dst, x_hi, x_lo, hi_done, lo_done):
                pe.wait_ge(chunk_hi[stage], c + 1)
                for part, x, done in ((w_hi, x_hi, hi_done), (w_lo, x_hi, None), (w_hi, x_lo, lo_done)):
                    if part is w_lo:
                        pe.wait_ge(chunk_lo[stage], c + 1)
                    for k in range(KD):
                        if done is not None:
                            pe.wait_ge(done[0], done[1] + k + 1)
                        last = nc.tensor.matmul(dst, chunk_part(part, chunk, c)[:, k, :], x[:, k, :],
                                                start=(part is w_hi and x is x_hi and k == 0),
                                                stop=(x is x_lo and k == KD - 1))
                return last

            def strip_product(stage, chunk, cs_, dst, x_hi, x_lo, release=None):
                for k in range(KD):
                    c = cs_[k // 2]
                    if k % 2 == 0:
                        pe.wait_ge(chunk_hi[stage], c + 1)
                        pe.wait_ge(chunk_lo[stage], c + 1)
                    nc.tensor.matmul(dst, x_hi[:, k, :], chunk_part(w_hi, chunk, c)[:, k % 2, :],
                                     start=(k == 0), stop=False)
                    nc.tensor.matmul(dst, x_hi[:, k, :], chunk_part(w_lo, chunk, c)[:, k % 2, :],
                                     start=False, stop=False)
                    last = nc.tensor.matmul(dst, x_lo[:, k, :], chunk_part(w_hi, chunk, c)[:, k % 2, :],
                                            start=False, stop=(k == KD - 1))
                    if release is not None and k % 2 == 1 and k < KD - 1:
                        last.then_inc(release, 1)
                return last

            for n, (kind, i, _e) in enumerate(PROD):
                if n == N_BEFORE_LAT:
                    pe.wait_ge(in_rest, 16)
                    latent_sums()
                bank_free(PROD, n, prod_a, prod_d)
                dst = bank[n % 4]
                if kind in loads and i == 0:
                    arrive(loads[kind])
                if kind in ("ql", "kvl", "kr", "naq", "nak"):
                    c = chunks_of(CHUNK1, n)[0]
                    cols = T if kind in ("ql", "naq") else 2 * T
                    m = QK if kind == "kr" else P
                    first = {0: 0, 3: KD}.get(n)
                    last = tile_product(0, CHUNK1, c, dst[0:m, 0:cols], hT_hi[:, :, 0:cols], hT_lo[:, :, 0:cols],
                                        None if first is None else (shifted[0], first),
                                        None if first is None else (shifted_lo, first))
                elif kind == "nav":
                    last = strip_product(0, CHUNK1, chunks_of(CHUNK1, NAV_DONE - 1), dst[:, :],
                                         hT_hi[:, :, i * P:(i + 1) * P], hT_lo[:, :, i * P:(i + 1) * P])
                elif kind == "uq":
                    if i == 0:
                        pe.wait_ge(lat_done, 5)
                        pe.wait_ge(prod_ready, n)
                    w = ring[:, slot_of(L_UQ), 0:2304].rearrange("p (k n) -> p k n", k=3)
                    for k in range(3):
                        last = nc.tensor.matmul(dst[0:QK, 0:T], w[:, k, i * QK:(i + 1) * QK], qlat[:, k, :],
                                                start=(k == 0), stop=(k == 2))
                elif kind == "kn":
                    w = ring[:, slot_of(L_UKV), 0:2048].rearrange("p (k n) -> p k n", k=2)
                    for k in range(2):
                        last = nc.tensor.matmul(dst[0:NOPE, :], w[:, k, i * P:i * P + NOPE], kvlat[:, k, :],
                                                start=(k == 0), stop=(k == 1))
                elif kind == "vm":
                    w = ring[:, slot_of(L_UKV), 0:2048].rearrange("p (k h n) -> p k h n", k=2, h=H)
                    for k in range(2):
                        last = nc.tensor.matmul(dst[:, :], kvlat[:, k, i * P:(i + 1) * P], w[:, k, :, NOPE:P],
                                                start=(k == 0), stop=(k == 1))
                elif kind == "rotk":
                    pe.wait_ge(prod_d, copied(PROD, 5)[1])
                    last = nc.tensor.matmul(dst[64:96, :], rot, kr, start=True, stop=True)
                elif kind == "rotq":
                    if i == 0:
                        pe.wait_ge(prod_a, copied(PROD, 25)[1])
                        pe.wait_ge(prod_d, copied(PROD, 26)[1])
                    last = nc.tensor.matmul(dst[64:96, :], rot, qT[64:96, 2 * i:2 * i + 2, :], start=True, stop=True)
                last.then_inc(prod_ready, 1)

            def scores(units, A, s):
                a, h, q, nk = units[s]
                if s >= 2:
                    pe.wait_ge(A["exped"], s - 1)
                lo = 64 * (h % 2)
                if a == 0:
                    lhs, rhs = qT[:, h, q * P:(q + 1) * P], kT[:, h, :]
                elif a == 1:
                    lhs, rhs = naq[lo:lo + 64, h // 2, q * P:(q + 1) * P], nak[lo:lo + 64, h // 2, :]
                else:
                    lhs, rhs = q2[lo:lo + 64, h // 2, q * P:(q + 1) * P], k2[lo:lo + 64, h // 2, 0:nk * P]
                nc.tensor.matmul(bank[s % 2][:, 0:nk * P], lhs, rhs, start=True, stop=True).then_inc(A["scores"], 1)

            def turns(units, A, s):
                nk = units[s][3]
                pe.wait_ge(A["scaled"], s + 1)
                if s >= 2:
                    pe.wait_ge(A["pt"], s - 1)
                for j in range(nk):
                    last = nc.tensor.transpose(bank[2 + s % 2][:, j * P:(j + 1) * P], att[:, s % 3, j * P:(j + 1) * P],
                                               ident)
                last.then_inc(A["turned"], 1)

            def values(units, A, i):
                a, h, _, _ = units[4 * i]
                v = (vm, nav, v2)[a]
                keys = units[4 * i + 1][3]
                pe.wait_ge(A["pt"], 4 * i + 4)
                if i >= 2:
                    pe.wait_ge(A["out"], i - 1)
                for j in range(keys):
                    lo = P * (a == 2 and j == 1)
                    for e in range(2):
                        last = nc.tensor.matmul(bank[4 + i % 2][HD * e:HD * (e + 1), lo:T],
                                                v[:, j, (h + e) * HD:(h + e + 1) * HD], ptT(a, h + e)[:, j, lo:T],
                                                start=(j == 0), stop=(j == keys - 1))
                last.then_inc(A["pv"], 1)

            def attention(units, A, between):
                for s in range(len(units) + 3):
                    if s < len(units):
                        scores(units, A, s)
                    if s >= 6 and s % 4 == 2:
                        values(units, A, (s - 6) // 4)
                    if 2 <= s < len(units) + 2:
                        turns(units, A, s - 2)
                    between(s)

            pe.wait_ge(prod_a, total(PROD, "A"))
            pe.wait_ge(prod_d, total(PROD, "D"))
            pe.wait_ge(kr_spread, 1)

            def rest_of_mod(s):
                if s % 4 == 1 and s // 4 < 8:
                    if s // 4:
                        pe.wait_ge(mod_copied, 4 + s // 4)
                    mod_stream(L_MOD2 + s // 4, 7)
                if s % 4 == 3 and s // 4 < 8:
                    mod_pick(4 + s // 4, modp2)

            attention(UNITS, ATT[0], rest_of_mod)
            assert len(UNITS) % 4 == 0 and (len(UNITS) + 2) % 4 == 2

            def out_projection(stage, chunk, c, x_lo, outs, pairs, ready, freed):
                for m in range(KD):
                    pe.wait_ge(chunk_hi[stage], c + m + 1)
                    pe.wait_ge(chunk_lo[stage], c + m + 1)
                    if m >= 4:
                        pe.wait_ge(freed, m - 3)
                    high, low = chunk_part(w_hi, chunk, c + m), chunk_part(w_lo, chunk, c + m)
                    for k in range(KD):
                        if m == 0 and k >= KD - pairs:
                            pe.wait_ge(outs, k - (KD - pairs) + 1)
                        dst = bank[m % 4][:, 0:T]
                        nc.tensor.matmul(dst, high[:, k, :], h2_hi[:, k, :], start=(k == 0), stop=False)
                        nc.tensor.matmul(dst, low[:, k, :], h2_hi[:, k, :], start=False, stop=False)
                        last = nc.tensor.matmul(dst, high[:, k, :], x_lo[:, k, :], start=False, stop=(k == KD - 1))
                    last.then_inc(ready, 1)

            out_projection(0, CHUNK1, OUT1, mix_lo[0], ATT[0]["out"], 8, proj_out, resid)

            def norm_sum(r):
                n = 2 if r == 2 else 1
                sums = bank[NORM_BANK[r]]
                for k in range(KD):
                    pe.wait_ge(squares[r], k + 1)
                    for q in range(NT):
                        last = nc.tensor.matmul(sums[:, n * q:n * (q + 1)], sq[:, k, q * P:(q + 1) * P],
                                                g_sq[:, k, 0:n], start=(k == 0 and q == 0), stop=(k == KD - 1),
                                                skip_group_check=True)
                last.then_inc(sumsq[r], 1)
                pe.wait_ge(std[r], 1)
                for c in range(NT * n):
                    dst = (bank[6 + (c < NT)][:, (c % NT) * P:(c % NT + 1) * P] if r == 2
                           else sums[:, T + c * P:T + (c + 1) * P])
                    last = nc.tensor.matmul(dst, rs[:, c:c + 1].broadcast_to([P, P]), ident, start=True, stop=True)
                last.then_inc(spread, 1)

            norm_sum(1)
            pe.wait_ge(in_row, 48)
            pe.wait_ge(shifted[1], KD)
            for k in range(KD):
                g = 32 * (k % 4)
                last = nc.tensor.matmul(bank[6][g:g + 32, 0:T], wr[:, k, :], h2[:, k, :], start=(k < 4), stop=(k >= 4))
            last.then_inc(logits_part, 1)
            for b in range(4):
                if b == 2:
                    pe.wait_ge(logits_copied, 1)
                    for q in range(NT):
                        last = nc.tensor.matmul(bank[6][:, 256 + 32 * q:256 + 32 * q + 20], logit_parts[:, q * P:(q + 1) * P],
                                                pick20, start=True, stop=True)
                    last.then_inc(logits, 1)
                for k in range(4):
                    last = nc.tensor.transpose(bank[b][:, k * P:(k + 1) * P],
                                               h2[:, 4 * (b % 2) + k, (b // 2) * P:(b // 2 + 1) * P], ident)
                last.then_inc(tok_t, 1)
            zero = cs[:, 0, 31:32].bitcast(mybir.dt.bfloat16)[:, 0:1]

            def clear(b):
                return nc.tensor.matmul(bank[b][:, :], zero.broadcast_to([P, P]), zero.broadcast_to([P, 512]),
                                        start=True, stop=False, skip_group_check=True)

            for b in (4, 5, 7):
                clear(b)
            pe.wait_ge(comb_done, NT)
            chosen = small[:, 14, :].rearrange("p (q e) -> p q e", q=NT)
            nc.tensor.matmul(bank[6][:, 192:208], upper, chosen[:, 0, :], start=True, stop=True)
            nc.tensor.matmul(bank[6][:, 208:224], ones, chosen[:, 0, :], start=True, stop=False)
            nc.tensor.matmul(bank[6][:, 208:224], upper, chosen[:, 1, :], start=False, stop=True)
            for q in range(NT):
                last = nc.tensor.matmul(bank[6][:, 224:240], ones, chosen[:, q, :], start=(q == 0), stop=(q == 1))
            last.then_inc(counted, 1)
            pe.wait_ge(turns_ready, 1)
            windows = pe.value_load(turns_i[0:1, 0:1], min_val=1, max_val=T // CAP)
            clear(6).then_inc(scattered, 1)
            pe.wait_ge(tok_a, 2)
            pe.wait_ge(tok_d, 2)

            def scatter(i):
                for m in range(KD):
                    last = nc.tensor.matmul(yacc(m), ysb[:, m * P:(m + 1) * P], place[:, i, :],
                                            start=False, stop=False, skip_group_check=True)
                last.then_inc(scattered, 1)

            with pe.Fori(0, windows) as w:
                def gather(at):
                    for k in range(KD):
                        for q in range(NT):
                            last = nc.tensor.matmul(bank[k // 4][:, (k % 4) * P:(k % 4 + 1) * P],
                                                    h2tok[:, q, k * P:(k + 1) * P],
                                                    arena[:, bass.ds(at + q * 1024, P)],
                                                    start=(q == 0), stop=(q == NT - 1))
                        if k % 4 == 3:
                            last.then_inc(gathered, 1)

                def pair(i, last_pair=False):
                    pe.wait_ge(xs_a, w * 8 + i + 1)
                    pe.wait_ge(xs_d, w * 8 + i + 1)
                    for j in range(2):
                        n = L_MOE + 2 * j
                        for e in range(2):
                            pe.wait_ge(landed[slot_of(n + e)], w * 128 + i * 16 + landed_count(n + e))
                        if j == 0:
                            pe.wait_ge(y_a, w * 9 + i + 1)
                            pe.wait_ge(y_d, w * 9 + i + 1)
                        for k in range(KD):
                            for e in range(2):
                                last = nc.tensor.matmul(bank[2 + j][CAP * e:CAP * (e + 1), :],
                                                        xs[:, k, CAP * e:CAP * (e + 1)], slot(n + e, KD)[:, k, :],
                                                        start=(k == 0), stop=(k == KD - 1))
                                if k == KD - 1:
                                    last.then_inc(used, 1)
                    scatter(i)
                    if not last_pair:
                        gather(i * P + P)
                    pe.wait_ge(hid_made, w * 8 + i + 1)
                    for f in range(4):
                        last = nc.tensor.transpose(bank[2][:, f * P:(f + 1) * P], hid[:, f * P:(f + 1) * P], ident)
                    last.then_inc(hid_t, 1)
                    pe.wait_ge(picked, w * 8 + i + 1)
                    for q in range(NT):
                        last = nc.tensor.transpose(bank[3][:, q * P:(q + 1) * P],
                                                   pick_w[:, q, :, :], ident)
                    last.then_inc(place_t, 1)
                    pe.wait_ge(hidT_done, w * 8 + i + 1)
                    for e in range(2):
                        pe.wait_ge(landed[slot_of(L_MOE + 4 + e)], w * 128 + i * 16 + landed_count(L_MOE + 4 + e))
                    for half in range(2):
                        if half == 1:
                            pe.wait_ge(place_done, w * 8 + i + 1)
                        for f in range(4):
                            for e in range(2):
                                last = nc.tensor.matmul(bank[2 + half][CAP * e:CAP * (e + 1), :],
                                                        hidT[:, f, CAP * e:CAP * (e + 1)],
                                                        slot(L_MOE + 4 + e, 4)[:, f, half * 512:(half + 1) * 512],
                                                        start=(f == 0), stop=(f == 3))
                                if half == 1 and f == 3:
                                    last.then_inc(used, 1)
                        if half == 0:
                            last.then_inc(y_half, 1)

                pe.wait_ge(picked_t, w * 2 + 2)
                gather(0)
                with pe.Fori(0, NPAIR - 1) as i:
                    pair(i)
                pair(NPAIR - 1, last_pair=True)
                pe.wait_ge(y_a, w * 9 + 9)
                pe.wait_ge(y_d, w * 9 + 9)
                scatter(NPAIR)
            norm_sum(2)

            lf = small[:, 2, 0:16].rearrange("p (q h) -> p q h", q=NT)
            for n, (kind, i, _e) in enumerate(PROD2):
                bank_free(PROD2, n, prod2_a, prod2_d)
                dst = bank[n % 4]
                if kind == "f":
                    for k in range(KD):
                        pe.wait_ge(normed[2], k + 1)
                    for q in range(NT):
                        for k in range(KD):
                            last = nc.tensor.matmul(dst[:, 8 * q:8 * q + 8], h2[:, k, q * P:(q + 1) * P], wf[:, k, :],
                                                    start=(k == 0), stop=(k == KD - 1))
                elif kind in ("u", "va", "v"):
                    if kind == "u" and i == 0:
                        pe.wait_ge(h2_hi_done, KD)
                        pe.wait_ge(h2_lo_done, KD)
                    last_use = [p[:2] for p in PROD2].index((kind, 1))
                    last = strip_product(1, CHUNK2, chunks_of(CHUNK2, last_use), dst[:, :],
                                         h2_hi[:, :, i * P:(i + 1) * P], h2_lo[:, :, i * P:(i + 1) * P],
                                         strip_read if i == 1 and kind != "v" else None)
                elif kind in ("q", "k"):
                    last = tile_product(1, CHUNK2, chunks_of(CHUNK2, n)[0], dst[:, 0:T], h2_hi, h2_lo, None, None)
                elif kind == "cq":
                    pe.wait_ge(lf_done, 1)
                    nc.tensor.matmul(dst[:, 0:8], upper, lf[:, 0, :], start=True, stop=True)
                    nc.tensor.matmul(dst[:, 8:16], ones, lf[:, 0, :], start=True, stop=False)
                    last = nc.tensor.matmul(dst[:, 8:16], upper, lf[:, 1, :], start=False, stop=True)
                elif kind == "nck":
                    for j in range(2):
                        h = 2 * i + j
                        nc.tensor.matmul(dst[:, j * T:(j + 1) * T], lf[:, 0, h:h + 1].broadcast_to([P, P]),
                                         upper_ones, start=True, stop=False)
                        last = nc.tensor.matmul(dst[:, j * T + P:(j + 1) * T], lf[:, 1, h:h + 1].broadcast_to([P, P]),
                                                upper, start=False, stop=True)
                last.then_inc(prod2_ready, 1)
            pe.wait_ge(vn_done, 1)
            pe.wait_ge(sg_zero, 1)
            for q in range(NT):
                for h in range(H):
                    last = nc.tensor.matmul(bank[6 + q][:, h * HD:(h + 1) * HD], sgw[:, h, :],
                                            vg[:, q, h * HD:(h + 1) * HD], start=True, stop=True)
                last.then_inc(sg_mm, 1)
            pe.wait_ge(prod2_a, total(PROD2, "A"))
            pe.wait_ge(prod2_d, total(PROD2, "D"))

            def turn_gated(s):
                if s == 3:
                    pe.wait_ge(sg_done, NT)
                    for c in range(4):
                        for q in range(NT):
                            last = nc.tensor.transpose(bank[6 + c // 2][:, (c % 2) * T + q * P:(c % 2) * T + (q + 1) * P],
                                                       osb[:, q, c * P:(c + 1) * P], ident)
                        if c % 2:
                            last.then_inc(sg_t, 1)

            attention(UNITS2, ATT[1], turn_gated)
            pe.wait_ge(sg_d, 2)
            out_projection(1, CHUNK2, OUT2, mix_lo[1], ATT[1]["out"], 4, proj2_out, resid2)
            norm_sum(3)

            def up_pair(i, j, first=False):
                if not (first):
                    pe.wait_ge(tap2, i * 8 + (2 * j - 6))
                for g in range(2):
                    dst = bank[j][:, g * T:(g + 1) * T]
                    start = first and j == 0 and g == 0
                    pe.wait_ge(wide_hi, i * 8 + (2 * j + g + 1))
                    for k in range(KD):
                        if start:
                            pe.wait_ge(h2_hi_done, KD + k + 1)
                        nc.tensor.matmul(dst, granule(w_hi, j, g)[:, k, :], h2_hi[:, k, :],
                                         start=(k == 0), stop=False)
                    pe.wait_ge(wide_lo, i * 8 + (2 * j + g + 1))
                    for k in range(KD):
                        nc.tensor.matmul(dst, granule(w_lo, j, g)[:, k, :], h2_hi[:, k, :], start=False, stop=False)
                    for k in range(KD):
                        if start:
                            pe.wait_ge(h2_lo_done, KD + k + 1)
                        last = nc.tensor.matmul(dst, granule(w_hi, j, g)[:, k, :], h2_lo[:, k, :],
                                                start=False, stop=(k == KD - 1))
                    last.then_inc(up_half, 1)

            for j in range(4):
                up_pair(0, j, True)
            with pe.Fori(1, NP // 4) as i:
                for j in range(4):
                    up_pair(i, j)
            for j in range(NP % 4):
                up_pair(NP // 4, j)

            def down_granule(b, at, first=False):
                for half in range(2):
                    kt = at * 2 + half
                    pe.wait_ge(wide_hi, at * 2 + (2 * NP + half + 1))
                    pe.wait_ge(hid_hi_done, at * 2 + (half + 1))
                    for m in range(KD):
                        nc.tensor.matmul(yacc(m), w_hi[:, b, half, m * P:(m + 1) * P], hid_hi[:, kt, :],
                                         start=(first and half == 0 and m % 2 == 0), stop=False,
                                         skip_group_check=True)
                    pe.wait_ge(wide_lo, at * 2 + (2 * NP + half + 1))
                    for m in range(KD):
                        nc.tensor.matmul(yacc(m), w_lo[:, b, half, m * P:(m + 1) * P], hid_hi[:, kt, :],
                                         start=False, stop=False, skip_group_check=True)
                    pe.wait_ge(hid_lo_done, at * 2 + (half + 1))
                    for m in range(KD):
                        last = nc.tensor.matmul(yacc(m), w_hi[:, b, half, m * P:(m + 1) * P], hid_lo[:, kt, :],
                                                start=False, stop=True, skip_group_check=True)
                    last.then_inc(down_half, 1)

            pe.wait_ge(resid2, KD)
            down_granule(0, 0, True)
            with pe.Fori(0, NP // 4) as i:
                for b in range(2):
                    down_granule(1 - b, i * 2 + (b + 1))
            norm_sum(4)

        @block.vector
        def _(dve):
            steps = [0]

            def link(ins):
                steps[0] += 1
                ins.then_inc(vstep, 1)
                dve.wait_ge(vstep, steps[0])

            V = nc.vector

            def bc(ap, axis, shape):
                return ap.unsqueeze(axis).broadcast_to(shape)

            def low_part(dst, src, high):
                return V.tensor_tensor(dst, src, high.bitcast(F32), ALU.subtract)

            def chunk_to_lo(stage, chunk, c):
                dve.wait_ge(chunk_hi[stage], c + 1)
                low_part(chunk_part(w_lo, chunk, c), chunk_src(chunk, c), chunk_part(w_hi, chunk, c)
                         ).then_inc(chunk_lo[stage], 1)

            V.memset(tiny[:, :], 0.0).then_inc(mod_first, 1)
            V.memset(cs[:, :, :], 0.0).then_inc(mod_first, 1)
            V.memset(g_sq[:, :, 0], 1.0).then_inc(mod_first, 1)
            dve.wait_ge(in_vec, 16)
            V.tensor_tensor(g_sq[:, :, 1], v_("g_final", 0, 8), v_("g_final", 0, 8), ALU.mult).then_inc(mod_first, 1)
            V.tensor_tensor(g_both[:, :], v_("g_final", 0, 8), v_("g_mix2", 0, 8), ALU.mult).then_inc(mod_first, 1)
            dve.wait_ge(sumsq[0], 1)
            V.tensor_scalar(rstd[:, 0:T], bank[7][:, 0:T], 1.0 / D, EPS, ALU.mult, ALU.add).then_inc(var[0], 1)
            dve.wait_ge(std[0], 1)
            link(V.reciprocal(rstd[:, 0:T], rstd[:, 0:T]))
            dve.wait_ge(in_ctx, 16)
            V.tensor_tensor(hT[:, :, T:2 * T], ctxT, ctxT, ALU.mult).then_inc(squares[0], 1)
            dve.wait_ge(mod_picked, 4)
            dve.wait_ge(in_vec, 16)
            link(V.tensor_tensor(mod[:, 0:16, :], bank[6][:, 0:32].rearrange("p (n c) -> p n c", c=2),
                                 bc(v_("b_mod", 0, 16), 2, [P, 16, 2]), ALU.add))
            link(V.scalar_tensor_tensor(A1[:, :, :], mod[:, 8:16, :], 1.0, bc(v_("g_attn", 0, 8), 2, [P, 8, 2]),
                                        ALU.add, ALU.mult))
            for s in range(2):
                if s == 1:
                    dve.wait_ge(sumsq[0], 2)
                    V.tensor_scalar(rstd[:, T:2 * T], bank[7][:, T:2 * T], 1.0 / D, EPS, ALU.mult, ALU.add
                                    ).then_inc(var[0], 1)
                    chunk_to_lo(0, CHUNK1, 3)
                    dve.wait_ge(std[0], 2)
                    link(V.reciprocal(rstd[:, T:2 * T], rstd[:, T:2 * T]))
                for k in range(KD):
                    src = (xT, ctxT)[s][:, k, :]
                    V.scalar_tensor_tensor(hT[:, k, s * T:(s + 1) * T], src, A1[:, k, s:s + 1],
                                           rstd[:, s * T:(s + 1) * T], ALU.mult, ALU.mult).then_inc(normed[0], 1)
                if s == 0:
                    for c in range(3):
                        chunk_to_lo(0, CHUNK1, c)
                for k in range(KD):
                    dve.wait_ge(shifted[0], KD * s + k + 1)
                    V.scalar_tensor_tensor(hT_lo[:, k, s * T:(s + 1) * T], hT[:, k, s * T:(s + 1) * T],
                                           mod[:, k, s:s + 1], hT_hi[:, k, s * T:(s + 1) * T].bitcast(F32),
                                           ALU.add, ALU.subtract).then_inc(shifted_lo, 1)
            dve.wait_ge(in_rest, 16)

            def rotate(q, r, tmp, c, s):
                link(V.tensor_tensor(tmp, r, s, ALU.mult))
                link(V.tensor_tensor(q, q, c, ALU.mult))
                return V.tensor_tensor(q, q, tmp, ALU.add)

            def out_of_psum(n):
                kind, i, e = PROD[n]
                src = bank[n % 4]
                dve.wait_ge(prod_ready, n + 1)
                if kind == "ql":
                    ins = V.tensor_copy(qlat[:, i, :], src[:, 0:T])
                elif kind == "kvl":
                    ins = V.tensor_copy(kvlat[:, i, :], src[:, :])
                elif kind == "kr":
                    ins = V.tensor_copy(kr, src[64:96, :])
                elif kind == "naq":
                    ins = V.tensor_scalar(naq[:, i, :], src[:, 0:T], HD ** -0.5, None, ALU.mult)
                elif kind == "nak":
                    ins = V.tensor_copy(nak[:, i, :], src[:, :])
                elif kind == "nav":
                    ins = V.tensor_copy(nav[:, i, :], src[:, :])
                elif kind == "uq":
                    ins = V.tensor_scalar(qT[:, i, :], src[0:QK, 0:T], QK ** -0.5, None, ALU.mult)
                elif kind == "kn":
                    ins = V.tensor_copy(kT[0:NOPE, i, :], src[0:NOPE, :])
                elif kind == "vm":
                    ins = V.tensor_copy(vm[:, i, :], src[:, :])
                elif kind == "rotk":
                    ins = rotate(kr, src[64:96, :], rtmp, cos, sin)
                elif kind == "rotq":
                    q = qT[64:96, 2 * i:2 * i + 2, :]
                    ins = rotate(q, src[64:96, :].rearrange("p (a t) -> p a t", a=2),
                                 rtmp.rearrange("p (a t) -> p a t", a=2),
                                 bc(cos[:, 0:T], 1, [32, 2, T]), bc(sin[:, 0:T], 1, [32, 2, T]))
                ins.then_inc(prod_d, 1)
                if kind == "rotk":
                    dve.wait_ge(prod_d, copied(PROD, n)[1])
                    dve.sem_inc(kr_done, 1)
                if kind == "rotq" or kind == "rotk":
                    dve.wait_ge(prod_d, copied(PROD, n)[1])

            for n, (kind, i, e) in enumerate(PROD):
                if n == N_BEFORE_LAT:
                    dve.wait_ge(lat_ss, 2)
                    V.tensor_scalar(rq, bank[4][:, 0:T], 1.0 / QL, EPS, ALU.mult, ALU.add).then_inc(lat_var, 1)
                    V.tensor_scalar(rkv, bank[5][:, :], 1.0 / KVL, EPS, ALU.mult, ALU.add).then_inc(lat_var, 1)
                    dve.wait_ge(lat_std, 2)
                    link(V.reciprocal(rq, rq))
                    link(V.reciprocal(rkv, rkv))
                    dve.wait_ge(prod_a, copied(PROD, 4)[1])
                    for k in range(3):
                        V.scalar_tensor_tensor(qlat[:, k, :], qlat[:, k, :], v_("g_qa", k), rq, ALU.mult, ALU.mult
                                               ).then_inc(lat_done, 1)
                    for k in range(2):
                        V.scalar_tensor_tensor(kvlat[:, k, :], kvlat[:, k, :], v_("g_kva", k), rkv, ALU.mult, ALU.mult
                                               ).then_inc(lat_done, 1)
                for c in chunks_after(CHUNK1, n):
                    chunk_to_lo(0, CHUNK1, c)
                if e == "D":
                    out_of_psum(n)

            def maxes(units, A, s):
                a, h, q, nk = units[s]
                u = 16 * a + 8 * q + h
                S = bank[s % 2]
                dve.wait_ge(A["scores"], s + 1)
                if a == 1:
                    if q == 0 and h % 4 == 0:
                        dve.wait_ge(bias_ready, h // 4 + 1)
                    link(V.tensor_tensor(S[:, 0:T], S[:, 0:T], bias[:, h, q, :], ALU.add))
                if a == 2:
                    if s == 0:
                        dve.wait_ge(nck_done, 2)
                    key = nck0[:, h, :] if q == 0 else nck[:, h, :]
                    link(V.scalar_tensor_tensor(S[:, 0:nk * P], S[:, 0:nk * P], cq[:, 8 * q + h:8 * q + h + 1], key,
                                                ALU.add, ALU.add))
                V.tensor_reduce(nmax[:, u:u + 1], S[:, 0:nk * P], AX, ALU.max, negate=True).then_inc(A["maxed"], 1)

            def scale(units, A, s):
                a, h, q, nk = units[s]
                u = 16 * a + 8 * q + h
                dve.wait_ge(A["exped"], s + 1)
                link(V.reciprocal(rinv[:, u:u + 1], rsum[:, u:u + 1]))
                V.tensor_scalar(att[:, s % 3, 0:nk * P], att[:, s % 3, 0:nk * P], rinv[:, u:u + 1], None, ALU.mult
                                ).then_inc(A["scaled"], 1)

            def outputs(units, A, i):
                a, h, _, _ = units[4 * i]
                dve.wait_ge(A["pv"], i + 1)
                k, src = 4 * (a > 0) + h // 2, bank[4 + i % 2][:, 0:T]
                link(V.tensor_copy(h2_hi[:, k, :], src))
                low_part(mix_lo[a // 2][:, k, :], src, h2_hi[:, k, :]).then_inc(A["out"], 1)

            def attention(units, A):
                for s in range(len(units) + 4):
                    if s < len(units):
                        maxes(units, A, s)
                    if 1 <= s <= len(units):
                        scale(units, A, s - 1)
                    if units is UNITS2 and s == 5:
                        dve.wait_ge(sg_t, 2)
                        link(V.tensor_copy(h2_hi[:, 2:4, :], bank[7][:, :].rearrange("p (a t) -> p a t", t=T)))
                        low_part(mix_lo[1][:, 2:4, :], bank[7][:, :].rearrange("p (a t) -> p a t", t=T),
                                 h2_hi[:, 2:4, :]).then_inc(sg_d, 1)
                        dve.wait_ge(sg_a, 1)
                        low_part(mix_lo[1][:, 0:2, :], bank[6][:, :].rearrange("p (a t) -> p a t", t=T),
                                 h2_hi[:, 0:2, :]).then_inc(sg_d, 1)
                    if s == len(units) + 1:
                        stage, chunk, c0 = ((0, CHUNK1, OUT1), (1, CHUNK2, OUT2))[units is UNITS2]
                        for c in range(c0, c0 + 2):
                            chunk_to_lo(stage, chunk, c)
                    if s >= 7 and s % 4 == 3:
                        outputs(units, A, (s - 7) // 4)

            cq = small[:, 3, 0:16]
            attention(UNITS, ATT[0])
            for c in range(OUT1 + 2, OUT1 + 4):
                chunk_to_lo(0, CHUNK1, c)

            dve.wait_ge(mod_picked, N_MOD)
            link(V.tensor_tensor(mod[:, 16:48, :], bank[6][:, 32:96].rearrange("p (n c) -> p n c", c=2),
                                 bc(v_("b_mod", 16, 32), 2, [P, 32, 2]), ALU.add))
            link(V.scalar_tensor_tensor(A2[:, :], mod[:, 32:40, 0], 1.0, v_("g_ffn", 0, 8), ALU.add, ALU.mult))
            for m in range(KD):
                dve.wait_ge(proj_out, m + 1)
                V.scalar_tensor_tensor(xT[:, m, :], bank[m % 4][:, 0:T], mod[:, 16 + m, 0:1], xT[:, m, :],
                                       ALU.mult, ALU.add).then_inc(resid, 1)
                if m < 4:
                    chunk_to_lo(0, CHUNK1, OUT1 + 4 + m)

            def norm(r, gain, dst):
                dve.wait_ge(sumsq[r], 1)
                link(V.tensor_scalar(rs[:, 0:2], bank[NORM_BANK[r]][:, 0:2], 1.0 / D, EPS, ALU.mult, ALU.add))
                V.reciprocal(rs[:, 0:2], rs[:, 0:2]).then_inc(var[r], 1)
                dve.wait_ge(spread, r)
                for k in range(KD):
                    V.scalar_tensor_tensor(dst[:, k, :], xT[:, k, :], gain(k), bank[NORM_BANK[r]][:, T:2 * T],
                                           ALU.mult, ALU.mult).then_inc(normed[r], 1)

            norm(1, lambda k: A2[:, k:k + 1], h2)

            link(V.memset(place[:, 0, :], 0.0))
            S_ = small

            def t3(i, n=4):
                return S_[:, i, 0:2 * n].rearrange("p (q n) -> p q n", q=NT)

            def top(values, scratch, onehot):
                link(V.tensor_reduce(S_[:, 8, 0:2], values, AX, ALU.max))
                link(V.tensor_tensor(scratch, values, bc(S_[:, 8, 0:2], 2, [P, NT, 4]), ALU.is_equal))
                link(V.tensor_tensor(scratch, scratch, bc(desc, 1, [P, NT, 4]), ALU.mult))
                link(V.tensor_reduce(S_[:, 9, 0:2], scratch, AX, ALU.max))
                link(V.tensor_tensor(onehot, scratch, bc(S_[:, 9, 0:2], 2, [P, NT, 4]), ALU.is_equal))

            dve.wait_ge(logits, 1)
            dve.wait_ge(in_row, 48)
            L = small[:, 10:12, 0:20]
            link(V.tensor_tensor(L, bank[6][:, 256:320].rearrange("p (q n) -> p q n", q=NT)[:, :, 0:20],
                                 bc(row[:, ROW["b_router"]:ROW["b_router"] + 20], 1, [P, NT, 20]), ALU.add))
            G, E = L[:, :, 0:4], L[:, :, 4:20].rearrange("p q (g e) -> p q g e", g=NG)
            top(G, t3(2), t3(3))
            V.tensor_tensor(t3(1), G, bc(S_[:, 8, 0:2], 2, [P, NT, 4]), ALU.subtract).then_inc(gdiff, 1)
            wide = small[:, 12:14, 0:16].rearrange("p q (g e) -> p q g e", g=NG)
            for q in range(NT):
                link(V.tensor_tensor(wide[:, q], E[:, q], bc(t3(3)[:, q, :], 2, [P, NG, EG]), ALU.mult))
                link(V.tensor_reduce(t3(4)[:, q, :], wide[:, q].rearrange("p g e -> p e g"), AX, ALU.add))
            link(V.tensor_reduce(S_[:, 6, 0:2], t3(4), AX, ALU.max))
            V.tensor_tensor(t3(5), t3(4), bc(S_[:, 6, 0:2], 2, [P, NT, 4]), ALU.subtract).then_inc(ediff, 1)
            dve.wait_ge(gexp, 1)
            link(V.tensor_reduce(S_[:, 7, 0:2], t3(1), AX, ALU.add))
            link(V.reciprocal(S_[:, 7, 0:2], S_[:, 7, 0:2]))
            dve.wait_ge(eexp, 1)
            link(V.tensor_reduce(S_[:, 6, 0:2], t3(5), AX, ALU.add))
            link(V.reciprocal(S_[:, 6, 0:2], S_[:, 6, 0:2]))
            link(V.tensor_tensor(t3(5), t3(5), bc(S_[:, 6, 0:2], 2, [P, NT, 4]), ALU.mult))
            top(t3(5), t3(2), t3(4))
            link(V.scalar_tensor_tensor(t3(1), t3(4), -2.0, t3(5), ALU.mult, ALU.add))
            top(t3(1), t3(2), t3(0))
            link(V.tensor_tensor(t3(0), t3(4), t3(0), ALU.add))
            link(V.tensor_tensor(t3(4), t3(0), t3(5), ALU.mult))
            link(V.tensor_reduce(S_[:, 6, 0:2], t3(4), AX, ALU.add))
            link(V.reciprocal(S_[:, 6, 0:2], S_[:, 6, 0:2]))
            link(V.tensor_tensor(t3(4), t3(4), bc(S_[:, 6, 0:2], 2, [P, NT, 4]), ALU.mult))
            link(V.tensor_tensor(t3(4), t3(4), bc(S_[:, 7, 0:2], 2, [P, NT, 4]), ALU.mult))
            comb = small[:, 15, :].rearrange("p (q g e) -> p q g e", q=NT, g=NG)
            chosen = small[:, 14, :].rearrange("p (q g e) -> p q g e", q=NT, g=NG)
            for q in range(NT):
                V.tensor_tensor(chosen[:, q], bc(t3(3)[:, q, :], 2, [P, NG, EG]), bc(t3(0)[:, q, :], 1, [P, NG, EG]),
                                ALU.mult).then_inc(comb_done, 1)
            for q in range(NT):
                link(V.tensor_tensor(comb[:, q], bc(t3(3)[:, q, :], 2, [P, NG, EG]),
                                     bc(t3(4)[:, q, :], 1, [P, NG, EG]), ALU.mult))
            for b in (1, 3):
                dve.wait_ge(tok_t, b + 1)
                V.tensor_copy(h2tok[:, b // 2, (b % 2) * 512:(b % 2 + 1) * 512], bank[b][:, :]).then_inc(tok_d, 1)
            dve.wait_ge(counted, 1)
            top_n, windows_f = turns_f[:, 0:1], turns_f[:, 1:2]
            link(V.tensor_tensor(posm[:, :], bank[6][:, 192:224], small[:, 14, :], ALU.mult))
            link(V.tensor_scalar(posm[:, :], posm[:, :], -1.0, None, ALU.add))
            link(V.tensor_reduce(top_n, bank[6][:, 224:240], AX, ALU.max))
            link(V.tensor_scalar(windows_f, top_n, float(CAP), 1.0, ALU.is_gt, ALU.add))
            for c in range(2, T // CAP):
                link(V.scalar_tensor_tensor(windows_f, top_n, float(c * CAP), windows_f, ALU.is_gt, ALU.add))
            link(V.tensor_scalar(turns_f[:, 2:3], windows_f, -1.0, None, ALU.add))
            V.tensor_copy(turns_i[:, :], turns_f[:, 1:3]).then_inc(turns_ready, 1)
            dve.wait_ge(turns_ready, 1)
            windows = dve.value_load(turns_i[0:1, 0:1], min_val=1, max_val=T // CAP)
            with dve.Fori(0, windows) as w:
                dve.wait_ge(scattered, w * 9 + 1)
                for q in range(NT):
                    V.tensor_tensor(pick_t[:, q], bc(iota, 1, [P, NE, CAP]),
                                    bc(posm[:, NE * q:NE * (q + 1)], 2, [P, NE, CAP]), ALU.is_equal
                                    ).then_inc(picked_t, 1)
                V.memset(ysb[:, 0:512], 0.0).then_inc(y_a, 1)
                V.memset(ysb[:, 512:1024], 0.0).then_inc(y_d, 1)
                dve.wait_ge(picked_t, w * 2 + 2)
                V.tensor_scalar(posm[:, :], posm[:, :], -float(CAP), None, ALU.add).then_inc(posm_moved, 1)
                weights = small[:, :, :].rearrange("p a b -> p (a b)")

                def inputs(p):
                    dve.wait_ge(gathered, p)
                    V.tensor_copy(xs[:, 4:8, :], bank[1][:, :].rearrange("p (k s) -> p k s", k=4)).then_inc(xs_d, 1)

                def pair(i, last=False):
                    dve.wait_ge(posm_moved, w + 1)
                    dve.wait_ge(silu_g, w * 8 + i + 1)
                    dve.wait_ge(used, w * 48 + i * 6 + 4)
                    V.tensor_tensor(hid, hid, bank[3][:, :], ALU.mult).then_inc(hid_made, 1)
                    if not last:
                        inputs(w * 16 + i * 2 + 4)
                    for q in range(NT):
                        ins = V.tensor_tensor(pick_w[:, q],
                                              arena[:, bass.ds(i * P + 1024 * q, P)].rearrange("p (e s) -> p e s", e=2),
                                              bc(weights[:, bass.ds(i * 2 + (15 * 32 + NE * q), 2)], 2, [P, 2, CAP]),
                                              ALU.mult)
                    ins.then_inc(picked, 1)
                    dve.wait_ge(hid_t, w * 8 + i + 1)
                    V.tensor_copy(hidT[:, :, :].rearrange("p f s -> p (f s)"), bank[2][:, :]).then_inc(hidT_done, 1)
                    dve.wait_ge(used, w * 48 + i * 6 + 6)
                    dve.wait_ge(scattered, w * 9 + i + 2)
                    V.tensor_copy(ysb[:, 512:1024], bank[3][:, :]).then_inc(y_d, 1)

                inputs(w * 16 + 2)
                with dve.Fori(0, NPAIR - 1) as i:
                    pair(i)
                pair(NPAIR - 1, last=True)
            dve.wait_ge(scattered, windows * 9 + 1)
            for m in range(KD):
                V.scalar_tensor_tensor(xT[:, m, :], yacc(m), mod[:, 40 + m, 0:1], xT[:, m, :], ALU.mult, ALU.add
                                       ).then_inc(resid_m, 1)
            s12 = bank[NORM_BANK[2]][:, 0:4].rearrange("p (q n) -> p n q", n=2)
            dve.wait_ge(sumsq[2], 1)
            link(V.tensor_scalar(rs[:, 0:2], s12[:, 0, :], 1.0 / D, EPS, ALU.mult, ALU.add))
            link(V.reciprocal(rs[:, 0:2], rs[:, 0:2]))
            link(V.scalar_tensor_tensor(rs[:, 2:4], s12[:, 1, :], 1.0 / D, rs[:, 0:2], ALU.mult, ALU.mult))
            link(V.tensor_scalar(rs[:, 2:4], rs[:, 2:4], EPS, None, ALU.add))
            link(V.reciprocal(rs[:, 2:4], rs[:, 2:4]))
            V.tensor_tensor(rs[:, 2:4], rs[:, 2:4], rs[:, 0:2], ALU.mult).then_inc(var[2], 1)
            dve.wait_ge(spread, 2)
            for k in range(KD):
                V.scalar_tensor_tensor(h2[:, k, :], xT[:, k, :], g_both[:, k:k + 1], bank[6][:, 0:T],
                                       ALU.mult, ALU.mult).then_inc(normed[2], 1)
            for c in range(2):
                chunk_to_lo(1, CHUNK2, c)
            for k in range(KD):
                dve.wait_ge(h2_hi_done, k + 1)
                low_part(h2_lo[:, k, :], h2[:, k, :], h2_hi[:, k, :]).then_inc(h2_lo_done, 1)
            for c in range(2, 4):
                chunk_to_lo(1, CHUNK2, c)
            for k in range(KD):
                V.scalar_tensor_tensor(xT[:, k, :], xT[:, k, :], v_("g_final", k), bank[7][:, 0:T],
                                       ALU.mult, ALU.mult).then_inc(y_made, 1)

            f2, fa, lfr = small[:, 0, 0:16], small[:, 1, 0:16], small[:, 2, 0:16]

            def out_of_psum2(n):
                kind, i, e = PROD2[n]
                src = bank[n % 4]
                dve.wait_ge(prod2_ready, n + 1)
                if kind == "f":
                    V.tensor_tensor(f2.rearrange("p (q h) -> p q h", q=NT),
                                    src[:, 0:16].rearrange("p (q h) -> p q h", q=NT),
                                    bc(row[:, ROW["f_bias"]:ROW["f_bias"] + 8], 1, [P, NT, 8]), ALU.add
                                    ).then_inc(prod2_d, 1)
                    dve.wait_ge(prod2_d, 1)
                    V.scalar_tensor_tensor(fa, f2, -1.0, f2, ALU.mult, ALU.min).then_inc(f_abs, 1)
                    link(V.tensor_scalar(f2, f2, 0.0, None, ALU.min))
                    dve.wait_ge(f_ln, 1)
                    V.tensor_tensor(lfr, f2, fa, ALU.subtract).then_inc(lf_done, 1)
                    return
                if kind == "q":
                    ins = V.tensor_scalar(q2[:, i, :], src[:, 0:T], HD ** -0.5, None, ALU.mult)
                elif kind == "k":
                    ins = V.tensor_copy(k2[:, i, :], src[:, 0:T])
                elif kind == "cq":
                    ins = V.tensor_copy(cq, src[:, 0:16])
                ins.then_inc(prod2_d, 1)

            def heads(t):
                return t.rearrange("p (h d) -> p h d", h=H)

            def layer_norm():
                dve.wait_ge(prod2_a, 4)
                mu, vr = small[:, 5, 0:16], small[:, 6, 0:16]
                v3 = vg[:, :, :].rearrange("p n (h d) -> p (n h) d", h=H)
                l3 = lnt[:, :, :].rearrange("p n (h d) -> p (n h) d", h=H)
                link(V.tensor_reduce(mu, v3, AX, ALU.add))
                link(V.tensor_scalar(mu, mu, 1.0 / HD, None, ALU.mult))
                link(V.tensor_tensor(v3, v3, bc(mu, 2, [P, 16, HD]), ALU.subtract))
                link(V.tensor_tensor(l3, v3, v3, ALU.mult))
                link(V.tensor_reduce(vr, l3, AX, ALU.add))
                V.tensor_scalar(vr, vr, 1.0 / HD, EPS, ALU.mult, ALU.add).then_inc(ln_var, 1)

            def layer_norm_end():
                vr = small[:, 6, 0:16]
                v3 = vg[:, :, :].rearrange("p n (h d) -> p (n h) d", h=H)
                dve.wait_ge(ln_std, 1)
                link(V.reciprocal(vr, vr))
                link(V.tensor_tensor(v3, v3, bc(vr, 2, [P, 16, HD]), ALU.mult))
                V.tensor_tensor(vg[:, :, :], vg[:, :, :], bc(row[:, ROW["sg_ln"]:ROW["sg_ln"] + 512], 1, [P, NT, 512]),
                                ALU.mult).then_inc(vn_done, 1)

            for n, (kind, i, e) in enumerate(PROD2):
                for c in chunks_after(CHUNK2, n):
                    chunk_to_lo(1, CHUNK2, c)
                if kind == "k" and i == 0:
                    layer_norm()
                if e == "D":
                    out_of_psum2(n)
            layer_norm_end()
            for q in range(NT):
                dve.wait_ge(sg_mm, q + 1)
                link(V.tensor_tensor(heads(osb[:, q, 0:512]), heads(bank[6 + q][:, :]),
                                     bc(v_("sg_b", 0, 8), 2, [P, H, HD]), ALU.add))
                V.tensor_tensor(osb[:, q, 0:512], osb[:, q, 0:512], ug[:, q, :], ALU.mult).then_inc(sg_done, 1)
            dve.wait_ge(prod2_d, total(PROD2, "D"))
            attention(UNITS2, ATT[1])
            def up_lo(at, j, half):
                dve.wait_ge(wide_hi, at)
                low_part(granule(w_lo, j, half), up_half_of(j, half), granule(w_hi, j, half)).then_inc(wide_lo, 1)

            def down_lo(d, half):
                dve.wait_ge(wide_hi, 2 * NP + 2 * d + half + 1)
                low_part(w_lo[:, d % 2, half, :], down_half_of(d, half), w_hi[:, d % 2, half, :]
                         ).then_inc(wide_lo, 1)

            for c in range(OUT2 + 2, OUT2 + 4):
                chunk_to_lo(1, CHUNK2, c)
            dve.wait_ge(y_made, KD)
            for m in range(KD):
                dve.wait_ge(proj2_out, m + 1)
                V.tensor_tensor(xT[:, m, :], bank[m % 4][:, 0:T], xT[:, m, :], ALU.add).then_inc(resid2, 1)
                if m < 4:
                    chunk_to_lo(1, CHUNK2, OUT2 + 4 + m)
                elif m < 6:
                    up_lo(m - 3, 0, m - 4)
            norm(3, lambda k: v_("g_ffn2", k), h2)
            for k in range(KD):
                dve.wait_ge(h2_hi_done, KD + k + 1)
                low_part(h2_lo[:, k, :], h2[:, k, :], h2_hi[:, k, :]).then_inc(h2_lo_done, 1)
            for half in range(2):
                up_lo(half + 3, 1, half)

            def hidden_lo(at, b, n):
                dve.wait_ge(hid_hi_done, n)
                low_part(hid_lo[:, at, :], yconv[:, b, 1, :], hid_hi[:, at, :]).then_inc(hid_lo_done, 1)

            def pair(i, j, first=False, last=False):
                b = j % 2
                for half in range(2):
                    if last:
                        down_lo(j, half)
                    else:
                        up_lo(i * 8 + (2 * j + half + 5), (j + 2) % 4, half)
                if not (first and j == 0):
                    hidden_lo(i * 4 + (j - 1), 1 - b, i * 4 + j)
                dve.wait_ge(conv0, i * 8 + (2 * j + 2))
                for g in range(2):
                    y, a = yconv[:, b, g, :], bank[j % 4][:, g * T:(g + 1) * T]
                    V.scalar_tensor_tensor(y[:, 1:T], a[:, 0:T - 1],
                                           vec[:, bass.ds(i * 4 + (j + 22 * g + VEC["w_conv"] + 44), 1)], y[:, 1:T],
                                           ALU.mult, ALU.add).then_inc(tap1, 1)
                for g in range(2):
                    y, a = yconv[:, b, g, :], bank[j % 4][:, g * T:(g + 1) * T]
                    dve.wait_ge(tap1, i * 8 + (2 * j + g + 1))
                    V.scalar_tensor_tensor(y[:, 2:T], a[:, 0:T - 2],
                                           vec[:, bass.ds(i * 4 + (j + 22 * g + VEC["w_conv"]), 1)], y[:, 2:T],
                                           ALU.mult, ALU.add).then_inc(tap2, 1)
                dve.wait_ge(tap2, i * 8 + (2 * j + 2))
                dve.wait_ge(silu_f, i * 4 + (j + 1))
                V.tensor_tensor(yconv[:, b, 1, :], yconv[:, b, 0, :], yconv[:, b, 1, :], ALU.mult
                                ).then_inc(hid_done, 1)

            for j in range(4):
                pair(0, j, first=True)
            with dve.Fori(1, NP // 4) as i:
                for j in range(4):
                    pair(i, j)
            for j in range(NP % 4):
                pair(NP // 4, j, last=True)
            hidden_lo(NP - 1, (NP - 1) % 2, NP)
            for d in range(2, NP // 2):
                for half in range(2):
                    down_lo(d, half)
            dve.wait_ge(down_half, NP)
            for m in range(KD):
                V.tensor_tensor(xT[:, m, :], yacc(m), xT[:, m, :], ALU.add).then_inc(resid3, 1)
            norm(4, lambda k: v_("g_final2", k), outT)


def kernel(**inputs):
    import numpy as _np
    import concourse.bacc as _bacc
    from concourse import mybir as _mybir
    from concourse.bass_utils import run_bass_kernel_spmd as _run

    a = {k: _np.asarray(v) for k, v in inputs.items()}

    def tiles(v):
        return v.reshape(-1, P).T

    def featuremajor(x):
        return _np.ascontiguousarray(x.T.reshape(KD, P, T).transpose(1, 0, 2))

    vec = _np.concatenate([
        _np.stack([tiles(a["c"][0]), tiles(a["c_ctx"])], axis=2).reshape(P, 16), tiles(a["b_mod"][0]),
        tiles(a["norm_attn_g"][0]), tiles(a["norm_ffn_g"][0]), tiles(a["q_a_norm_g"][0]), tiles(a["kv_a_norm_g"][0]),
        tiles(a["final_norm_g"]), tiles(a["norm_mix_g_2"][0]), tiles(a["norm_ffn_g_2"][0]), tiles(a["b_conv_2"][0]),
        tiles(a["w_conv_2"][0].reshape(-1)), tiles(a["norm_final_g_2"]), a["sg_b_2"][0].T], axis=1)
    row = _np.concatenate([a["b_router_group"][0], a["b_router_expert"][0], a["f_bias_2"][0],
                           a["sg_ln_g_2"][0].reshape(-1)])[None]
    wr = _np.concatenate([a["w_router_group"][0], a["w_router_expert"][0]], axis=1).reshape(KD, P, 20)
    wr = _np.concatenate([wr, _np.zeros((KD, P, 12), _np.float32)], axis=2)
    i, j = _np.arange(P)[:, None], _np.arange(P)[None]
    con = _np.zeros((P, NCON), _np.float32)
    con[:, CON["ident"]:CON["ident"] + P] = i == j
    con[:, CON["tri"]:CON["tri"] + P] = _np.where(j <= i, 0.0, -BIG)
    con[:, CON["upper"]:CON["upper"] + P] = i <= j
    con[:, CON["ones"]:CON["ones"] + P] = 1.0
    col, key = (i % GRID_W), _np.arange(GRID_W)[None]
    start = _np.clip(col - 8, 0, GRID_W - 16)
    con[:, CON["namask"]:CON["namask"] + GRID_W] = _np.where((key >= start) & (key < start + 16), 0.0, -BIG)
    r, m = _np.arange(32)[:, None], _np.arange(32)[None]
    con[64:96, CON["rot"]:CON["rot"] + 32] = _np.where(r == m + 16, -1.0, 0.0) + _np.where(r == m - 16, 1.0, 0.0)
    half = ROPE // 2
    inv = (_np.float32(10000.0) ** (-_np.arange(0, half, 2, dtype=_np.float32) / _np.float32(half))).astype(_np.float32)
    pos = _np.arange(T)
    ang = _np.concatenate([(pos // GRID_W).astype(_np.float32)[:, None] * inv,
                           (pos % GRID_W).astype(_np.float32)[:, None] * inv], axis=1).T
    con[64:96, CON["cos"]:CON["cos"] + 512] = 1.0
    con[64:96, CON["cos"]:CON["cos"] + T] = _np.tile(_np.cos(ang), (2, 1))
    con[64:96, CON["sin"]:CON["sin"] + T] = _np.tile(_np.sin(ang), (2, 1))
    con[:, CON["desc"]:CON["desc"] + 4] = [4.0, 3.0, 2.0, 1.0]
    con[:, CON["iota"]:CON["iota"] + CAP] = _np.arange(CAP)
    con[:, CON["pick"]] = i[:, 0] % 32 == 0
    con[:, CON["pick"] + 1] = i[:, 0] % 32 == 1
    con[:, CON["pick20"]:CON["pick20"] + 20] = i % 32 == _np.arange(20)
    q, k = _np.arange(T), _np.arange(T)
    dr = k[None] // GRID_W - q[:, None] // GRID_W + 7
    dc = _np.clip(k[None] % GRID_W - q[:, None] % GRID_W + 15, 0, 30)
    bias = a["na_rel_bias"][0][:, dr, dc].reshape(H, NT, P, T).transpose(2, 0, 1, 3).reshape(P, -1)

    feeds = {
        "xT": featuremajor(a["x"][0]), "ctxT": featuremajor(a["ctx"][0]), "vec": vec, "row": row, "con": con,
        "w_mod": a["w_mod"][0], "w_in": a["w_in"][0], "w_uq": a["w_uq"][0], "w_ukv": a["w_ukv"][0],
        "bias": bias, "w_out": a["w_out"][0], "wr": wr.transpose(1, 0, 2),
        "w_gate": a["w_gate"][0], "w_up": a["w_up"][0], "w_down": a["w_down"][0],
        "w_in2": a["w_in_2"][0], "wf": a["w_in_2"][0][:, 2560:].reshape(KD, P, 8).transpose(1, 0, 2),
        "sgw": a["sg_w_2"][0].transpose(2, 0, 1), "w_out2": a["w_out_2"][0],
        "w_up2": a["w_up_2"][0], "w_down2": a["w_down_2"][0],
    }
    nc = _bacc.Bacc("TRN2", target_bir_lowering=False, num_devices=1)
    arrays, args = {}, []
    for name, v in feeds.items():
        v = _np.ascontiguousarray(v)
        arrays[f"in_{name}"] = v
        args.append(nc.dram_tensor(f"in_{name}", v.shape, _mybir.dt.from_np(v.dtype), kind="ExternalInput").ap())
    args.append(nc.dram_tensor("out_T", (P, KD, T), F32, kind="ExternalOutput").ap())
    block_pair_kernel(nc, *args)
    got = _run(nc, [arrays], core_ids=[0]).results[0]["out_T"]
    return _np.ascontiguousarray(got.transpose(1, 0, 2).reshape(D, T).T)[None]
```
